# Optimizing a Trainium2 kernel written in Bass

```python
import jax
import jax.numpy as jnp
from jax import lax
import numpy as np
import math
import jax, jax.numpy as jnp

D_MODEL = 1024
BATCH = 1
SEQ = 512
DEPTH = 2

HEAD_DIM = 64
ROT_DIM = HEAD_DIM // 4
ROPE_THETA = 500000.0
NORM_EPS = 1e-6
Q_BLOCK = 128
D_FF = 2816

SB_HEADS = 4
NSA_HEADS = 8
NSA_GROUPS = 2
NSA_HPG = NSA_HEADS // NSA_GROUPS
NSA_CMP_LEN = 32
NSA_CMP_STRIDE = 16
NSA_CMP_HIDDEN = 2 * HEAD_DIM
NSA_SEL_LEN = 64
NSA_SEL_N = 16
NSA_WINDOW = 512
NSA_FORCED_SCORE = 1.0e4
DSA_HEADS = 4
DSA_IDX_HEADS = 8
DSA_IDX_DIM = 32
DSA_IDX_ROT = DSA_IDX_DIM // 4
DSA_TOPK = 256

SB_W = SB_HEADS * HEAD_DIM
NSA_QW = NSA_HEADS * HEAD_DIM
NSA_KVW = NSA_GROUPS * HEAD_DIM
DSA_QW = DSA_HEADS * HEAD_DIM
IN_WIDTHS = (SB_W, SB_W, SB_W,
             NSA_QW, NSA_KVW, NSA_KVW, NSA_KVW, NSA_KVW, NSA_KVW, NSA_KVW, 3 * NSA_HEADS,
             DSA_QW, HEAD_DIM, HEAD_DIM, DSA_IDX_HEADS * DSA_IDX_DIM, DSA_IDX_DIM, DSA_IDX_HEADS)
D_IN = sum(IN_WIDTHS)


def rms_norm(x, g):
    xf = x.astype(jnp.float32)
    y = xf * lax.rsqrt(jnp.mean(xf * xf, axis=-1, keepdims=True) + NORM_EPS)
    return (y * g.astype(jnp.float32)).astype(x.dtype)

def rope_tables(pos, rot_dim):
    inv = ROPE_THETA ** (-jnp.arange(0, rot_dim, 2, dtype=jnp.float32) / rot_dim)
    ang = pos.astype(jnp.float32)[:, None] * inv[None, :]
    return jnp.cos(ang), jnp.sin(ang)

def apply_rope(x, cos, sin):
    half = cos.shape[-1]
    xf = x[..., :2 * half].astype(jnp.float32)
    x1, x2 = xf[..., :half], xf[..., half:]
    c, s = cos[:, None, :], sin[:, None, :]
    rot = jnp.concatenate([x1 * c - x2 * s, x2 * c + x1 * s], axis=-1).astype(x.dtype)
    return jnp.concatenate([rot, x[..., 2 * half:]], axis=-1)

def masked_softmax(s, mask):
    s = jnp.where(mask, s.astype(jnp.float32), -jnp.inf)
    m = jnp.max(s, axis=-1, keepdims=True)
    m = jnp.where(jnp.isfinite(m), m, 0.0)
    p = jnp.exp(s - m)
    den = jnp.sum(p, axis=-1, keepdims=True)
    return p / jnp.where(den > 0, den, 1.0)

def unblock(y):
    n, b, t = y.shape[:3]
    return jnp.moveaxis(y, 0, 1).reshape((b, n * t) + y.shape[3:])

def swiglu_ffn(x, g, w_gu, w_down):
    h = rms_norm(x, g)
    gate, up = jnp.split(h @ w_gu, 2, axis=-1)
    return (jax.nn.silu(gate) * up) @ w_down

def stick_breaking_attention(q, k, v):
    B, S, H, d = q.shape
    scale = d ** -0.5
    kh = k.transpose(0, 2, 1, 3)
    vh = v.transpose(0, 2, 1, 3)
    s_pos = jnp.arange(S)

    def block(i):
        q0 = i * Q_BLOCK
        qb = lax.dynamic_slice_in_dim(q, q0, Q_BLOCK, axis=1)
        z = jnp.einsum('bthd,bhsd->bhts', qb, kh).astype(jnp.float32) * scale
        t_pos = q0 + jnp.arange(Q_BLOCK)
        past = s_pos[None, :] < t_pos[:, None]
        log_1m = jnp.where(past, jax.nn.log_sigmoid(-z), 0.0)
        tail = lax.cumsum(log_1m, axis=3, reverse=True) - log_1m
        w = jnp.where(past, jnp.exp(jax.nn.log_sigmoid(z) + tail), 0.0)
        return jnp.einsum('bhts,bhsd->bthd', w.astype(v.dtype), vh)

    return unblock(lax.map(block, jnp.arange(S // Q_BLOCK)))

def nsa_compress(x, pe, w1, w2):
    B, S, G, d = x.shape
    nchunk = S // NSA_CMP_STRIDE
    r = NSA_CMP_LEN // NSA_CMP_STRIDE
    nc = nchunk - r + 1
    chunks = x.reshape(B, nchunk, NSA_CMP_STRIDE, G, d)
    blocks = jnp.concatenate([chunks[:, m:m + nc] for m in range(r)], axis=2)
    blocks = blocks + pe[None, None, :, None, :]
    flat = blocks.transpose(0, 1, 3, 2, 4).reshape(B, nc, G, NSA_CMP_LEN * d)
    return jax.nn.silu(flat @ w1) @ w2

def nsa_attention(q, k_cmp, v_cmp, k_sel, v_sel, k_win, v_win, gate_logits,
                  q_norm, k_norm, pe, w1, w2, cos, sin):
    B, S, _, d = q.shape
    G, hpg, T = NSA_GROUPS, NSA_HPG, Q_BLOCK
    scale = d ** -0.5
    dt = v_sel.dtype
    qg = apply_rope(rms_norm(q, q_norm), cos, sin).reshape(B, S, G, hpg, d)
    k_sel = apply_rope(rms_norm(k_sel, k_norm[1]), cos, sin)
    k_win = apply_rope(rms_norm(k_win, k_norm[2]), cos, sin)
    gates = jax.nn.sigmoid(gate_logits).reshape(B, S, G, hpg, 3)

    kc = rms_norm(nsa_compress(k_cmp, pe[0], w1[0], w2[0]), k_norm[0])
    nc = kc.shape[1]
    cmp_start = jnp.arange(nc) * NSA_CMP_STRIDE
    cmp_end = cmp_start + NSA_CMP_LEN - 1
    cos_c, sin_c = rope_tables(cmp_end, ROT_DIM)
    kc = apply_rope(kc, cos_c, sin_c).transpose(0, 2, 1, 3)
    vc = nsa_compress(v_cmp, pe[1], w1[1], w2[1]).transpose(0, 2, 1, 3)

    ns = S // NSA_SEL_LEN
    n_sel = min(NSA_SEL_N, ns)
    ks_blocks = k_sel.reshape(B, ns, NSA_SEL_LEN, G, d).transpose(0, 3, 1, 2, 4)
    vs_blocks = v_sel.reshape(B, ns, NSA_SEL_LEN, G, d).transpose(0, 3, 1, 2, 4)
    sel_start = jnp.arange(ns) * NSA_SEL_LEN
    overlap = ((cmp_start[:, None] < sel_start[None, :] + NSA_SEL_LEN)
               & (cmp_end[:, None] >= sel_start[None, :])).astype(jnp.float32)
    gather_blocks = jax.vmap(jax.vmap(lambda src, ix: src[ix]))

    pad = ((0, 0), (NSA_WINDOW, 0), (0, 0), (0, 0))
    kw_pad = jnp.pad(k_win, pad)
    vw_pad = jnp.pad(v_win, pad)

    def block(i):
        q0 = i * T
        t_pos = q0 + jnp.arange(T)
        qb = lax.dynamic_slice_in_dim(qg, q0, T, axis=1)

        sc = jnp.einsum('btghd,bgcd->bghtc', qb, kc) * scale
        pc = masked_softmax(sc, cmp_end[None, :] <= t_pos[:, None])
        o_cmp = jnp.einsum('bghtc,bgcd->btghd', pc.astype(dt), vc)

        imp = jnp.einsum('bghtc,cn->bgtn', pc, overlap)
        j = jnp.arange(ns)[None, :]
        cur = (t_pos // NSA_SEL_LEN)[:, None]
        visible = j * NSA_SEL_LEN <= t_pos[:, None]
        forced = (j == 0) | (j == cur) | (j == cur - 1)
        score = jnp.where(visible, jnp.where(forced, NSA_FORCED_SCORE, imp), -jnp.inf)
        _, sel = lax.top_k(score, n_sel)
        k_g = gather_blocks(ks_blocks, sel)
        v_g = gather_blocks(vs_blocks, sel).reshape(B, G, T, n_sel * NSA_SEL_LEN, d)
        tok = sel[..., None] * NSA_SEL_LEN + jnp.arange(NSA_SEL_LEN)
        smask = (tok <= t_pos[:, None, None]).reshape(B, G, 1, T, n_sel * NSA_SEL_LEN)
        ss = jnp.einsum('btghd,bgtnld->bghtnl', qb, k_g) * scale
        ps = masked_softmax(ss.reshape(B, G, hpg, T, n_sel * NSA_SEL_LEN), smask)
        o_sel = jnp.einsum('bghtm,bgtmd->btghd', ps.astype(dt), v_g)

        kwb = lax.dynamic_slice_in_dim(kw_pad, q0, T + NSA_WINDOW, axis=1)
        vwb = lax.dynamic_slice_in_dim(vw_pad, q0, T + NSA_WINDOW, axis=1)
        s_abs = q0 - NSA_WINDOW + jnp.arange(T + NSA_WINDOW)
        wmask = ((s_abs[None, :] <= t_pos[:, None]) & (s_abs[None, :] > t_pos[:, None] - NSA_WINDOW)
                 & (s_abs[None, :] >= 0))
        sw = jnp.einsum('btghd,bsgd->bghts', qb, kwb) * scale
        pw = masked_softmax(sw, wmask)
        o_win = jnp.einsum('bghts,bsgd->btghd', pw.astype(dt), vwb)

        g = lax.dynamic_slice_in_dim(gates, q0, T, axis=1)
        return g[..., 0:1] * o_cmp + g[..., 1:2] * o_sel + g[..., 2:3] * o_win

    out = unblock(lax.map(block, jnp.arange(S // T)))
    return out.reshape(B, S, NSA_HEADS * d)

def dsa_attention(q, k, v, iq, ik, iw, q_norm, k_norm, cos, sin, cos_i, sin_i):
    B, S, _, d = q.shape
    T = Q_BLOCK
    scale = d ** -0.5
    dt = v.dtype
    top_k = min(DSA_TOPK, S // 4)
    q = apply_rope(rms_norm(q, q_norm), cos, sin)
    k = apply_rope(rms_norm(k[:, :, None, :], k_norm), cos, sin)[:, :, 0, :]
    iq = apply_rope(iq, cos_i, sin_i)
    ik = apply_rope(ik[:, :, None, :], cos_i, sin_i)[:, :, 0, :]
    iw = iw.astype(jnp.float32) * (DSA_IDX_HEADS ** -0.5) * (DSA_IDX_DIM ** -0.5)
    s_pos = jnp.arange(S)
    gather_rows = jax.vmap(lambda src, ix: src[ix])

    def block(i):
        q0 = i * T
        t_pos = q0 + jnp.arange(T)
        qi = lax.dynamic_slice_in_dim(iq, q0, T, axis=1)
        wi = lax.dynamic_slice_in_dim(iw, q0, T, axis=1)
        logits = jax.nn.relu(jnp.einsum('bthd,bsd->bths', qi, ik).astype(jnp.float32))
        score = jnp.einsum('bths,bth->bts', logits, wi)
        score = jnp.where(s_pos[None, None, :] <= t_pos[None, :, None], score, -jnp.inf)
        _, idx = lax.top_k(score, top_k)
        kg = gather_rows(k, idx)
        vg = gather_rows(v, idx)
        qb = lax.dynamic_slice_in_dim(q, q0, T, axis=1)
        sc = jnp.einsum('bthd,btkd->bhtk', qb, kg) * scale
        p = masked_softmax(sc, (idx <= t_pos[None, :, None])[:, None])
        return jnp.einsum('bhtk,btkd->bthd', p.astype(dt), vg)

    out = unblock(lax.map(block, jnp.arange(S // T)))
    return out.reshape(B, S, DSA_HEADS * d)

def hybrid_mixer(h, w_in, w_gate, nsa_q_norm, nsa_k_norm, nsa_cmp_pe, nsa_cmp_w1, nsa_cmp_w2,
                 dsa_q_norm, dsa_k_norm, w_br_a, w_br_b, w_br_c, w_out, cos, sin, cos_i, sin_i):
    B, S, _ = h.shape
    offs = np.cumsum(IN_WIDTHS)[:-1].tolist()
    (sb_q, sb_k, sb_v, nq, nkc, nvc, nks, nvs, nkw, nvw, ngate,
     dq, dk, dv, iq, ik, iw) = jnp.split(h @ w_in, offs, axis=-1)

    def heads(t, n, d):
        return t.reshape(B, S, n, d)

    o_a = stick_breaking_attention(heads(sb_q, SB_HEADS, HEAD_DIM), heads(sb_k, SB_HEADS, HEAD_DIM),
                                   heads(sb_v, SB_HEADS, HEAD_DIM)).reshape(B, S, SB_W)
    kv = lambda t: heads(t, NSA_GROUPS, HEAD_DIM)
    o_b = nsa_attention(heads(nq, NSA_HEADS, HEAD_DIM), kv(nkc), kv(nvc), kv(nks), kv(nvs), kv(nkw), kv(nvw),
                        heads(ngate, NSA_HEADS, 3), nsa_q_norm, nsa_k_norm, nsa_cmp_pe, nsa_cmp_w1, nsa_cmp_w2,
                        cos, sin)
    o_c = dsa_attention(heads(dq, DSA_HEADS, HEAD_DIM), dk, dv, heads(iq, DSA_IDX_HEADS, DSA_IDX_DIM), ik, iw,
                        dsa_q_norm, dsa_k_norm, cos, sin, cos_i, sin_i)

    g_a, g_b, g_c = jnp.split(jax.nn.sigmoid(h @ w_gate), 3, axis=-1)
    merged = g_a * (o_a @ w_br_a) + g_b * (o_b @ w_br_b) + g_c * (o_c @ w_br_c)
    return merged @ w_out

def first_inputs(seed: int = 0) -> dict:
    key = jax.random.key(seed)
    ks = jax.random.split(key, 21)
    f32 = jnp.float32

    def normal(k, shape, scale):
        return jax.random.normal(k, shape, f32) * scale

    def gain(k, shape):
        return 1.0 + 0.02 * jax.random.normal(k, shape, f32)

    D, L = D_MODEL, DEPTH
    cmp_in = NSA_CMP_LEN * HEAD_DIM
    return {
        "x": jax.random.normal(ks[0], (BATCH, SEQ, D), f32),
        "ffn1_norm": gain(ks[1], (L, D)),
        "ffn1_w_gu": normal(ks[2], (L, D, 2 * D_FF), D ** -0.5),
        "ffn1_w_down": normal(ks[3], (L, D_FF, D), D_FF ** -0.5),
        "mix_norm": gain(ks[4], (L, D)),
        "w_in": normal(ks[5], (L, D, D_IN), D ** -0.5),
        "w_gate": normal(ks[6], (L, D, 3 * D), D ** -0.5),
        "nsa_q_norm": gain(ks[7], (L, HEAD_DIM)),
        "nsa_k_norm": gain(ks[8], (L, 3, HEAD_DIM)),
        "nsa_cmp_pe": normal(ks[9], (L, 2, NSA_CMP_LEN, HEAD_DIM), 0.1),
        "nsa_cmp_w1": normal(ks[10], (L, 2, cmp_in, NSA_CMP_HIDDEN), cmp_in ** -0.5),
        "nsa_cmp_w2": normal(ks[11], (L, 2, NSA_CMP_HIDDEN, HEAD_DIM), NSA_CMP_HIDDEN ** -0.5),
        "dsa_q_norm": gain(ks[12], (L, HEAD_DIM)),
        "dsa_k_norm": gain(ks[13], (L, HEAD_DIM)),
        "w_br_a": normal(ks[14], (L, SB_W, D), SB_W ** -0.5),
        "w_br_b": normal(ks[15], (L, NSA_QW, D), NSA_QW ** -0.5),
        "w_br_c": normal(ks[16], (L, DSA_QW, D), DSA_QW ** -0.5),
        "w_out": normal(ks[17], (L, D, D), D ** -0.5),
        "ffn2_norm": gain(ks[18], (L, D)),
        "ffn2_w_gu": normal(ks[19], (L, D, 2 * D_FF), D ** -0.5),
        "ffn2_w_down": normal(ks[20], (L, D_FF, D), D_FF ** -0.5),
    }

def first_block(x, ffn1_norm, ffn1_w_gu, ffn1_w_down, mix_norm, w_in, w_gate, nsa_q_norm, nsa_k_norm,
              nsa_cmp_pe, nsa_cmp_w1, nsa_cmp_w2, dsa_q_norm, dsa_k_norm, w_br_a, w_br_b, w_br_c, w_out,
              ffn2_norm, ffn2_w_gu, ffn2_w_down):
    S = x.shape[1]
    pos = jnp.arange(S)
    cos, sin = rope_tables(pos, ROT_DIM)
    cos_i, sin_i = rope_tables(pos, DSA_IDX_ROT)
    for l in range(DEPTH):
        x = x + 0.5 * swiglu_ffn(x, ffn1_norm[l], ffn1_w_gu[l], ffn1_w_down[l])
        h = rms_norm(x, mix_norm[l])
        x = x + hybrid_mixer(h, w_in[l], w_gate[l], nsa_q_norm[l], nsa_k_norm[l], nsa_cmp_pe[l],
                             nsa_cmp_w1[l], nsa_cmp_w2[l], dsa_q_norm[l], dsa_k_norm[l],
                             w_br_a[l], w_br_b[l], w_br_c[l], w_out[l], cos, sin, cos_i, sin_i)
        x = x + 0.5 * swiglu_ffn(x, ffn2_norm[l], ffn2_w_gu[l], ffn2_w_down[l])
    return x


DEPTH_2 = 1

HEADS_PER_GROUP = 8
DILATED_GROUPS = ((128, 1), (512, 4), (2048, 16))
N_GROUPS = len(DILATED_GROUPS)
N_ATTN_HEADS = N_GROUPS * HEADS_PER_GROUP
ATTN_W = N_ATTN_HEADS * HEAD_DIM
ATTN_OUT_W = HEADS_PER_GROUP * HEAD_DIM
BLOCK = 128
REL_BUCKETS = 32
REL_MAX_DISTANCE = 2048
CONV_CHANNELS = D_MODEL
CONV_WIDTH = 31
FFN_HIDDEN = -(-8 * D_MODEL // (3 * 256)) * 256
IN_W = 3 * ATTN_W + 2 * CONV_CHANNELS + 2 * D_MODEL
RMS_EPS = 1e-6
LN_EPS = 1e-5
NEG_INF = -1e30


def rms_norm_2(x, g):
    xf = x.astype(jnp.float32)
    y = xf * lax.rsqrt(jnp.mean(xf * xf, axis=-1, keepdims=True) + RMS_EPS)
    return (y * g.astype(jnp.float32)).astype(x.dtype)

def layer_norm(x, g, b):
    xf = x.astype(jnp.float32)
    mu = jnp.mean(xf, axis=-1, keepdims=True)
    xc = xf - mu
    y = xc * lax.rsqrt(jnp.mean(xc * xc, axis=-1, keepdims=True) + LN_EPS)
    return (y * g.astype(jnp.float32) + b.astype(jnp.float32)).astype(x.dtype)

def rel_bucket(dist):
    max_exact = REL_BUCKETS // 2
    d = jnp.maximum(dist, 0)
    df = jnp.maximum(d, 1).astype(jnp.float32)
    large = max_exact + (jnp.log(df / max_exact) / math.log(REL_MAX_DISTANCE / max_exact)
                         * (REL_BUCKETS - max_exact)).astype(jnp.int32)
    large = jnp.minimum(large, REL_BUCKETS - 1)
    return jnp.where(d < max_exact, d, large)

def dilated_group_attention(q, k, v, bias_tab, window, dilation):
    B, S, H, Dh = q.shape
    span = window // dilation
    L = S // dilation
    nb = -(-L // BLOCK)
    Lp = nb * BLOCK
    n_prev = -(-span // BLOCK)
    kb_len = (n_prev + 1) * BLOCK

    def to_sub(t, front):
        t = t.reshape(B, L, dilation, H, Dh).transpose(0, 2, 1, 3, 4)
        return jnp.pad(t, ((0, 0), (0, 0), (front, Lp - L), (0, 0), (0, 0)))

    qb = to_sub(q, 0).reshape(B, dilation, nb, BLOCK, H, Dh)

    def band(t):
        tb = to_sub(t, n_prev * BLOCK).reshape(B, dilation, nb + n_prev, BLOCK, H, Dh)
        return jnp.concatenate([tb[:, :, j:j + nb] for j in range(n_prev + 1)], axis=3)

    kb, vb = band(k), band(v)
    a = jnp.arange(BLOCK, dtype=jnp.int32)[:, None]
    c = jnp.arange(kb_len, dtype=jnp.int32)[None, :]
    offset = a - c + n_prev * BLOCK
    bias = bias_tab[rel_bucket(offset * dilation)].astype(jnp.float32).transpose(2, 0, 1)
    kj = (jnp.arange(nb, dtype=jnp.int32)[:, None, None] - n_prev) * BLOCK + c[None]
    valid = (offset >= 0) & (offset <= span) & (kj >= 0)

    s = jnp.einsum('brnqhd,brnkhd->brnhqk', qb, kb).astype(jnp.float32) * (Dh ** -0.5) + bias
    s = jnp.where(valid[:, None], s, NEG_INF)
    lse = jax.nn.logsumexp(s, axis=-1)
    p = jnp.exp(s - lse[..., None])
    o = jnp.einsum('brnhqk,brnkhd->brnqhd', p, vb.astype(jnp.float32))
    o = o.reshape(B, dilation, Lp, H, Dh)[:, :, :L].transpose(0, 2, 1, 3, 4).reshape(B, S, H, Dh)
    lse = lse.transpose(0, 1, 2, 4, 3).reshape(B, dilation, Lp, H)[:, :, :L]
    lse = lse.transpose(0, 2, 1, 3).reshape(B, S, H)
    return o, lse

def dilated_attention_mixer(q, k, v, rel_bias_table, w_attn_out):
    B, S = q.shape[0], q.shape[1]
    outs, lses = [], []
    for g, (window, dilation) in enumerate(DILATED_GROUPS):
        tab = rel_bias_table[:, g * HEADS_PER_GROUP:(g + 1) * HEADS_PER_GROUP]
        o_g, lse_g = dilated_group_attention(q[:, :, g], k[:, :, g], v[:, :, g], tab, window, dilation)
        outs.append(o_g)
        lses.append(lse_g)
    alpha = jax.nn.softmax(jnp.stack(lses, axis=0), axis=0)
    o = jnp.einsum('gbsh,gbshd->bshd', alpha, jnp.stack(outs, axis=0))
    o = o.reshape(B, S, ATTN_OUT_W).astype(w_attn_out.dtype)
    return o @ w_attn_out

def conformer_conv_mixer(glu_in, b_glu, w_dw, b_dw, g_ln, b_ln, w_conv_out, b_conv_out):
    h = glu_in + b_glu
    u, gate = jnp.split(h, 2, axis=-1)
    u = u * jax.nn.sigmoid(gate)
    u = lax.conv_general_dilated(
        u, w_dw.reshape(CONV_WIDTH, 1, CONV_CHANNELS).astype(u.dtype),
        window_strides=(1,), padding=[(CONV_WIDTH - 1, 0)],
        dimension_numbers=('NWC', 'WIO', 'NWC'),
        feature_group_count=CONV_CHANNELS) + b_dw
    u = jax.nn.silu(layer_norm(u, g_ln, b_ln))
    return u @ w_conv_out + b_conv_out

def swiglu_ffn_2(h, w_ffn_in, w_ffn_out):
    gate, up = jnp.split(h @ w_ffn_in, 2, axis=-1)
    return (jax.nn.silu(gate) * up) @ w_ffn_out

def second_inputs(seed: int = 0) -> dict:
    key = jax.random.key(seed)
    ks = jax.random.split(key, 20)
    f32 = jnp.float32

    def nrm(k, shape, scale):
        return jax.random.normal(k, shape, f32) * scale

    def gain(k, shape):
        return 1.0 + 0.05 * jax.random.normal(k, shape, f32)

    return {
        "x": jax.random.normal(ks[0], (BATCH, SEQ, D_MODEL), f32),
        "rel_bias_table": nrm(ks[1], (REL_BUCKETS, N_ATTN_HEADS), 0.2),
        "g_pre_mix": gain(ks[2], (DEPTH_2, D_MODEL)),
        "w_in": nrm(ks[3], (DEPTH_2, D_MODEL, IN_W), D_MODEL ** -0.5),
        "b_glu": nrm(ks[4], (DEPTH_2, 2 * CONV_CHANNELS), 0.02),
        "w_dw": nrm(ks[5], (DEPTH_2, CONV_WIDTH, CONV_CHANNELS), CONV_WIDTH ** -0.5),
        "b_dw": nrm(ks[6], (DEPTH_2, CONV_CHANNELS), 0.02),
        "g_conv_ln": gain(ks[7], (DEPTH_2, CONV_CHANNELS)),
        "b_conv_ln": nrm(ks[8], (DEPTH_2, CONV_CHANNELS), 0.02),
        "w_conv_out": nrm(ks[9], (DEPTH_2, CONV_CHANNELS, D_MODEL), CONV_CHANNELS ** -0.5),
        "b_conv_out": nrm(ks[10], (DEPTH_2, D_MODEL), 0.02),
        "w_attn_out": nrm(ks[11], (DEPTH_2, ATTN_OUT_W, D_MODEL), ATTN_OUT_W ** -0.5),
        "w_mix_out": nrm(ks[12], (DEPTH_2, D_MODEL, D_MODEL), D_MODEL ** -0.5),
        "g_post_mix": gain(ks[13], (DEPTH_2, D_MODEL)),
        "g_pre_ffn": gain(ks[14], (DEPTH_2, D_MODEL)),
        "w_ffn_in": nrm(ks[15], (DEPTH_2, D_MODEL, 2 * FFN_HIDDEN), D_MODEL ** -0.5),
        "w_ffn_out": nrm(ks[16], (DEPTH_2, FFN_HIDDEN, D_MODEL), FFN_HIDDEN ** -0.5),
        "g_post_ffn": gain(ks[17], (DEPTH_2, D_MODEL)),
    }

def second_block(x, rel_bias_table, g_pre_mix, w_in, b_glu, w_dw, b_dw, g_conv_ln, b_conv_ln,
              w_conv_out, b_conv_out, w_attn_out, w_mix_out, g_post_mix, g_pre_ffn,
              w_ffn_in, w_ffn_out, g_post_ffn):
    B, S, D = x.shape
    for l in range(DEPTH_2):
        h = rms_norm_2(x, g_pre_mix[l])
        z = h @ w_in[l]
        q, k, v, glu_in, z_ga, z_gc = jnp.split(
            z, np.cumsum([ATTN_W, ATTN_W, ATTN_W, 2 * CONV_CHANNELS, D_MODEL]).tolist(), axis=-1)
        shp = (B, S, N_GROUPS, HEADS_PER_GROUP, HEAD_DIM)
        y_attn = dilated_attention_mixer(q.reshape(shp), k.reshape(shp), v.reshape(shp),
                                         rel_bias_table, w_attn_out[l])
        y_conv = conformer_conv_mixer(glu_in, b_glu[l], w_dw[l], b_dw[l], g_conv_ln[l],
                                      b_conv_ln[l], w_conv_out[l], b_conv_out[l])
        merged = jax.nn.sigmoid(z_ga) * y_attn + jax.nn.sigmoid(z_gc) * y_conv
        x = x + rms_norm_2(merged @ w_mix_out[l], g_post_mix[l])
        h = rms_norm_2(x, g_pre_ffn[l])
        x = x + rms_norm_2(swiglu_ffn_2(h, w_ffn_in[l], w_ffn_out[l]), g_post_ffn[l])
    return x


def setup_inputs(seed=0):
    out = dict(first_inputs(seed))
    for name, value in second_inputs(seed + 1).items():
        if name != "x":
            out[name + "_2"] = value
    return out


def reference(
    x, ffn1_norm, ffn1_w_gu, ffn1_w_down, mix_norm, w_in, w_gate, nsa_q_norm, nsa_k_norm,
    nsa_cmp_pe, nsa_cmp_w1, nsa_cmp_w2, dsa_q_norm, dsa_k_norm, w_br_a, w_br_b, w_br_c, w_out,
    ffn2_norm, ffn2_w_gu, ffn2_w_down, rel_bias_table_2, g_pre_mix_2, w_in_2, b_glu_2, w_dw_2,
    b_dw_2, g_conv_ln_2, b_conv_ln_2, w_conv_out_2, b_conv_out_2, w_attn_out_2, w_mix_out_2,
    g_post_mix_2, g_pre_ffn_2, w_ffn_in_2, w_ffn_out_2, g_post_ffn_2,
):
    x = first_block(
        x, ffn1_norm, ffn1_w_gu, ffn1_w_down, mix_norm, w_in, w_gate, nsa_q_norm, nsa_k_norm,
        nsa_cmp_pe, nsa_cmp_w1, nsa_cmp_w2, dsa_q_norm, dsa_k_norm, w_br_a, w_br_b, w_br_c,
        w_out, ffn2_norm, ffn2_w_gu, ffn2_w_down,
    )
    return second_block(
        x, rel_bias_table_2, g_pre_mix_2, w_in_2, b_glu_2, w_dw_2, b_dw_2, g_conv_ln_2,
        b_conv_ln_2, w_conv_out_2, b_conv_out_2, w_attn_out_2, w_mix_out_2, g_post_mix_2,
        g_pre_ffn_2, w_ffn_in_2, w_ffn_out_2, g_post_ffn_2,
    )


_drawn_inputs = setup_inputs


def setup_inputs(seed=0):
    import zlib

    import numpy as np

    out = dict(_drawn_inputs(seed))
    spreads = {}
    factors = {'ffn1_norm': 2.922,
     'nsa_q_norm': 8.0,
     'nsa_k_norm': 8.0,
     'dsa_q_norm': 8.0,
     'dsa_k_norm': 8.0,
     'ffn2_norm': 4.012,
     'b_glu_2': 24.033,
     'b_conv_ln_2': 24.805,
     'rel_bias_table_2': 8.0,
     'g_pre_mix_2': 8.0,
     'b_dw_2': 31.689,
     'g_conv_ln_2': 8.0,
     'b_conv_out_2': 37.349,
     'g_post_mix_2': 8.0,
     'g_pre_ffn_2': 7.27,
     'g_post_ffn_2': 8.0}
    for name, (base, spread) in spreads.items():
        noise = np.random.default_rng([zlib.crc32(name.encode()), seed]).standard_normal(out[name].shape)
        drawn = base * np.exp(spread * noise) if base else spread * noise
        out[name] = jnp.asarray(drawn.astype(out[name].dtype))
    for name, factor in factors.items():
        out[name] = (out[name] * factor).astype(out[name].dtype)
    return out
```

```python
import math
from contextlib import ExitStack

import numpy as np
import concourse.bass as bass
from concourse import mybir

P = 128
F32 = mybir.dt.float32
F32R = mybir.dt.float32r
ALU = mybir.AluOpType
ACT = mybir.ActivationFunctionType
AX = mybir.AxisListType

D, S, L = 1024, 512, 2
KD = D // P
TB = S // P
DFF = 2816
FT = DFF // P
EPS = 1e-6
LN_EPS = 1e-5
NEG = -1e30

UNIT = 8 * P
SLOTS = 4
AHEAD = 3
FFN_UNITS = 2 * FT + KD * 3

HD, G, SB_H = 64, 2, 4
STRIDE, NC = 16, 32
IDX_D = 32
SMALL = HD + 24 + 8
QS = HD ** -0.5

NG, NH2, CW = 3, 8, 31
CU = S + CW - 1
BW = 640
B2_WIDTHS = dict(b_value=KD, b_gate=KD, b_dw=KD, w_dw=KD * CW, g_ln=KD, b_ln=KD, b_conv_out=KD, g_post_mix=KD, g_post_ffn=KD)
B2 = {n: (sum(list(B2_WIDTHS.values())[:i]), w) for i, (n, w) in enumerate(B2_WIDTHS.items())}
B2_COLS = sum(B2_WIDTHS.values())
SBUF_END = 229344


class Place:

    def __init__(self, nc, start):
        self.nc, self.at, self.most = nc, start, start

    def tensor(self, name, cols, dtype=F32):
        t = self.nc.alloc_sbuf_tensor_at(name, [P, cols], dtype, offset=self.at)
        self.at += -(-cols * 4 // 32) * 32
        assert self.at <= 229368, (name, self.at)
        return t


def program(nc, A, out, layers=L, dumps=()):
    n_units = A["units"].shape[0]

    fixed = Place(nc, 16512)
    x = fixed.tensor("x", KD * S)
    h_hi_at = fixed.at
    h_hi = fixed.tensor("h_hi", KD * S, F32R)
    h_lo = fixed.tensor("h_lo", KD * S, F32R)
    raw = [fixed.tensor(f"unit_raw{s}", UNIT) for s in range(SLOTS)]
    w_hi = [fixed.tensor(f"unit_hi{s}", UNIT, F32R) for s in range(SLOTS)]
    w_lo = [fixed.tensor(f"unit_lo{s}", UNIT, F32R) for s in range(SLOTS)]
    cst = fixed.tensor("constants", A["constants"].shape[1])
    gains = fixed.tensor("gains", A["gains"].shape[2])
    tiny = fixed.tensor("norm_small", 8)
    eps_col = fixed.tensor("eps_col", 2)
    val = [fixed.tensor(f"val{i}", S) for i in range(2)]
    sq = [fixed.tensor(f"sq{i}", S) for i in range(2)]
    ssq = fixed.tensor("ssq", S)
    diag = val[0]
    ident, ones = cst[:, 0:P], cst[:, P:2 * P]
    inv_d_sq = cst[:, 2 * P:3 * P]
    inv_d = inv_d_sq[:, 0:1]
    arena = fixed.at
    ffn = Place(nc, arena)
    act_hi = ffn.tensor("act_hi", FT * S, F32R)
    act_lo = ffn.tensor("act_lo", FT * S, F32R)
    silu = [ffn.tensor(f"silu{i}", S) for i in range(2)]
    mix = Place(nc, arena)
    o_nat = mix.tensor("o_nat", TB * D)
    part3 = Place(nc, mix.at)
    o_hi = part3.tensor("o_hi", KD * S, F32R)
    o_lo = part3.tensor("o_lo", KD * S, F32R)
    m_hi = part3.tensor("m_hi", KD * S, F32R)
    m_lo = part3.tensor("m_lo", KD * S, F32R)
    mc = mix.tensor("mixer_constants", A["mixer_constants"].shape[1])
    heads_t = mix.tensor("heads_t", 12 * S)
    v_nat = mix.tensor("v_nat", TB * 512)
    small = mix.tensor("small", TB * SMALL)
    sb_t = mix.tensor("sb_t", 4 * S)
    kc_t = mix.tensor("kc_t", NC)
    vc_blk = mix.tensor("vc_blk", G * 256)
    part1 = Place(nc, mix.at)
    gn = part1.tensor("mixer_gains", A["mixer_gains"].shape[2])
    xc_hi = [part1.tensor(f"xc_hi{i}", S + STRIDE, F32R) for i in range(4)]
    xc_lo = [part1.tensor(f"xc_lo{i}", S + STRIDE, F32R) for i in range(4)]
    zn = [part1.tensor(f"zn{i}", 512) for i in range(TB)]
    zsq = part1.tensor("zsq", 512)
    kcn = part1.tensor("kcn", P)
    rot = [part1.tensor(f"rot{i}", P) for i in range(2)]
    hid = [part1.tensor(f"hid{i}", P) for i in range(4)]
    hss = part1.tensor("head_sums", 32)
    hstd = part1.tensor("head_std", 32)
    hrs = part1.tensor("head_rstd", 8)
    part2 = Place(nc, mix.at)
    sb_z = part2.tensor("sb_z", 1280)
    sb_a = part2.tensor("sb_a", 1280)
    sb_p = part2.tensor("sb_p", 1280)
    relu, neg_s = val, sq
    index_s = part2.tensor("index_s", S)
    picked = part2.tensor("picked", S)
    mask_k = part2.tensor("mask_k", S)
    prob = [part2.tensor(f"prob{i}", S) for i in range(2)]
    prob_t = [part2.tensor(f"prob_t{i}", S) for i in range(2)]
    cmp_s, cmp_p, cmp_t = (part2.tensor(n, 256) for n in ("cmp_s", "cmp_p", "cmp_t"))
    cmp_m = part2.tensor("cmp_m", 16)
    top8 = part2.tensor("top8", 8)
    neg_m = part2.tensor("neg_m", 80)
    den = part2.tensor("den", 80)
    coef = part2.tensor("coef", 32)
    zsq2 = relu
    sig = [part3.tensor(f"sig{i}", S) for i in range(3)]
    part = [silu_tile for silu_tile in (part3.tensor(f"part{i}", S) for i in range(3))]
    norm_heads = (8, 8, 2)

    def w2(kv):
        return gn[:, 1280 + kv * HD:1280 + (kv + 1) * HD]

    def pe_t(q):
        return gn[:, 1408 + q * STRIDE:1408 + (q + 1) * STRIDE]

    def const(n, cols=[0]):
        cols[0] += n
        return mc[:, cols[0] - n:cols[0]]

    tri, mask_c, mask_strict, mask_cmp = const(P), const(S), const(P), const(TB * NC)
    cos16, sin16, cos8, sin8 = const(TB * 16), const(TB * 16), const(TB * 8), const(TB * 8)
    cos_c, sin_c = const(16), const(16)
    one_col = ones[:, 0:1]
    y = nc.alloc_sbuf_tensor_at("y", [P, KD * S], F32, offset=h_hi_at)
    b2 = nc.alloc_sbuf_tensor_at("block2_columns", [P, B2_COLS], F32, offset=SBUF_END - B2_COLS * 4)
    start = Place(nc, arena)
    tab_rep = start.tensor("bias_table", NG * NH2 * P)
    one_hot = start.tensor("bias_one_hot", NG * BW)
    bias_row = [start.tensor(f"bias_row{i}", BW) for i in range(2)]
    blk = Place(nc, arena)
    u_conv = blk.tensor("u_conv", KD * CU)
    ya = nc.alloc_sbuf_tensor_at("ya", [P, KD * S], F32, offset=arena)
    merge = Place(nc, blk.at)
    m_hi2 = merge.tensor("m_hi2", KD * S, F32R)
    m_lo2 = merge.tensor("m_lo2", KD * S, F32R)
    c_hi = merge.tensor("c_hi", KD * S, F32R)
    c_lo = merge.tensor("c_lo", KD * S, F32R)
    sig2 = [merge.tensor(f"sig2_{i}", S) for i in range(2)]
    part2_ = [merge.tensor(f"part2_{i}", S) for i in range(2)]
    o2 = blk.tensor("o2", TB * NH2 * HD)
    split_o = Place(nc, blk.at)
    o_hi2 = split_o.tensor("o_hi2", 4 * S, F32R)
    o_lo2 = split_o.tensor("o_lo2", 4 * S, F32R)
    v2 = blk.tensor("v2", TB * NG * 512)
    qk = [blk.tensor(f"qk{i}", 6 * S) for i in range(2)]
    neg_s2, prob2, prob_t2 = (blk.tensor(n, 1280) for n in ("neg_s2", "prob2", "prob_t2"))
    bias_t = [blk.tensor(f"bias_t{i}", 1280) for i in range(2)]
    neg_m3 = blk.tensor("neg_m3", 8)
    neg_m2, den2, rden2 = (blk.tensor(n, 32) for n in ("neg_m2", "den2", "rden2"))
    o_bank_cols = slice(256, 256 + HD)
    bias_dram = nc.dram_tensor("bias_rows", (NG * NH2, P * BW), F32, kind="Internal").ap()

    def bc(name, i):
        return b2[:, B2[name][0] + i:B2[name][0] + i + 1]


    def tile(t, k, n=S):
        return t[:, k * n:(k + 1) * n]

    bank = [nc.alloc_psum_tensor(f"bank{i}", [P, S], F32) for i in range(8)]

    o_bank = bank[5][:, 256:256 + HD]

    sem = nc.alloc_semaphore
    loaded, gains_loaded, consts_loaded = sem("x_loaded"), sem("gains_loaded"), sem("constants_loaded")
    raw_full = [sem(f"raw_full{s}") for s in range(SLOTS)]
    unit_hi, unit_lo, unit_used = sem("unit_hi_done"), sem("unit_lo_done"), sem("unit_used")
    arrived, released = sem("arrived"), sem("released")
    passed = sem("passed")
    stored, x_final = sem("stored"), sem("x_final")
    bias_stored = [sem(f"bias_stored{i}") for i in range(2)]
    bias_in = [sem(f"bias_in{i}") for i in range(2)]
    s = {}
    for n in ("gains_in bias_tab_in bias_mm bias_out_a bias_out_v glu qk_out o_out conv job_parts mean centred c_norm c_val c_hi c_lo ya_out x_post y_norm "
              "stat_sum stat_std stat_rs stat_diag rstd h_f32 h_hi h_lo "
              "dve_step x_val x_hi x_lo pad sb_out v_out t_out turned roped small_out hid cmp_mm cmp_turned mixer_in zn head_sum head_std gates vcb_zero "
              "job_red job_sc job_exp job_tr job_pv pt_out sb_z sb_sp sb_c sb_w sb_o sb_d sb_zm sb_abs sb_e sb_ln idx_mm idx_relu idx_acc "
              "cmp_sc cmp_exp cmp_tr cmp_pt cmp_o cmp_sub merged_o o_hi o_lo o_tr sig branches part_sum m_val m_hi m_lo "
              "silu prod act_hi act_lo x_new sq zeroed ssq_add").split():
        s[n] = sem(n)
    nums = [v.num for v in s.values()]
    assert nums == list(range(nums[0], nums[0] + len(nums)))
    phase_sems = range(nums[0], nums[-1] + 1)

    def fence(e, f):
        e.drain().then_inc(arrived, 1)
        if e is nc.gpsimd:
            e.wait_ge(arrived, 4 * f + 4)
            e.sem_inc(passed, 1)
            e.sem_clear(phase_sems)
            e.drain().then_inc(released, 1)
        e.wait_ge(released, f + 1)
        e.sem_inc(passed, 1)

    def split_hi(act, r, u):
        act.wait_ge(raw_full[u % SLOTS], 16 * (r + u // SLOTS + 1))
        if not isinstance(r, int) or r * SLOTS + u >= SLOTS:
            act.wait_ge(unit_used, SLOTS * r + u - (SLOTS - 1))
        nc.scalar.activation(w_hi[u % SLOTS][:], raw[u % SLOTS][:], ACT.Copy).then_inc(unit_hi, 1)

    def split_lo(dve, r, u):
        dve.wait_ge(unit_hi, SLOTS * r + u + 1)
        nc.vector.tensor_tensor(w_lo[u % SLOTS][:], raw[u % SLOTS][:], w_hi[u % SLOTS][:].bitcast(F32),
                                ALU.subtract).then_inc(unit_lo, 1)

    def three(out_ap, w_h, w_l, r_h, r_l, first, last):
        nc.tensor.matmul(out_ap, w_h, r_h, start=first, stop=False)
        nc.tensor.matmul(out_ap, w_h, r_l, start=False, stop=False)
        return nc.tensor.matmul(out_ap, w_l, r_h, start=False, stop=last)

    def unit_product(pe, r, u, dst, hi, lo, k0=0, n=8, first=True, last=True):
        pe.wait_ge(unit_lo, SLOTS * r + u + 1)
        for k in range(n):
            w = slice(k * P, (k + 1) * P)
            mm = three(dst, w_hi[u % SLOTS][:, w], w_lo[u % SLOTS][:, w], tile(hi, k0 + k), tile(lo, k0 + k),
                       first and k == 0, last and k == n - 1)
        mm.then_inc(unit_used, 1)

    def both(e, body, last):
        if last:
            body(0)
            body(1, final=True)
        else:
            with e.Fori(0, 2) as i:
                body(i)

    def stats_pe(pe, use):
        for b in range(TB):
            mm = nc.tensor.matmul(bank[7][:, b:b + 1], ssq[:, b * P:(b + 1) * P], inv_d, start=True, stop=True)
        mm.then_inc(s["stat_sum"], 1)
        pe.wait_ge(s["stat_diag"], TB * (use + 1))
        nc.tensor.matmul(bank[6][:], ones, diag[:], start=True, stop=True).then_inc(s["rstd"], 1)

    def stats_act(act, use, eps):
        act.wait_ge(s["stat_sum"], use + 1)
        nc.scalar.activation(tiny[:, 0:TB], bank[7][:, 0:TB], ACT.Sqrt, bias=eps).then_inc(s["stat_std"], 1)

    def stats_dve(dve, use):
        dve.wait_ge(s["stat_std"], use + 1)
        nc.vector.reciprocal(tiny[:, 4:4 + TB], tiny[:, 0:TB]).then_inc(s["stat_rs"], 1)
        dve.wait_ge(s["stat_rs"], use + 1)
        for b in range(TB):
            nc.vector.tensor_scalar(diag[:, b * P:(b + 1) * P], ident, tiny[:, 4 + b:5 + b], None,
                                    ALU.mult).then_inc(s["stat_diag"], 1)
        dve.wait_ge(s["rstd"], use + 1)

    def norm_pe(pe):
        stats_pe(pe, 0)

    def norm_act(act):
        stats_act(act, 0, eps_col[:, 0:1])
        for k in range(KD):
            act.wait_ge(s["h_f32"], k + 1)
            nc.scalar.activation(tile(h_hi, k), val[k % 2][:], ACT.Copy).then_inc(s["h_hi"], 1)

    def norm_dve(dve, g):
        stats_dve(dve, 0)
        for k in range(KD + 1):
            if k < KD:
                if k >= 2:
                    dve.wait_ge(s["h_lo"], k - 1)
                nc.vector.scalar_tensor_tensor(out=val[k % 2][:], in0=tile(x, k), scalar=gains[:, g + k:g + k + 1],
                                               in1=bank[6][:], op0=ALU.mult, op1=ALU.mult).then_inc(s["h_f32"], 1)
            if k >= 1:
                dve.wait_ge(s["h_hi"], k)
                nc.vector.tensor_tensor(tile(h_lo, k - 1), val[(k - 1) % 2][:], tile(h_hi, k - 1).bitcast(F32),
                                        ALU.subtract).then_inc(s["h_lo"], 1)

    def ffn_pe(pe, f, r, post=False):
        fence(pe, f)
        norm_pe(pe)
        pe.wait_ge(s["h_lo"], KD)
        with pe.Fori(0, FT // 2) as i:
            for t in range(2):
                pe.wait_ge(s["prod"], 2 * i + t + 1)
                for gu in range(2):
                    unit_product(pe, r + i, 2 * t + gu, bank[t + 2 * gu][:], h_hi, h_lo)
        rd = r + FT // 2
        pe.wait_ge(s["act_lo"], FT)
        with pe.Fori(0, 2) as i:
            for t in range(4):
                pe.wait_ge(s["x_new"], 4 * i + t + 1)
                for j, n in enumerate((8, 8, 6)):
                    unit_product(pe, rd + 3 * i, 3 * t + j, bank[4 + t % 2][:], act_hi, act_lo, 8 * j, n, j == 0, j == 2)
        if post:
            pe.wait_ge(s["ssq_add"], 2 + KD)
            stats_pe(pe, 1)

    def ffn_act(act, f, r, load=None, last=False):
        fence(act, f)
        if load is not None:
            act.dma_start(gains[:], A["gains"][load]).then_inc(s["gains_in"], 16)
        norm_act(act)
        with act.Fori(0, FT // 2) as i:
            for t in range(2):
                split_hi(act, r + i, 2 * t + AHEAD)
                act.wait_ge(unit_used, SLOTS * (r + i) + 2 * t + 1)
                nc.scalar.activation(silu[t][:], bank[t][:], ACT.Silu).then_inc(s["silu"], 1)
                split_hi(act, r + i, 2 * t + 1 + AHEAD)
                act.wait_ge(s["prod"], 2 * i + t + 3)
                nc.scalar.activation(act_hi[:, bass.ds(2 * i * S + t * S, S)], val[t][:], ACT.Copy).then_inc(s["act_hi"], 1)
        rd = r + FT // 2
        res = y if last else x

        def down(i, final=False):
            for t in range(4):
                for j in range(3):
                    if not final or 3 * t + j + AHEAD < 12:
                        split_hi(act, rd + 3 * i, 3 * t + j + AHEAD)
                act.wait_ge(s["x_new"], 4 * i + t + 3)
                act.wait_ge(s["ssq_add"], 4 * i + t + 1)
                nc.scalar.activation(sq[t % 2][:], res[:, bass.ds(4 * i * S + t * S, S)], ACT.Square).then_inc(s["sq"], 1)

        both(act, down, last)
        if last:
            stats_act(act, 1, eps_col[:, 0:1])

    def ffn_dve(dve, f, r, g, load=None, last=False):
        fence(dve, f)
        if load is not None:
            dve.wait_ge(s["gains_in"], 16)
        norm_dve(dve, g)
        dve.sem_inc(s["prod"], 2)
        dve.sem_inc(s["x_new"], 2)
        with dve.Fori(0, FT // 2) as i:
            for t in range(2):
                for gu in range(2):
                    split_lo(dve, r + i, 2 * t + gu + AHEAD)
                dve.wait_ge(unit_used, SLOTS * (r + i) + 2 * t + 2)
                dve.wait_ge(s["silu"], 2 * i + t + 1)
                nc.vector.tensor_tensor(val[t][:], silu[t][:], bank[2 + t][:], ALU.mult).then_inc(s["prod"], 1)
                dve.wait_ge(s["act_hi"], 2 * i + t + 1)
                a = bass.ds(2 * i * S + t * S, S)
                nc.vector.tensor_tensor(act_lo[:, a], val[t][:], act_hi[:, a].bitcast(F32),
                                        ALU.subtract).then_inc(s["act_lo"], 1)
        rd = r + FT // 2

        def down(i, final=False):
            for t in range(4):
                for j in range(3):
                    if not final or 3 * t + j + AHEAD < 12:
                        split_lo(dve, rd + 3 * i, 3 * t + j + AHEAD)
                dve.wait_ge(unit_used, SLOTS * (rd + 3 * i) + 3 * t + 3)
                a = bass.ds(4 * i * S + t * S, S)
                if last:
                    ins = nc.vector.tensor_copy(y[:, a], bank[4 + t % 2][:])
                else:
                    ins = nc.vector.scalar_tensor_tensor(out=x[:, a], in0=bank[4 + t % 2][:], scalar=0.5, in1=x[:, a],
                                                         op0=ALU.mult, op1=ALU.add)
                ins.then_inc(s["x_new"], 1)

        both(dve, down, last)
        if last:
            stats_dve(dve, 1)
            post_dve(dve, "g_post_ffn", x_final)

    def ffn_pool(pool, f):
        fence(pool, f)
        pool.wait_ge(s["stat_sum"], 1)
        nc.gpsimd.memset(ssq[:], 0.0).then_inc(s["ssq_add"], 2)
        sum_squares(pool)

    def sum_squares(pool, use=0):
        for m in range(KD):
            pool.wait_ge(s["sq"], KD * use + m + 1)
            pool.wait_ge(s["ssq_add"], (KD + 2) * use + m + 2)
            nc.gpsimd.tensor_tensor(ssq[:], ssq[:], sq[m % 2][:], ALU.add).then_inc(s["ssq_add"], 1)
    NAT_BANKS = ([6, 7, 0, 1], [2, 3, 4, 5])

    def chunk_banks(c):
        return NAT_BANKS[(c + 1) % 2]

    def natural_unit(pe, r, u, banks, k0, nk, cols, first, last):
        pe.wait_ge(unit_lo, SLOTS * r + u + 1)
        for k in range(nk):
            w = slice(k * cols, (k + 1) * cols)
            for b in range(TB):
                t = slice((k0 + k) * S + b * P, (k0 + k) * S + (b + 1) * P)
                mm = three(bank[banks[b]][:, 0:cols], h_hi[:, t], h_lo[:, t], w_hi[u % SLOTS][:, w],
                           w_lo[u % SLOTS][:, w], first and k == 0, last and k == nk - 1)
        mm.then_inc(unit_used, 1)

    def transposes(pe, c, b):
        pe.wait_ge(s["roped"], 4 * c + b + 1)
        for j in range(4):
            mm = nc.tensor.transpose(bank[chunk_banks(c)[b]][:, j * P:(j + 1) * P], zn[b][:, j * P:(j + 1) * P], ident)
        mm.then_inc(s["turned"], 1)

    TURN_AFTER = {15: [(0, 0), (0, 1)], 16: [(0, 2)], 17: [(0, 3)], 19: [(1, 0), (1, 1)], 20: [(1, 2)], 21: [(1, 3)],
                  23: [(2, 0), (2, 1)], 24: [(2, 2)], 25: [(2, 3)]}

    def mix1_pe(pe, f, r):
        fence(pe, f)
        norm_pe(pe)
        pe.wait_ge(s["h_lo"], KD)
        for u in range(6):
            unit_product(pe, r, u, bank[u][:], h_hi, h_lo)
        for u in range(6, 24):
            c = (u - 10) // 4 if u < 22 else 3
            j = (u - 10) % 4 if u < 22 else u - 22
            if j == 0:
                if c == -1:
                    pe.wait_ge(s["x_val"], 4)
                elif c == 0:
                    pe.wait_ge(s["sb_out"], 4)
                elif c == 1:
                    pe.wait_ge(s["v_out"], TB)
                elif c == 2:
                    pe.wait_ge(s["t_out"], TB)
                else:
                    pe.wait_ge(s["t_out"], 2 * TB)
            if c < 3:
                natural_unit(pe, r, u, chunk_banks(c), 2 * j, 2, 512, j == 0, j == 3)
            else:
                natural_unit(pe, r, u, chunk_banks(c), 4 * j, 4, SMALL, j == 0, j == 1)
            for cb in TURN_AFTER.get(u, ()):
                transposes(pe, *cb)
        pe.wait_ge(s["x_lo"], 4)
        pe.wait_ge(s["small_out"], TB)
        for u in range(24, 32):
            kv, part = (u - 24) // 4, (u - 24) % 4
            pe.wait_ge(unit_lo, SLOTS * r + u + 1)
            for g in range(G):
                half = slice(64 * g, 64 * g + 64)
                for i in range(8):
                    pos = 8 * (part % 2) + i
                    q = 2 * kv + part // 2
                    xh = xc_hi[q][half, :].rearrange("p (c l) -> p c l", l=STRIDE)[:, part // 2:part // 2 + NC, pos]
                    xl = xc_lo[q][half, :].rearrange("p (c l) -> p c l", l=STRIDE)[:, part // 2:part // 2 + NC, pos]
                    w = slice(i * P, (i + 1) * P)
                    mm = three(bank[[6, 7, 0, 1][2 * kv + g]][:, 0:NC], w_hi[u % SLOTS][half, w], w_lo[u % SLOTS][half, w],
                               xh, xl, part == 0 and i == 0, part == 3 and i == 7)
            mm.then_inc(unit_used, 1)
            for cb in TURN_AFTER.get(u, ()):
                transposes(pe, *cb)
        pe.wait_ge(s["t_out"], 3 * TB)
        pe.wait_ge(s["hid"], 4)
        for g in range(G):
            mm = nc.tensor.matmul(bank[2][0:NC, g * HD:(g + 1) * HD], hid[2 * 0 + g][:, 0:NC], w2(0), start=True, stop=True)
        for g in range(G):
            mm = nc.tensor.matmul(bank[3][:, g * HD:(g + 1) * HD], hid[2 + g][:, 0:P], w2(1), start=True, stop=True)
        mm.then_inc(s["cmp_mm"], 1)
        pe.wait_ge(s["roped"], 13)
        nc.tensor.transpose(bank[4][:, 0:NC], kcn[0:NC, 0:P], ident[0:NC, 0:NC]).then_inc(s["cmp_turned"], 1)

    def mix1_act(act, f, r, l):
        fence(act, f)
        act.dma_start(mc[:], A["mixer_constants"]).then_inc(s["mixer_in"], 16)
        act.dma_start(gn[:], A["mixer_gains"][l]).then_inc(s["mixer_in"], 16)
        norm_act(act)
        ends = {13: 0, 17: 1, 21: 2}
        act.wait_ge(s["mixer_in"], 32)
        for u in range(32):
            def out_t(c, b):
                act.wait_ge(s["turned"], 4 * c + b + 1)
                src = bank[chunk_banks(c)[b]][:, 0:512].rearrange("p (j t) -> p j t", j=4)
                dst = heads_t[:, 4 * c * S:4 * (c + 1) * S].rearrange("p (j t) -> p j t", j=4)[:, :, b * P:(b + 1) * P]
                for lo, hi, scale in {0: ((0, 4, QS),), 1: ((0, 2, 1.0), (2, 4, QS)), 2: ((0, 4, 1.0),)}[c]:
                    a = nc.scalar.activation(dst[:, lo:hi, :], src[:, lo:hi, :], ACT.Copy, scale=scale)
                a.then_inc(s["t_out"], 1)

            for c in range(3):
                for b, at in enumerate((16, 16, 17, 18)):
                    if u == at + 4 * c:
                        out_t(c, b)
            split_hi(act, r, u + AHEAD)
            if u in (1, 2, 3, 4):
                q = u - 1
                act.wait_ge(s["x_val"], q + 1)
                act.wait_ge(s["pad"], 1)
                nc.scalar.activation(xc_hi[q][:, 0:S], val[q % 2][:], ACT.Copy).then_inc(s["x_hi"], 1)
            if 2 <= u < 6:
                act.wait_ge(unit_used, SLOTS * r + u + 1)
                nc.scalar.activation(sb_t[:, (u - 2) * S:(u - 1) * S], bank[u][:], ACT.Copy,
                                     scale=QS if u < 4 else 1.0).then_inc(s["sb_out"], 1)
            if u == 9:
                act.wait_ge(unit_used, SLOTS * r + u + 1)
                for b in range(TB):
                    nc.scalar.activation(v_nat[:, b * 512:(b + 1) * 512], bank[chunk_banks(-1)[b]][:], ACT.Copy).then_inc(s["v_out"], 1)
            if u in ends:
                act.wait_ge(unit_used, SLOTS * r + u + 1)
                for b in range(TB):
                    if ends[u] >= 1:
                        act.wait_ge(s["turned"], 4 * (ends[u] - 1) + b + 1)
                    nc.scalar.activation(zn[b][:], bank[chunk_banks(ends[u])[b]][:], ACT.Copy).then_inc(s["zn"], 1)
            for c in range(3):
                for b, at in enumerate((14, 14, 15, 15)):
                    if u == at + 4 * c:
                        n = norm_heads[c]
                        act.wait_ge(s["head_sum"], 4 * c + b + 1)
                        nc.scalar.activation(hstd[:, b * 8:b * 8 + n], hss[:, b * 8:b * 8 + n], ACT.Sqrt,
                                             bias=eps_col[:, 0:1], scale=1.0 / HD).then_inc(s["head_std"], 1)
            if u == 23:
                act.wait_ge(unit_used, SLOTS * r + u + 1)
                for b in range(TB):
                    nc.scalar.activation(small[:, b * SMALL:(b + 1) * SMALL], bank[chunk_banks(3)[b]][:, 0:SMALL], ACT.Copy).then_inc(s["small_out"], 1)
            if u in (28, 31):
                kv = 0 if u == 28 else 1
                act.wait_ge(unit_used, SLOTS * r + (28 if kv == 0 else 32))
                for g in range(G):
                    src = bank[[6, 7, 0, 1][2 * kv + g]][:, 0:NC]
                    n = 1 if kv == 0 else 4
                    nc.scalar.activation(hid[2 * kv + g][:, 0:n * NC].rearrange("p (n c) -> p n c", n=n),
                                         src.unsqueeze(1).to_broadcast([P, n, NC]), ACT.Silu).then_inc(s["hid"], 1)
        act.wait_ge(s["small_out"], TB)
        sm = small[:].rearrange("p (b c) -> p b c", b=TB)
        nc.scalar.activation(sm[:, :, HD:HD + 24], sm[:, :, HD:HD + 24], ACT.Sigmoid).then_inc(s["gates"], 1)
        act.wait_ge(s["cmp_mm"], 1)
        nc.scalar.activation(kcn[0:NC, 0:P], bank[2][0:NC, 0:P], ACT.Copy).then_inc(s["zn"], 1)
        act.wait_ge(s["vcb_zero"], 1)
        for g in range(G):
            for h in range(4):
                rows = slice(32 * h, 32 * h + 32)
                nc.scalar.activation(vc_blk[rows, g * 256 + h * HD:g * 256 + (h + 1) * HD],
                                     bank[3][rows, g * HD:(g + 1) * HD], ACT.Copy)
        act.wait_ge(s["head_sum"], 13)
        nc.scalar.activation(hstd[0:NC, 0:2], hss[0:NC, 0:2], ACT.Sqrt, bias=eps_col[0:NC, 0:1],
                             scale=1.0 / HD).then_inc(s["head_std"], 1)
        act.wait_ge(s["cmp_turned"], 1)
        nc.scalar.activation(kc_t[:], bank[4][:, 0:NC], ACT.Copy)

    def mix1_dve(dve, f, r, g_norm):
        fence(dve, f)
        steps = [0]

        def link(ins):
            steps[0] += 1
            ins.then_inc(s["dve_step"], 1)
            dve.wait_ge(s["dve_step"], steps[0])

        norm_dve(dve, g_norm)

        def squares(q, z, rows, n):
            dve.wait_ge(s["zn"], q + 1)
            if q > 0:
                dve.wait_ge(s["head_sum"], q)
                dve.wait_ge(s["roped"], q // 4 * 4)
            link(nc.vector.tensor_tensor(zsq[rows, 0:n * HD], z[rows, 0:n * HD], z[rows, 0:n * HD], ALU.mult))
            b = q % 4 if q < 12 else 0
            nc.vector.tensor_reduce(hss[rows, b * 8:b * 8 + n], zsq[rows, 0:n * HD].rearrange("p (h d) -> p h d", d=HD),
                                    AX.X, ALU.add).then_inc(s["head_sum"], 1)

        def rope(z, rows, n, hd, half, cos, sin):
            zv = z.rearrange("p (h d) -> p h d", d=hd)
            m = n * 2 * half
            pa = rot[0][rows, 0:m].rearrange("p (h d) -> p h d", h=n)
            pb = rot[1][rows, 0:m].rearrange("p (h d) -> p h d", h=n)
            nc.vector.tensor_tensor(pa, zv[:, :, 0:2 * half], cos.unsqueeze(1).to_broadcast([cos.shape[0], n, 2 * half]), ALU.mult)
            nc.vector.tensor_tensor(pb[:, :, 0:half], zv[:, :, half:2 * half],
                                    sin[:, 0:half].unsqueeze(1).to_broadcast([cos.shape[0], n, half]), ALU.mult)
            link(nc.vector.tensor_tensor(pb[:, :, half:2 * half], zv[:, :, 0:half],
                                         sin[:, half:2 * half].unsqueeze(1).to_broadcast([cos.shape[0], n, half]), ALU.mult))
            return nc.vector.tensor_tensor(zv[:, :, 0:2 * half], pa, pb, ALU.add)

        def normalise(q, z, rows, n, gain, cos, sin):
            b = q % 4 if q < 12 else 0
            p = rows.stop
            dve.wait_ge(s["head_std"], q + 1)
            link(nc.vector.reciprocal(hrs[rows, 0:n], hstd[rows, b * 8:b * 8 + n]))
            zv = z[rows, 0:n * HD].rearrange("p (h d) -> p h d", d=HD)
            link(nc.vector.tensor_tensor(zv, zv, hrs[rows, 0:n].unsqueeze(2).to_broadcast([p, n, HD]), ALU.mult))
            link(nc.vector.tensor_tensor(z[rows, 0:n * HD], z[rows, 0:n * HD], gain, ALU.mult))
            return rope(z[rows, 0:n * HD], rows, n, HD, 8, cos, sin)

        every = slice(0, P)
        for u in range(32):
            split_lo(dve, r, u + AHEAD)
            if u in (1, 2, 3, 4):
                q = u - 1
                if q == 0:
                    dve.wait_ge(s["mixer_in"], 32)
                    for t in xc_hi + xc_lo:
                        z = nc.vector.memset(t[:, S:S + STRIDE].bitcast(F32), 0.0)
                    z.then_inc(s["pad"], 1)
                if q >= 2:
                    dve.wait_ge(s["x_lo"], q - 1)
                dve.wait_ge(unit_used, SLOTS * r + 2)
                nc.vector.tensor_tensor(val[q % 2][:].rearrange("p (c l) -> p c l", l=STRIDE),
                                        bank[q // 2][:].rearrange("p (c l) -> p c l", l=STRIDE),
                                        pe_t(q).unsqueeze(1).to_broadcast([P, S // STRIDE, STRIDE]), ALU.add).then_inc(s["x_val"], 1)
                dve.wait_ge(s["x_hi"], q + 1)
                nc.vector.tensor_tensor(xc_lo[q][:, 0:S], val[q % 2][:], xc_hi[q][:, 0:S].bitcast(F32),
                                        ALU.subtract).then_inc(s["x_lo"], 1)
            for c in range(3):
                for pair, at in enumerate((14, 15)):
                    if u != at + 4 * c:
                        continue
                    n = norm_heads[c]
                    blocks = (2 * pair, 2 * pair + 1)
                    for b in blocks:
                        squares(4 * c + b, zn[b], every, n)
                    for b in blocks:
                        last = normalise(4 * c + b, zn[b], every, n, gn[:, c * 512:c * 512 + n * HD],
                                         cos16[:, b * 16:(b + 1) * 16], sin16[:, b * 16:(b + 1) * 16])
                        if c == 2:
                            link(last)
                            last = rope(zn[b][:, 128:512], every, 12, IDX_D, 4, cos8[:, b * 8:(b + 1) * 8], sin8[:, b * 8:(b + 1) * 8])
                        last.then_inc(s["roped"], 1)
        nc.vector.memset(vc_blk[:], 0.0).then_inc(s["vcb_zero"], 1)
        dve.wait_ge(s["gates"], 1)
        sm = small[:].rearrange("p (b c) -> p b c", b=TB)
        nc.vector.tensor_scalar(sm[:, :, HD + 24:HD + 32], sm[:, :, HD + 24:HD + 32], float(np.float32(8 ** -0.5)), float(np.float32(32 ** -0.5)), ALU.mult, ALU.mult)
        rows = slice(0, NC)
        squares(12, kcn, rows, 2)
        normalise(12, kcn, rows, 2, gn[0:NC, 1152:1280], cos_c[0:NC, :], sin_c[0:NC, :]).then_inc(s["roped"], 1)

    def scores_q(tile_i, half, b):
        return heads_t[half, tile_i * S + b * P:tile_i * S + (b + 1) * P]

    def job(b, j):
        n = (b + 1) * P
        if j < 16:
            h, win = j % 8, j // 8
            half = slice(64 * (h // 4), 64 * (h // 4) + 64)
            vcol = SB_H * HD + win * 128 + (h // 4) * HD
            return (scores_q(h % 4, half, b), heads_t[half, (4 + win) * S:(4 + win) * S + n],
                    [v_nat[:, kb * 512 + vcol:kb * 512 + vcol + HD] for kb in range(b + 1)],
                    bank[4 + win][:, h * HD:(h + 1) * HD])
        h = j - 16
        half = slice(64 * (h % 2), 64 * (h % 2) + 64)
        return (scores_q(6 + h // 2, half, b), heads_t[half, 8 * S:8 * S + n],
                [small[:, kb * SMALL:kb * SMALL + HD] for kb in range(b + 1)], bank[7][:, h * HD:(h + 1) * HD])

    JOBS = 20
    SB_OFF = {0: 0, 1: 512, 3: 896, 2: 1024}

    def sb_bank(j):
        return {0: bank[0][:, 0:512], 1: bank[1][:, 0:384], 3: bank[1][:, 384:512], 2: bank[2][:, 0:256]}[j]

    def mix2_pe(pe, f):
        fence(pe, f)
        idx_no = [0]

        def stick(h):
            half = slice(64 * (h % 2), 64 * (h % 2) + 64)
            if h > 0:
                pe.wait_ge(s["job_red"], JOBS * h)
                pe.wait_ge(s["pt_out"], JOBS * h)
            for j in (0, 1, 3, 2):
                mm = nc.tensor.matmul(sb_bank(j), sb_t[half, (2 + h // 2) * S + j * P:(2 + h // 2) * S + (j + 1) * P],
                                      sb_t[half, (h // 2) * S + j * P:(h // 2) * S + S], start=True, stop=True)
            mm.then_inc(s["sb_z"], 1)
            pe.wait_ge(s["sb_sp"], h + 1)
            for j in (0, 1, 3, 2):
                n = S - j * P
                nc.tensor.matmul(sb_bank(j), tri, sb_p[:, SB_OFF[j]:SB_OFF[j] + n], start=True, stop=(j == 3))
                for jj in range(j + 1, 4):
                    mm = nc.tensor.matmul(sb_bank(j)[:, (jj - j) * P:n], ones, sb_p[:, SB_OFF[jj]:SB_OFF[jj] + S - jj * P],
                                          start=False, stop=(jj == 3))
            mm.then_inc(s["sb_c"], 1)
            pe.wait_ge(s["sb_w"], h + 1)
            for b in range(TB):
                for j in range(b + 1):
                    w = SB_OFF[j] + (b - j) * P
                    mm = nc.tensor.matmul(bank[3][:, b * HD:(b + 1) * HD], sb_a[:, w:w + P],
                                          v_nat[:, j * 512 + h * HD:j * 512 + (h + 1) * HD], start=(j == 0), stop=(j == b))
            mm.then_inc(s["sb_o"], 1)

        def index(b):
            n = (b + 1) * P
            for h in range(8):
                q = idx_no[0]
                if q % 8 == 0:
                    pe.wait_ge(s["sb_d"], b + 1)
                if q >= 2:
                    pe.wait_ge(s["idx_relu"], q - 1)
                rows = slice(32 * (h % 4), 32 * (h % 4) + 32)
                nc.tensor.matmul(bank[h % 2][:, 0:n], heads_t[rows, (9 + h // 4) * S + b * P:(9 + h // 4) * S + (b + 1) * P],
                                 heads_t[rows, 11 * S:11 * S + n], start=True, stop=True).then_inc(s["idx_mm"], 1)
                idx_no[0] += 1

        def compressed(b):
            if b > 0:
                pe.wait_ge(s["merged_o"], b)
            for h in range(8):
                half = slice(64 * (h // 4), 64 * (h // 4) + 64)
                mm = nc.tensor.matmul(bank[6 + h // 4][:, h % 4 * NC:(h % 4 + 1) * NC], scores_q(h % 4, half, b), kc_t[half, :], start=True, stop=True)
            mm.then_inc(s["cmp_sc"], 1)
            pe.wait_ge(s["cmp_exp"], b + 1)
            for g in range(G):
                mm = nc.tensor.transpose(bank[7][:, g * P:(g + 1) * P], cmp_p[:, g * P:(g + 1) * P], ident)
            mm.then_inc(s["cmp_tr"], 1)
            pe.wait_ge(s["cmp_pt"], b + 1)
            for g in range(G):
                mm = nc.tensor.matmul(bank[6][:, g * 256:(g + 1) * 256], cmp_t[:, g * P:(g + 1) * P],
                                      vc_blk[:, g * 256:(g + 1) * 256], start=True, stop=True)
            mm.then_inc(s["cmp_o"], 1)

        def scores(b, j):
            q, k, _, _ = job(b, j)
            n = JOBS * b + j
            if j == 0:
                pe.wait_ge(s["sb_out"], b + 1)
                pe.wait_ge(s["sb_d"], b + 1)
                if b > 0:
                    pe.wait_ge(s["idx_relu"], 8 * b)
            if j >= 2:
                pe.wait_ge(s["job_red"], n - 1)
            nc.tensor.matmul(bank[n % 2][:, 0:(b + 1) * P], q, k, start=True, stop=True).then_inc(s["job_sc"], 1)

        def turn(b, j):
            n = JOBS * b + j
            pe.wait_ge(s["job_exp"], n + 1)
            if j >= 2:
                pe.wait_ge(s["pt_out"], n - 1)
            for kb in range(b + 1):
                mm = nc.tensor.transpose(bank[2 + n % 2][:, kb * P:(kb + 1) * P], prob[n % 2][:, kb * P:(kb + 1) * P], ident)
            mm.then_inc(s["job_tr"], 1)

        def values(b, j):
            _, _, v, o = job(b, j)
            n = JOBS * b + j
            pe.wait_ge(s["pt_out"], n + 1)
            for kb in range(b + 1):
                mm = nc.tensor.matmul(o, prob_t[n % 2][:, kb * P:(kb + 1) * P], v[kb], start=(kb == 0), stop=(kb == b))
            mm.then_inc(s["job_pv"], 1)

        for b in range(TB):
            stick(b)
            if b > 0:
                index(b)
            compressed(b)
            for j in range(JOBS + 2):
                if j < JOBS:
                    scores(b, j)
                if 1 <= j <= JOBS:
                    turn(b, j - 1)
                if j >= 2:
                    values(b, j - 2)

    def mix2_act(act, f):
        fence(act, f)
        idx_no = [0]
        for b in range(TB):
            act.wait_ge(s["sb_zm"], b + 1)
            nc.scalar.activation(sb_a[:], sb_z[:], ACT.Abs).then_inc(s["sb_abs"], 1)
            act.wait_ge(s["sb_abs"], b + 1)
            nc.scalar.activation(sb_a[:], sb_a[:], ACT.Exp, scale=-1.0).then_inc(s["sb_e"], 1)
            act.wait_ge(s["sb_e"], b + 1)
            nc.scalar.activation(sb_a[:], sb_a[:], ACT.Ln, bias=one_col).then_inc(s["sb_ln"], 1)
            act.wait_ge(s["sb_d"], b + 1)
            nc.scalar.activation(sb_a[:], sb_a[:], ACT.Exp).then_inc(s["sb_w"], 1)
            act.wait_ge(s["sb_o"], b + 1)
            nc.scalar.activation(o_nat[:].rearrange("p (b c) -> p b c", b=TB)[:, :, b * HD:(b + 1) * HD],
                                 bank[3][:, 0:TB * HD].rearrange("p (b c) -> p b c", b=TB), ACT.Copy).then_inc(s["sb_out"], 1)
            if b > 0:
                n = (b + 1) * P
                for h in range(8):
                    q = idx_no[0]
                    act.wait_ge(s["idx_mm"], q + 1)
                    if q >= 2:
                        act.wait_ge(s["idx_acc"], q - 1)
                    nc.scalar.activation(relu[q % 2][:, 0:n], bank[h % 2][:, 0:n], ACT.Relu).then_inc(s["idx_relu"], 1)
                    idx_no[0] += 1
            act.wait_ge(s["cmp_sub"], b + 1)
            nc.scalar.activation(cmp_p[:], cmp_s[:], ACT.Exp).then_inc(s["cmp_exp"], 1)
            act.wait_ge(s["cmp_tr"], b + 1)
            nc.scalar.activation(cmp_t[:], bank[7][:, 0:256], ACT.Copy).then_inc(s["cmp_pt"], 1)
            for j in range(JOBS + 1):
                n = JOBS * b + j
                w = (b + 1) * P
                if j < JOBS:
                    act.wait_ge(s["job_red"], n + 1)
                    if n >= 2:
                        act.wait_ge(s["job_tr"], n - 1)
                    nc.scalar.activation(prob[n % 2][:, 0:w], neg_s[n % 2][:, 0:w], ACT.Exp, scale=-1.0,
                                         bias=neg_m[:, n:n + 1], accum_out=den[:, n:n + 1]).then_inc(s["job_exp"], 1)
                if j >= 1:
                    m = n - 1
                    act.wait_ge(s["job_tr"], m + 1)
                    if m >= 2:
                        act.wait_ge(s["job_pv"], m - 1)
                    nc.scalar.activation(prob_t[m % 2][:, 0:w], bank[2 + m % 2][:, 0:w], ACT.Copy).then_inc(s["pt_out"], 1)

    def mix2_dve(dve, f):
        fence(dve, f)
        steps = [0]

        def link(ins):
            steps[0] += 1
            ins.then_inc(s["dve_step"], 1)
            dve.wait_ge(s["dve_step"], steps[0])

        sm = small[:].rearrange("p (b c) -> p b c", b=TB)
        idx_no = [0]
        for b in range(TB):
            n = (b + 1) * P
            dve.wait_ge(s["sb_z"], b + 1)
            nc.vector.tensor_copy(sb_z[:, 0:512], bank[0][:])
            nc.vector.tensor_copy(sb_z[:, 512:1024], bank[1][:])
            link(nc.vector.tensor_copy(sb_z[:, 1024:1280], bank[2][:, 0:256]))
            for j in range(4):
                d = sb_z[:, SB_OFF[j]:SB_OFF[j] + P]
                last = nc.vector.tensor_tensor(d, d, mask_strict, ALU.add)
            last.then_inc(s["sb_zm"], 1)
            dve.wait_ge(s["sb_ln"], b + 1)
            nc.vector.scalar_tensor_tensor(out=sb_p[:], in0=sb_z[:], scalar=0.0, in1=sb_a[:], op0=ALU.max,
                                           op1=ALU.add).then_inc(s["sb_sp"], 1)
            dve.wait_ge(s["sb_c"], b + 1)
            nc.vector.tensor_tensor(sb_a[:, 0:512], sb_z[:, 0:512], bank[0][:], ALU.subtract)
            nc.vector.tensor_tensor(sb_a[:, 512:1024], sb_z[:, 512:1024], bank[1][:], ALU.subtract)
            nc.vector.tensor_tensor(sb_a[:, 1024:1280], sb_z[:, 1024:1280], bank[2][:, 0:256], ALU.subtract).then_inc(s["sb_d"], 1)
            if b > 0:
                for h in range(8):
                    q = idx_no[0]
                    dve.wait_ge(s["idx_relu"], q + 1)
                    if h > 0:
                        dve.wait_ge(s["idx_acc"], q)
                    prev = index_s[:, 0:n] if h else mask_c[:, 512 - n:512]
                    nc.vector.scalar_tensor_tensor(out=index_s[:, 0:n], in0=relu[q % 2][:, 0:n], scalar=sm[:, b, HD + 24 + h:HD + 25 + h],
                                                   in1=prev, op0=ALU.mult, op1=ALU.add).then_inc(s["idx_acc"], 1)
                    idx_no[0] += 1
                dve.wait_ge(s["idx_acc"], idx_no[0])
            dve.wait_ge(s["cmp_sc"], b + 1)
            cs = cmp_s[:].rearrange("p (h c) -> p h c", h=8)
            for g in range(G):
                last = nc.vector.tensor_tensor(cs[:, 4 * g:4 * g + 4, :], bank[6 + g][:, 0:P].rearrange("p (h c) -> p h c", h=4),
                                               mask_cmp[:, b * NC:(b + 1) * NC].unsqueeze(1).to_broadcast([P, 4, NC]), ALU.add)
            link(last)
            link(nc.vector.tensor_reduce(cmp_m[:, 0:8], cs, AX.X, ALU.max))
            link(nc.vector.tensor_scalar(cmp_m[:, 0:8], cmp_m[:, 0:8], -1e20, None, ALU.max))
            nc.vector.tensor_tensor(cs, cs, cmp_m[:, 0:8].unsqueeze(2).to_broadcast([P, 8, NC]), ALU.subtract).then_inc(s["cmp_sub"], 1)
            dve.wait_ge(s["cmp_exp"], b + 1)
            link(nc.vector.tensor_reduce(cmp_m[:, 8:16], cmp_p[:].rearrange("p (h c) -> p h c", h=8), AX.X, ALU.add))
            link(nc.vector.tensor_scalar(cmp_m[:, 8:16], cmp_m[:, 8:16], 0.5, None, ALU.max))
            for j in range(JOBS):
                q = JOBS * b + j
                mask = mask_c[:, 512 - n:512] if j < 16 or b == 0 else mask_k[:, 0:n]
                dve.wait_ge(s["job_sc"], q + 1)
                if q >= 2:
                    dve.wait_ge(s["job_exp"], q - 1)
                nc.vector.tensor_tensor_reduce(out=neg_s[q % 2][:, 0:n], in0=bank[q % 2][:, 0:n], in1=mask, scale=-1.0,
                                               scalar=3e38, op0=ALU.add, op1=ALU.min,
                                               accum_out=neg_m[:, q:q + 1]).then_inc(s["job_red"], 1)
                if b > 0 and j < 16:
                    src = index_s if j == 0 else picked
                    link(nc.vector.max(top8[:, 0:8], src[:, 0:n]))
                    link(nc.vector.match_replace(picked[:, 0:n], top8[:, 0:8], src[:, 0:n], -3e38))
                    if j == 15:
                        link(nc.vector.tensor_scalar(mask_k[:, 0:n], picked[:, 0:n], -2e38, NEG, ALU.is_gt, ALU.mult))
            dve.wait_ge(s["job_pv"], JOBS * (b + 1))
            dve.wait_ge(s["cmp_o"], b + 1)
            nc.vector.reciprocal(coef[:, 0:JOBS], den[:, JOBS * b:JOBS * (b + 1)])
            link(nc.vector.reciprocal(coef[:, 20:28], cmp_m[:, 8:16]))
            gate = sm[:, b, HD:HD + 24].rearrange("p (h k) -> p k h", k=3)
            nc.vector.tensor_tensor(coef[:, 0:8], coef[:, 0:8], gate[:, 1, :], ALU.mult)
            nc.vector.tensor_tensor(coef[:, 8:16], coef[:, 8:16], gate[:, 2, :], ALU.mult)
            link(nc.vector.tensor_tensor(coef[:, 20:28], coef[:, 20:28], gate[:, 0, :], ALU.mult))
            ob = o_nat[:, b * 1024 + 256:b * 1024 + 768].rearrange("p (h d) -> p h d", d=HD)
            oc = o_nat[:, b * 1024 + 768:b * 1024 + 1024].rearrange("p (h d) -> p h d", d=HD)

            def scaled(dst, src, c, h):
                return nc.vector.tensor_tensor(dst, src[:, 0:h * HD].rearrange("p (h d) -> p h d", d=HD),
                                               coef[:, c:c + h].unsqueeze(2).to_broadcast([P, h, HD]), ALU.mult)

            t0 = zsq2[0][:].rearrange("p (h d) -> p h d", d=HD)
            t1 = zsq2[1][:].rearrange("p (h d) -> p h d", d=HD)
            scaled(oc, bank[7], 16, 4)
            scaled(t0, bank[4], 0, 8)
            scaled(t1, bank[5], 8, 8)
            link(scaled(ob, bank[6], 20, 8))
            link(nc.vector.tensor_tensor(ob, ob, t0, ALU.add))
            nc.vector.tensor_tensor(ob, ob, t1, ALU.add).then_inc(s["merged_o"], 1)

    def mix3_pe(pe, f, r):
        fence(pe, f)
        for t in range(KD):
            if t >= 2:
                pe.wait_ge(s["o_lo"], t - 1)
            for b in range(TB):
                mm = nc.tensor.transpose(bank[6 + t % 2][:, b * P:(b + 1) * P], o_nat[:, b * 1024 + t * P:b * 1024 + (t + 1) * P], ident)
            mm.then_inc(s["o_tr"], 1)
        pe.wait_ge(s["o_lo"], KD)
        with pe.Fori(0, KD) as m:
            for g in range(3):
                pe.wait_ge(s["sig"], 3 * m + g + 1)
                unit_product(pe, r + m, g, bank[g][:], h_hi, h_lo)
            pe.wait_ge(s["branches"], m + 1)
            pe.wait_ge(unit_lo, SLOTS * (r + m) + 3 + 1)
            for k in range(KD):
                br = 0 if k < 2 else 1 if k < 6 else 2
                w = slice(k * P, (k + 1) * P)
                mm = three(bank[3 + br][:], w_hi[3][:, w], w_lo[3][:, w], tile(o_hi, k), tile(o_lo, k), k in (0, 2, 6), k in (1, 5, 7))
            mm.then_inc(unit_used, 1)
        pe.wait_ge(s["m_lo"], KD)
        rd = r + KD
        with pe.Fori(0, 2) as i:
            for t in range(4):
                pe.wait_ge(s["x_new"], 4 * i + t + 1)
                unit_product(pe, rd + i, t, bank[6 + t % 2][:], m_hi, m_lo)

    def mix3_act(act, f, r):
        fence(act, f)
        for t in range(KD):
            act.wait_ge(s["o_tr"], t + 1)
            nc.scalar.activation(tile(o_hi, t), bank[6 + t % 2][:], ACT.Copy).then_inc(s["o_hi"], 1)
        act.sem_inc(s["sig"], 3)
        with act.Fori(0, KD) as m:
            for g in range(3):
                split_hi(act, r + m, g + AHEAD)
                act.wait_ge(unit_used, SLOTS * (r + m) + g + 1)
                act.wait_ge(s["branches"], m + 1)
                nc.scalar.activation(sig[g][:], bank[g][:], ACT.Sigmoid).then_inc(s["sig"], 1)
            split_hi(act, r + m, 3 + AHEAD)
            act.wait_ge(s["m_val"], m + 1)
            nc.scalar.activation(m_hi[:, bass.ds(m * S, S)], val[0][:], ACT.Copy).then_inc(s["m_hi"], 1)
        rd = r + KD
        with act.Fori(0, 2) as i:
            for t in range(4):
                split_hi(act, rd + i, t + AHEAD)
                act.wait_ge(s["x_new"], 4 * i + t + 3)
                act.wait_ge(s["ssq_add"], 4 * i + t + 1)
                nc.scalar.activation(sq[t % 2][:], x[:, bass.ds(4 * i * S + t * S, S)], ACT.Square).then_inc(s["sq"], 1)

    def mix3_dve(dve, f, r):
        fence(dve, f)
        dve.sem_inc(s["x_new"], 2)
        dve.sem_inc(s["branches"], 1)
        for t in range(KD):
            dve.wait_ge(s["o_hi"], t + 1)
            nc.vector.tensor_tensor(tile(o_lo, t), bank[6 + t % 2][:], tile(o_hi, t).bitcast(F32), ALU.subtract).then_inc(s["o_lo"], 1)
        with dve.Fori(0, KD) as m:
            for g in range(4):
                split_lo(dve, r + m, g + AHEAD)
            dve.wait_ge(unit_used, SLOTS * (r + m) + 4)
            dve.wait_ge(s["sig"], 3 * m + 6)
            nc.vector.tensor_tensor(part[0][:], sig[0][:], bank[3][:], ALU.mult)
            nc.vector.tensor_tensor(part[1][:], sig[1][:], bank[4][:], ALU.mult)
            nc.vector.tensor_tensor(part[2][:], sig[2][:], bank[5][:], ALU.mult).then_inc(s["branches"], 1)
            dve.wait_ge(s["branches"], m + 2)
            nc.vector.tensor_tensor(part[0][:], part[0][:], part[1][:], ALU.add).then_inc(s["part_sum"], 1)
            dve.wait_ge(s["part_sum"], m + 1)
            nc.vector.tensor_tensor(val[0][:], part[0][:], part[2][:], ALU.add).then_inc(s["m_val"], 1)
            dve.wait_ge(s["m_hi"], m + 1)
            a = bass.ds(m * S, S)
            nc.vector.tensor_tensor(m_lo[:, a], val[0][:], m_hi[:, a].bitcast(F32), ALU.subtract).then_inc(s["m_lo"], 1)
        rd = r + KD
        with dve.Fori(0, 2) as i:
            for t in range(4):
                split_lo(dve, rd + i, t + AHEAD)
                dve.wait_ge(unit_used, SLOTS * (rd + i) + t + 1)
                xm = x[:, bass.ds(4 * i * S + t * S, S)]
                nc.vector.tensor_tensor(xm, xm, bank[6 + t % 2][:], ALU.add).then_inc(s["x_new"], 1)

    def mix3_pool(pool, f):
        fence(pool, f)
        nc.gpsimd.memset(ssq[:], 0.0).then_inc(s["ssq_add"], 2)
        sum_squares(pool)

    def bias_rows_pe(pe):
        pe.wait_ge(s["bias_tab_in"], 32)
        for i in range(NG * NH2):
            if i >= 2:
                pe.wait_ge(s["bias_out_a"], i - 1)
                pe.wait_ge(s["bias_out_v"], i - 1)
            lhs = tab_rep[0:33, i * P:(i + 1) * P]
            hot = one_hot[0:33, (i // NH2) * BW:(i // NH2 + 1) * BW]
            nc.tensor.matmul(bank[2 * (i % 2)][:], lhs, hot[:, 0:512], start=True, stop=True)
            nc.tensor.matmul(bank[2 * (i % 2) + 1][:, 0:P], lhs, hot[:, 512:BW], start=True, stop=True).then_inc(s["bias_mm"], 1)

    def bias_loads_act(act):
        act.dma_start(tab_rep[0:33, :], A["bias_table"]).then_inc(s["bias_tab_in"], 16)
        act.dma_start(one_hot[0:33, :], A["bias_one_hot"]).then_inc(s["bias_tab_in"], 16)

    def bias_rows_act(act, first, end):
        for i in range(first, end):
            act.wait_ge(s["bias_mm"], i + 1)
            if i >= 2:
                act.wait_ge(bias_stored[i % 2], 16 * (i // 2))
            nc.scalar.activation(bias_row[i % 2][:, 0:512], bank[2 * (i % 2)][:], ACT.Copy).then_inc(s["bias_out_a"], 1)

    def bias_rows_dve(dve):
        for i in range(NG * NH2):
            dve.wait_ge(s["bias_mm"], i + 1)
            if i >= 2:
                dve.wait_ge(bias_stored[i % 2], 16 * (i // 2))
            nc.vector.tensor_copy(bias_row[i % 2][:, 512:BW], bank[2 * (i % 2) + 1][:, 0:P]).then_inc(s["bias_out_v"], 1)

    def bias_rows_pool(pool, first, end):
        for i in range(first, end):
            pool.wait_ge(s["bias_out_a"], i + 1)
            pool.wait_ge(s["bias_out_v"], i + 1)
            pool.dma_start(bias_dram[i].rearrange("(a w) -> a w", w=BW), bias_row[i % 2][:]).then_inc(bias_stored[i % 2], 16)

    PAIRS = NH2 // 2
    VB = ([0, 1, 2, 3], [4, 5, 6, 7], [0, 1, 2, 3])

    def spans(b):
        n0, n = min(b + 1, 2) * P, (b + 1) * P
        return ((0, n0), (n0, n), (n0 + n, n)), n0 + 2 * n

    def job2(n):
        return n // 8, n // 4, n % 4

    def qk_tile(p, h, i):
        return slice(64 * (h % 2), 64 * (h % 2) + 64), qk[p % 2], i * S

    def blk1_pe(pe, f, r):
        fence(pe, f)
        norm_pe(pe)
        pe.wait_ge(s["h_lo"], KD)
        for u in range(12):
            g, j = divmod(u, 4)
            if u == 8:
                pe.wait_ge(s["v_out"], TB)
            natural_unit(pe, r, u, VB[g], 2 * j, 2, 512, j == 0, j == 3)
        for u in range(12, 28):
            c, j = divmod(u - 12, 2)
            if j == 0:
                if c < 2:
                    pe.wait_ge(s["v_out"], 2 * TB)
                else:
                    pe.wait_ge(s["glu"], c - 1)
            unit_product(pe, r, u, bank[4 + 2 * (c % 2) + j][:], h_hi, h_lo)

        def sc(n):
            p, h, b = job2(n)
            if n == 0:
                pe.wait_ge(s["v_out"], 3 * TB)
                pe.wait_ge(s["glu"], KD)
            else:
                pe.wait_ge(s["job_red"], n)
            pe.wait_ge(s["qk_out"], 6 * (p + 1))
            for g, (_, w) in enumerate(spans(b)[0]):
                half, t, q0 = qk_tile(p, h, 2 * g)
                _, _, k0 = qk_tile(p, h, 2 * g + 1)
                first_key = (b + 1) * P - w
                mm = nc.tensor.matmul(bank[2 + g][:, 0:w], t[half, q0 + b * P:q0 + (b + 1) * P],
                                      t[half, k0 + first_key:k0 + first_key + w], start=True, stop=True)
            mm.then_inc(s["job_sc"], 1)

        def tr(n):
            b = n % 4
            pe.wait_ge(s["job_exp"], n + 1)
            if n >= 1:
                pe.wait_ge(s["pt_out"], n)
            else:
                pe.wait_ge(s["glu"], KD)
            for g in (1, 2, 0):
                at, w = spans(b)[0][g]
                if g == 0 and n >= 1:
                    pe.wait_ge(s["o_out"], n)
                for kb in range(w // P):
                    mm = nc.tensor.transpose(bank[5 + g][:, kb * P:(kb + 1) * P], prob2[:, at + kb * P:at + (kb + 1) * P], ident)
            mm.then_inc(s["job_tr"], 1)

        def pv(n):
            p, h, b = job2(n)
            pe.wait_ge(s["pt_out"], n + 1)
            if n >= 1:
                pe.wait_ge(s["o_out"], n)
            parts = [(at + kb * P, g, b + 1 - w // P + kb) for g, (at, w) in enumerate(spans(b)[0]) for kb in range(w // P)]
            for i, (col, g, kb) in enumerate(parts):
                v0 = kb * 3 * 512 + g * 512 + h * HD
                mm = nc.tensor.matmul(o_bank, prob_t2[:, col:col + P], v2[:, v0:v0 + HD],
                                      start=(i == 0), stop=(i == len(parts) - 1))
            mm.then_inc(s["job_pv"], 1)

        def slot(p, t):
            if 0 <= t - 2 < 8:
                pv(8 * p + t - 2)
            if 0 <= t - 1 < 8:
                tr(8 * p + t - 1)
            if t < 8:
                sc(8 * p + t)

        for p in range(PAIRS):
            for i in range(6):
                u = 28 + 6 * p + i
                pe.wait_ge(s["v_out"], 3 * TB)
                if 6 * p + i >= 2:
                    pe.wait_ge(s["qk_out"], 6 * p + i - 1)
                pe.wait_ge(unit_lo, SLOTS * r + u + 1)
                for k in range(KD):
                    w = slice(k * P, (k + 1) * P)
                    mm = three(bank[i % 2][:], w_hi[u % SLOTS][:, w], w_lo[u % SLOTS][:, w], tile(h_hi, k), tile(h_lo, k),
                               k == 0, k == KD - 1)
                    if k == 3 and p > 0:
                        slot(p - 1, 2 * i)
                mm.then_inc(unit_used, 1)
                if p > 0:
                    slot(p - 1, 2 * i + 1)
        for t in range(10):
            slot(PAIRS - 1, t)

    def blk1_act(act, f, r):
        fence(act, f)
        act.dma_start(gains[:], A["gains"][L]).then_inc(s["gains_in"], 16)
        act.dma_start(b2[:], A["block2_columns"]).then_inc(s["mixer_in"], 16)
        norm_act(act)
        for u in range(12):
            split_hi(act, r, u + AHEAD)
            if u % 4 == 3:
                g = u // 4
                act.wait_ge(unit_used, SLOTS * r + u + 1)
                for b in range(TB):
                    nc.scalar.activation(v2[:, b * 1536 + g * 512:b * 1536 + (g + 1) * 512], bank[VB[g][b]][:], ACT.Copy).then_inc(s["v_out"], 1)
        act.wait_ge(s["mixer_in"], 16)
        for u in range(12, 28):
            c, j = divmod(u - 12, 2)
            split_hi(act, r, u + AHEAD)
            if j == 1:
                act.wait_ge(unit_used, SLOTS * r + u + 1)
                if c >= 2:
                    act.wait_ge(s["glu"], c - 1)
                nc.scalar.activation(sq[c % 2][:], bank[5 + 2 * (c % 2)][:], ACT.Sigmoid, bias=bc("b_gate", c)).then_inc(s["sig"], 1)

        def slot(p, t):
            if not 1 <= t <= 8:
                return
            n = 8 * p + t - 1
            b = n % 4
            (c0, c1, c2), width = spans(b)
            act.wait_ge(s["job_red"], n + 1)
            if n >= 1:
                act.wait_ge(s["job_tr"], n)
            nc.scalar.activation(prob2[:, 0:width], neg_s2[:, 0:width], ACT.Exp, scale=-1.0, bias=neg_m2[:, n:n + 1],
                                 accum_out=den2[:, n:n + 1]).then_inc(s["job_exp"], 1)
            act.wait_ge(s["job_tr"], n + 1)
            if n >= 1:
                act.wait_ge(s["job_pv"], n)
            for g, (at, w) in enumerate((c0, c1, c2)):
                a = nc.scalar.activation(prob_t2[:, at:at + w], bank[5 + g][:, 0:w], ACT.Copy)
            a.then_inc(s["pt_out"], 1)

        for p in range(PAIRS):
            for i in range(6):
                u = 28 + 6 * p + i
                split_hi(act, r, u + AHEAD)
                if p > 0:
                    slot(p - 1, 2 * i)
                act.wait_ge(unit_used, SLOTS * r + u + 1)
                if p >= 2 and i == 0:
                    act.wait_ge(s["job_pv"], 8 * (p - 1))
                nc.scalar.activation(qk[p % 2][:, i * S:(i + 1) * S], bank[i % 2][:], ACT.Copy,
                                     scale=QS if i % 2 == 0 else 1.0).then_inc(s["qk_out"], 1)
                if p > 0:
                    slot(p - 1, 2 * i + 1)
        for t in range(10):
            slot(PAIRS - 1, t)

    def blk1_dve(dve, f, r):
        fence(dve, f)
        dve.wait_ge(s["gains_in"], 16)
        norm_dve(dve, 0)
        taps = [(c, k) for c in range(KD) for k in range(CW)]
        at = [0]

        def convolve(count, tiles):
            while count > 0 and at[0] < len(taps) and taps[at[0]][0] < tiles:
                c, k = taps[at[0]]
                u0 = c * CU
                w = bc("w_dw", c * CW + k)
                if at[0] > 0:
                    dve.wait_ge(s["conv"], at[0])
                if k == 0:
                    dve.wait_ge(s["glu"], c + 1)
                    ins = nc.vector.tensor_scalar(val[0][:], u_conv[:, u0:u0 + S], w, bc("b_dw", c), ALU.mult, ALU.add)
                else:
                    dst = val[0][:] if k < CW - 1 else u_conv[:, u0 + CW - 1:u0 + CU]
                    ins = nc.vector.scalar_tensor_tensor(out=dst, in0=u_conv[:, u0 + k:u0 + k + S], scalar=w, in1=val[0][:],
                                                         op0=ALU.mult, op1=ALU.add)
                ins.then_inc(s["conv"], 1)
                at[0] += 1
                count -= 1

        for u in range(12):
            split_lo(dve, r, u + AHEAD)
        dve.wait_ge(s["mixer_in"], 16)
        nc.vector.memset(u_conv[:], 0.0).then_inc(s["pad"], 1)
        dve.wait_ge(s["pad"], 1)
        for u in range(12, 28):
            c, j = divmod(u - 12, 2)
            split_lo(dve, r, u + AHEAD)
            if j == 1:
                dve.wait_ge(unit_used, SLOTS * r + u + 1)
                dve.wait_ge(s["sig"], c + 1)
                nc.vector.scalar_tensor_tensor(out=u_conv[:, c * CU + CW - 1:(c + 1) * CU], in0=bank[4 + 2 * (c % 2)][:],
                                               scalar=bc("b_value", c), in1=sq[c % 2][:], op0=ALU.add, op1=ALU.mult).then_inc(s["glu"], 1)
            convolve(6, (u - 11) // 2)

        def slot(p, t):
            if 0 <= t - 2 < 8:
                n = 8 * p + t - 2
                _, h, b = job2(n)
                dve.wait_ge(s["job_pv"], n + 1)
                nc.vector.reciprocal(rden2[:, n:n + 1], den2[:, n:n + 1]).then_inc(s["dve_step"], 1)
                dve.wait_ge(s["dve_step"], n + 1)
                nc.vector.tensor_scalar(o2[:, b * 512 + h * HD:b * 512 + (h + 1) * HD], o_bank, rden2[:, n:n + 1], None,
                                        ALU.mult).then_inc(s["o_out"], 1)
            if t < 8:
                n = 8 * p + t
                _, h, b = job2(n)
                dve.wait_ge(s["job_sc"], n + 1)
                dve.wait_ge(bias_in[h % 2], 16 * 3 * (h // 2 + 1))
                if n >= 1:
                    dve.wait_ge(s["job_exp"], n)
                for g, (c0, w) in enumerate(spans(b)[0]):
                    off = (256, 768, 1280)[g]
                    ins = nc.vector.tensor_tensor_reduce(out=neg_s2[:, c0:c0 + w], in0=bank[2 + g][:, 0:w],
                                                         in1=bias_t[h % 2][:, off - w:off], scale=-1.0, scalar=3e38,
                                                         op0=ALU.add, op1=ALU.min, accum_out=neg_m3[:, g:g + 1])
                ins.then_inc(s["job_parts"], 1)
                dve.wait_ge(s["job_parts"], n + 1)
                nc.vector.tensor_reduce(neg_m2[:, n:n + 1], neg_m3[:, 0:3], AX.X, ALU.min).then_inc(s["job_red"], 1)
                dve.wait_ge(s["job_red"], n + 1)

        for p in range(PAIRS):
            for i in range(6):
                u = 28 + 6 * p + i
                split_lo(dve, r, u + AHEAD)
                for half in range(2):
                    if p > 0:
                        slot(p - 1, 2 * i + half)
                    convolve(3, KD)
        for t in range(10):
            slot(PAIRS - 1, t)
            convolve(3, KD)
        convolve(1000, KD)

    def blk1_pool(pool, f):
        fence(pool, f)
        for h in range(NH2):
            if h >= 2:
                pool.wait_ge(s["job_red"], 4 * (h - 1))
            for g in range(NG):
                src = bias_dram[g * NH2 + h][P - 1:P - 1 + P * (BW - 1)].rearrange("(a w) -> a w", w=BW - 1)
                lo = 256 if g == 0 else 0
                off = (0, 256, 768)[g]
                pool.dma_start(bias_t[h % 2][:, off:off + 512 - lo], src[:, lo:512]).then_inc(bias_in[h % 2], 16)

    def blk2_pe(pe, f, r):
        fence(pe, f)
        for k in range(KD):
            mm = nc.tensor.matmul(bank[5][:], inv_d_sq, u_conv[:, k * CU + CW - 1:(k + 1) * CU], start=(k == 0), stop=(k == KD - 1))
        mm.then_inc(s["mean"], 1)
        for t in range(4):
            if t >= 2:
                pe.wait_ge(s["o_lo"], t - 1)
            for b in range(TB):
                mm = nc.tensor.transpose(bank[t % 2][:, b * P:(b + 1) * P], o2[:, b * 512 + t * P:b * 512 + (t + 1) * P], ident)
            mm.then_inc(s["o_tr"], 1)
        pe.wait_ge(s["ssq_add"], 2 + KD)
        stats_pe(pe, 0)
        pe.wait_ge(s["o_lo"], 4)
        pe.wait_ge(s["c_val"], KD)
        for u in range(4):
            pe.wait_ge(unit_lo, SLOTS * r + u + 1)
            for i in range(2):
                if 2 * u + i >= 2:
                    pe.wait_ge(s["ya_out"], 2 * u + i - 1)
                for k in range(4):
                    w = slice((4 * i + k) * P, (4 * i + k + 1) * P)
                    mm = three(bank[i][:], w_hi[u][:, w], w_lo[u][:, w], tile(o_hi2, k), tile(o_lo2, k), k == 0, k == 3)
            mm.then_inc(unit_used, 1)
        pe.wait_ge(s["ya_out"], KD)
        pe.wait_ge(s["c_lo"], KD)
        with pe.Fori(0, 2) as i:
            for t in range(4):
                pe.wait_ge(s["m_val"], 4 * i + t + 1)
                for j in range(3):
                    hi, lo = (c_hi, c_lo) if j == 2 else (h_hi, h_lo)
                    unit_product(pe, r + 1 + 3 * i, 3 * t + j, bank[3 * (t % 2) + j][:], hi, lo)
        pe.wait_ge(s["m_lo"], KD)
        with pe.Fori(0, 2) as i:
            for t in range(4):
                pe.wait_ge(s["x_new"], 4 * i + t + 1)
                unit_product(pe, r + 7 + i, t, bank[6 + t % 2][:], m_hi2, m_lo2)
        pe.wait_ge(s["ssq_add"], 4 + 2 * KD)
        stats_pe(pe, 1)

    def blk2_act(act, f, r):
        fence(act, f)
        for t in range(4):
            act.wait_ge(s["o_tr"], t + 1)
            nc.scalar.activation(tile(o_hi2, t), bank[t % 2][:], ACT.Copy).then_inc(s["o_hi"], 1)
        for k in range(KD):
            act.wait_ge(s["centred"], k + 1)
            act.wait_ge(s["ssq_add"], k + 1)
            nc.scalar.activation(sq[k % 2][:], u_conv[:, k * CU + CW - 1:(k + 1) * CU], ACT.Square).then_inc(s["sq"], 1)
        stats_act(act, 0, eps_col[:, 1:2])
        for k in range(KD):
            act.wait_ge(s["c_norm"], k + 1)
            nc.scalar.activation(val[k % 2][:], val[k % 2][:], ACT.Silu, bias=bc("b_ln", k)).then_inc(s["c_val"], 1)
            act.wait_ge(s["c_val"], k + 1)
            nc.scalar.activation(tile(c_hi, k), val[k % 2][:], ACT.Copy).then_inc(s["c_hi"], 1)
        for u in range(4):
            split_hi(act, r, u + AHEAD)
            for i in range(2):
                m = 2 * u + i
                act.wait_ge(unit_used, SLOTS * r + u + 1)
                nc.scalar.activation(tile(ya, m), bank[i][:], ACT.Copy).then_inc(s["ya_out"], 1)
        with act.Fori(0, 2) as i:
            for t in range(4):
                for j in range(3):
                    split_hi(act, r + 1 + 3 * i, 3 * t + j + AHEAD)
                    if j < 2:
                        act.wait_ge(unit_used, SLOTS * (r + 1 + 3 * i) + 3 * t + j + 1)
                        act.wait_ge(s["branches"], 4 * i + t + 1)
                        nc.scalar.activation(sig2[j][:], bank[3 * (t % 2) + j][:], ACT.Sigmoid).then_inc(s["sig"], 1)
                act.wait_ge(s["m_val"], 4 * i + t + 3)
                nc.scalar.activation(m_hi2[:, bass.ds(4 * i * S + t * S, S)], val[t % 2][:], ACT.Copy).then_inc(s["m_hi"], 1)
        with act.Fori(0, 2) as i:
            for t in range(4):
                split_hi(act, r + 7 + i, t + AHEAD)
                act.wait_ge(s["x_new"], 4 * i + t + 3)
                act.wait_ge(s["ssq_add"], KD + 2 + 4 * i + t + 1)
                nc.scalar.activation(sq[t % 2][:], y[:, bass.ds(4 * i * S + t * S, S)], ACT.Square).then_inc(s["sq"], 1)
        stats_act(act, 1, eps_col[:, 0:1])
        for k in range(KD):
            act.wait_ge(s["x_post"], k + 1)
            act.wait_ge(s["ssq_add"], 2 * KD + 4 + k + 1)
            nc.scalar.activation(sq[k % 2][:], tile(x, k), ACT.Square).then_inc(s["sq"], 1)

    def blk2_dve(dve, f, r):
        fence(dve, f)
        dve.sem_inc(s["m_val"], 2)
        dve.sem_inc(s["branches"], 1)
        dve.sem_inc(s["x_new"], 2)
        for t in range(4):
            dve.wait_ge(s["o_hi"], t + 1)
            nc.vector.tensor_tensor(tile(o_lo2, t), bank[t % 2][:], tile(o_hi2, t).bitcast(F32), ALU.subtract).then_inc(s["o_lo"], 1)
        dve.wait_ge(s["mean"], 1)
        for k in range(KD):
            uk = u_conv[:, k * CU + CW - 1:(k + 1) * CU]
            nc.vector.tensor_tensor(uk, uk, bank[5][:], ALU.subtract).then_inc(s["centred"], 1)
        stats_dve(dve, 0)
        for k in range(KD + 1):
            if k < KD:
                if k >= 2:
                    dve.wait_ge(s["c_lo"], k - 1)
                nc.vector.scalar_tensor_tensor(out=val[k % 2][:], in0=u_conv[:, k * CU + CW - 1:(k + 1) * CU],
                                               scalar=bc("g_ln", k), in1=bank[6][:], op0=ALU.mult, op1=ALU.mult).then_inc(s["c_norm"], 1)
            if k >= 1:
                dve.wait_ge(s["c_hi"], k)
                nc.vector.tensor_tensor(tile(c_lo, k - 1), val[(k - 1) % 2][:], tile(c_hi, k - 1).bitcast(F32),
                                        ALU.subtract).then_inc(s["c_lo"], 1)
        for u in range(4):
            split_lo(dve, r, u + AHEAD)
        with dve.Fori(0, 2) as i:
            for t in range(4):
                for j in range(3):
                    split_lo(dve, r + 1 + 3 * i, 3 * t + j + AHEAD)
                dve.wait_ge(unit_used, SLOTS * (r + 1 + 3 * i) + 3 * t + 3)
                dve.wait_ge(s["sig"], 8 * i + 2 * t + 2)
                a = bass.ds(4 * i * S + t * S, S)
                nc.vector.tensor_tensor(part2_[0][:], sig2[0][:], ya[:, a], ALU.mult)
                nc.vector.scalar_tensor_tensor(out=part2_[1][:], in0=bank[3 * (t % 2) + 2][:], scalar=b2[:, bass.ds(B2["b_conv_out"][0] + 4 * i + t, 1)],
                                               in1=sig2[1][:], op0=ALU.add, op1=ALU.mult).then_inc(s["branches"], 1)
                dve.wait_ge(s["branches"], 4 * i + t + 2)
                nc.vector.tensor_tensor(val[t % 2][:], part2_[0][:], part2_[1][:], ALU.add).then_inc(s["m_val"], 1)
                dve.wait_ge(s["m_hi"], 4 * i + t + 1)
                nc.vector.tensor_tensor(m_lo2[:, a], val[t % 2][:], m_hi2[:, a].bitcast(F32), ALU.subtract).then_inc(s["m_lo"], 1)
        with dve.Fori(0, 2) as i:
            for t in range(4):
                split_lo(dve, r + 7 + i, t + AHEAD)
                dve.wait_ge(unit_used, SLOTS * (r + 7 + i) + t + 1)
                nc.vector.tensor_copy(y[:, bass.ds(4 * i * S + t * S, S)], bank[6 + t % 2][:]).then_inc(s["x_new"], 1)
        stats_dve(dve, 1)
        post_dve(dve, "g_post_mix", s["x_post"])

    def blk2_pool(pool, f):
        fence(pool, f)
        nc.gpsimd.memset(ssq[:], 0.0).then_inc(s["ssq_add"], 2)
        sum_squares(pool)
        pool.wait_ge(s["stat_sum"], 1)
        nc.gpsimd.memset(ssq[:], 0.0).then_inc(s["ssq_add"], 2)
        sum_squares(pool, 1)
        pool.wait_ge(s["stat_sum"], 2)
        nc.gpsimd.memset(ssq[:], 0.0).then_inc(s["ssq_add"], 2)
        sum_squares(pool, 2)

    def post_dve(dve, gain, done):
        for k in range(KD):
            if k >= 2:
                dve.wait_ge(done, k - 1)
            nc.vector.scalar_tensor_tensor(out=val[k % 2][:], in0=tile(y, k), scalar=bc(gain, k), in1=bank[6][:],
                                           op0=ALU.mult, op1=ALU.mult).then_inc(s["y_norm"], 1)
            dve.wait_ge(s["y_norm"], k + 1)
            nc.vector.tensor_tensor(tile(x, k), tile(x, k), val[k % 2][:], ALU.add).then_inc(done, 1)

    BIAS_FIRST = 10
    PER_LAYER, PHASES = 52, 5
    R2, F2 = L * PER_LAYER, L * PHASES

    with nc.Block() as block:
        @block.sync
        def _(sp):
            sp.dma_start(cst[:], A["constants"]).then_inc(consts_loaded, 16)
            sp.dma_start(x[:], A["x"]).then_inc(loaded, 16)
            for q in range(SLOTS):
                sp.dma_start(raw[q][:], A["units"][q]).then_inc(raw_full[q], 16)
            with sp.Fori(1, n_units // SLOTS) as r:
                for q in range(SLOTS):
                    sp.wait_ge(unit_lo, SLOTS * r + q - (SLOTS - 1))
                    sp.dma_start(raw[q][:], A["units"][SLOTS * r + q]).then_inc(raw_full[q], 16)
            for k in range(KD):
                sp.wait_ge(x_final, k + 1)
                sp.dma_start(out[:, k * S:(k + 1) * S], tile(x, k)).then_inc(stored, 16)
            sp.wait_ge(stored, 16 * KD)

        @block.tensor
        def _(pe):
            bias_rows_pe(pe)
            pe.wait_ge(consts_loaded, 16)
            with pe.Fori(0, L) as l:
                r, f = l * PER_LAYER, l * PHASES
                ffn_pe(pe, f, r)
                mix1_pe(pe, f + 1, r + 17)
                mix2_pe(pe, f + 2)
                mix3_pe(pe, f + 3, r + 25)
                ffn_pe(pe, f + 4, r + 35)
            blk1_pe(pe, F2, R2)
            blk2_pe(pe, F2 + 1, R2 + 13)
            ffn_pe(pe, F2 + 2, R2 + 22, post=True)

        @block.scalar
        def _(act):
            bias_loads_act(act)
            bias_rows_act(act, 0, BIAS_FIRST)
            act.wait_ge(loaded, 16)
            for m in range(KD):
                act.wait_ge(s["ssq_add"], m + 1)
                nc.scalar.activation(sq[m % 2][:], tile(x, m), ACT.Square).then_inc(s["sq"], 1)
            bias_rows_act(act, BIAS_FIRST, NG * NH2)
            for u in range(AHEAD):
                split_hi(act, 0, u)
            with act.Fori(0, L) as l:
                r, f = l * PER_LAYER, l * PHASES
                ffn_act(act, f, r, load=l)
                mix1_act(act, f + 1, r + 17, l)
                mix2_act(act, f + 2)
                mix3_act(act, f + 3, r + 25)
                ffn_act(act, f + 4, r + 35)
            blk1_act(act, F2, R2)
            blk2_act(act, F2 + 1, R2 + 13)
            ffn_act(act, F2 + 2, R2 + 22, last=True)

        @block.vector
        def _(dve):
            nc.vector.memset(eps_col[:, 0:1], EPS)
            nc.vector.memset(eps_col[:, 1:2], LN_EPS)
            bias_rows_dve(dve)
            dve.wait_ge(consts_loaded, 16)
            dve.wait_ge(loaded, 16)
            for u in range(AHEAD):
                split_lo(dve, 0, u)
            with dve.Fori(0, L) as l:
                r, f = l * PER_LAYER, l * PHASES
                ffn_dve(dve, f, r, 0, load=l)
                mix1_dve(dve, f + 1, r + 17, KD)
                mix2_dve(dve, f + 2)
                mix3_dve(dve, f + 3, r + 25)
                ffn_dve(dve, f + 4, r + 35, 2 * KD)
            blk1_dve(dve, F2, R2)
            blk2_dve(dve, F2 + 1, R2 + 13)
            ffn_dve(dve, F2 + 2, R2 + 22, KD, last=True)

        @block.gpsimd
        def _(pool):
            bias_rows_pool(pool, 0, BIAS_FIRST)
            nc.gpsimd.memset(ssq[:], 0.0).then_inc(s["ssq_add"], 2)
            sum_squares(pool)
            bias_rows_pool(pool, BIAS_FIRST, NG * NH2)
            for q in range(2):
                pool.wait_ge(bias_stored[q], 16 * NG * NH2 // 2)
            with pool.Fori(0, L) as l:
                f = l * PHASES
                ffn_pool(pool, f)
                fence(pool, f + 1)
                fence(pool, f + 2)
                mix3_pool(pool, f + 3)
                ffn_pool(pool, f + 4)
            blk1_pool(pool, F2)
            blk2_pool(pool, F2 + 1)
            ffn_pool(pool, F2 + 2)


def column_tiles(w):
    k, c = w.shape
    return w.reshape(k // P, P, c // P, P).transpose(2, 1, 0, 3)


def whole_units(w):
    return column_tiles(w).reshape(-1, P, UNIT)


def gate_up_units(w):
    return w.reshape(KD, P, 2, FT, P).transpose(3, 2, 1, 0, 4).reshape(2 * FT, P, UNIT)


def down_units(w):
    tiles = column_tiles(w)
    units = np.zeros((KD, 3, P, 8, P), np.float32)
    for j, n in enumerate((8, 8, 6)):
        units[:, j, :, :n] = tiles[:, :, 8 * j:8 * j + n]
    return units.reshape(3 * KD, P, UNIT)


def natural_units(w):
    q = w.shape[1] // 512
    return w.reshape(4, 2, P, q, 512).transpose(3, 0, 2, 1, 4).reshape(4 * q, P, UNIT)


def small_units(w):
    units = np.zeros((2, P, UNIT), np.float32)
    units[:, :, :4 * SMALL] = w.reshape(2, 4, P, SMALL).transpose(0, 2, 1, 3).reshape(2, P, 4 * SMALL)
    return units


def columns(v):
    return v.reshape(-1, P).T


def mixer_units(a, l):
    w, parts, at = a["w_in"][l], {}, 0
    for name, width in (("sb_q", 256), ("sb_k", 256), ("sb_v", 256), ("nq", 512), ("nkc", 128), ("nvc", 128),
                        ("nks", 128), ("nvs", 128), ("nkw", 128), ("nvw", 128), ("gate", 24), ("dq", 256),
                        ("dk", HD), ("dv", HD), ("iq", 256), ("ik", IDX_D), ("iw", 8)):
        parts[name] = w[:, at:at + width]
        at += width
    nq = parts["nq"].reshape(D, G, 4, HD).transpose(0, 2, 1, 3).reshape(D, 512)
    turned = np.concatenate([parts[n] for n in ("nkc", "nvc", "sb_q", "sb_k")], 1)
    values = np.concatenate([parts[n] for n in ("sb_v", "nvs", "nvw")], 1)
    heads = np.concatenate([nq] + [parts[n] for n in ("nks", "nkw", "dq", "dk", "dk", "iq", "ik", "ik", "ik", "ik")], 1)
    small = np.concatenate([parts[n] for n in ("dv", "gate", "iw")], 1)
    w1 = a["nsa_cmp_w1"][l].reshape(2, 4, 8, HD, P).transpose(0, 1, 3, 2, 4).reshape(8, HD, UNIT)
    gates = whole_units(a["w_gate"][l]).reshape(3, KD, P, UNIT)
    branches = whole_units(np.concatenate([a["w_br_a"][l], a["w_br_b"][l], a["w_br_c"][l]], 0))[None]
    return [whole_units(turned), natural_units(values), natural_units(heads), small_units(small),
            np.concatenate([w1, w1], 1), np.concatenate([gates, branches]).transpose(1, 0, 2, 3).reshape(4 * KD, P, UNIT),
            whole_units(a["w_out"][l])]


def block2_units(a):
    w = a["w_in_2"][0]
    aw = NG * NH2 * HD
    q, k, v = w[:, :aw], w[:, aw:2 * aw], w[:, 2 * aw:3 * aw]
    glu, ga, gc = w[:, 3 * aw:3 * aw + 2 * D], w[:, 3 * aw + 2 * D:3 * aw + 3 * D], w[:, 3 * aw + 3 * D:]
    glu = whole_units(glu).reshape(2, KD, P, UNIT).transpose(1, 0, 2, 3).reshape(2 * KD, P, UNIT)
    qk = np.stack([whole_units(q).reshape(NG, NH2 // 2, P, UNIT), whole_units(k).reshape(NG, NH2 // 2, P, UNIT)], 1)
    qk = qk.transpose(2, 0, 1, 3, 4).reshape(-1, P, UNIT)
    ao = column_tiles(a["w_attn_out_2"][0]).reshape(4, 2, P, 4, P).transpose(0, 2, 1, 3, 4).reshape(4, P, UNIT)
    merge = np.stack([whole_units(ga), whole_units(gc), whole_units(a["w_conv_out_2"][0])], 1).reshape(-1, P, UNIT)
    return [natural_units(v), glu, qk, ao, merge, whole_units(a["w_mix_out_2"][0])]


def mixer_gains(a, l):
    q, k, dq, dk = a["nsa_q_norm"][l], a["nsa_k_norm"][l], a["dsa_q_norm"][l], a["dsa_k_norm"][l]
    row = np.concatenate([q] * 8 + [k[1]] * 2 + [k[2]] * 2 + [dq] * 4 + [dk] * 2 + [k[0]] * 2)
    w2 = a["nsa_cmp_w2"][l].transpose(1, 0, 2).reshape(P, 2 * HD)
    pos = a["nsa_cmp_pe"][l].reshape(2, 2, STRIDE, HD).transpose(3, 0, 1, 2).reshape(HD, 4 * STRIDE)
    return np.concatenate([np.broadcast_to(row, (P, len(row))), w2, np.concatenate([pos, pos])], 1)


def rope_table(pos, rot):
    inv = (np.float32(500000.0) ** (-np.arange(0, rot, 2, dtype=np.float32) / np.float32(rot))).astype(np.float32)
    angle = pos.astype(np.float32)[:, None] * inv[None, :]
    c, sn = np.cos(angle), np.sin(angle)
    return np.concatenate([c, c], 1), np.concatenate([-sn, sn], 1)


def by_block(t):
    return t.reshape(TB, P, -1).transpose(1, 0, 2).reshape(P, -1)


def mixer_constants():
    i, t = np.arange(P), np.arange(S)
    later = i[:, None] >= i[None, :]
    causal = np.where(i[:, None] + S - P - t[None, :] >= 0, 0.0, NEG)
    strict = np.where(i[:, None] < i[None, :], 0.0, NEG)
    compressed = np.where(STRIDE * np.arange(NC)[None, :] + 2 * STRIDE - 1 <= t[:, None], 0.0, NEG)
    tables = [by_block(x) for x in (*rope_table(t, 16), *rope_table(t, 8))]
    return np.concatenate([later, causal, strict, by_block(compressed), *tables, *rope_table(STRIDE * i + 2 * STRIDE - 1, 16)],
                          1).astype(np.float32)


def bias_one_hot():
    dist = S - 1 - np.arange(BW)
    d = np.maximum(dist, 0)
    far = 16 + (np.log(np.maximum(d, 1).astype(np.float32) / np.float32(16)) / np.float32(math.log(2048 / 16)) * np.float32(16)).astype(np.int32)
    bucket = np.where(d < 16, d, np.minimum(far, 31))
    out = np.zeros((33, NG, BW), np.float32)
    for g, step in enumerate((1, 4, 16)):
        valid = (dist >= 0) & (dist % step == 0) & (dist <= 128 * step)
        out[bucket[valid], g, np.arange(BW)[valid]] = 1.0
        out[32, g, ~valid] = NEG
    return out.reshape(33, NG * BW)


def layout(a):
    units = []
    for l in range(L):
        units += [gate_up_units(a["ffn1_w_gu"][l]), down_units(a["ffn1_w_down"][l]), *mixer_units(a, l),
                  gate_up_units(a["ffn2_w_gu"][l]), down_units(a["ffn2_w_down"][l])]
    units += [*block2_units(a), gate_up_units(a["w_ffn_in_2"][0]), down_units(a["w_ffn_out_2"][0])]
    gains = [np.concatenate([columns(a[n][l]) for n in ("ffn1_norm", "mix_norm", "ffn2_norm")], 1) for l in range(L)]
    gains.append(np.concatenate([columns(a[n][0]) for n in ("g_pre_mix_2", "g_pre_ffn_2", "g_pre_ffn_2")], 1))
    b_glu = a["b_glu_2"][0]
    block2 = [columns(b_glu[:D]), columns(b_glu[D:]), columns(a["b_dw_2"][0]),
              a["w_dw_2"][0].reshape(CW, KD, P).transpose(2, 1, 0).reshape(P, KD * CW)]
    block2 += [columns(a[n][0]) for n in ("g_conv_ln_2", "b_conv_ln_2", "b_conv_out_2", "g_post_mix_2", "g_post_ffn_2")]
    table = np.ones((33, NG * NH2, P), np.float32)
    table[:32] = a["rel_bias_table_2"][:, :, None]
    return dict(
        x=a["x"][0].reshape(S, KD, P).transpose(2, 1, 0).reshape(P, KD * S),
        units=np.concatenate(units),
        constants=np.concatenate([np.eye(P), np.ones((P, P)), np.full((P, P), 1.0 / D)], 1).astype(np.float32),
        gains=np.stack(gains),
        mixer_constants=mixer_constants(),
        mixer_gains=np.stack([mixer_gains(a, l) for l in range(L)]),
        block2_columns=np.concatenate(block2, 1),
        bias_table=table.reshape(33, NG * NH2 * P),
        bias_one_hot=bias_one_hot(),
    )


def kernel(**inputs):
    import concourse.bacc as bacc
    from concourse.bass_utils import run_bass_kernel_spmd

    nc = bacc.Bacc("TRN2", target_bir_lowering=False, num_devices=1)
    arrays = {n: np.ascontiguousarray(v) for n, v in layout({n: np.asarray(v) for n, v in inputs.items()}).items()}
    aps = {n: nc.dram_tensor(f"in_{n}", v.shape, F32, kind="ExternalInput").ap() for n, v in arrays.items()}
    out = nc.dram_tensor("out_x", (P, KD * S), F32, kind="ExternalOutput").ap()
    program(nc, aps, out)
    got = run_bass_kernel_spmd(nc, [{f"in_{n}": v for n, v in arrays.items()}], core_ids=[0]).results[0]["out_x"]
    return got.reshape(P, KD, S).transpose(2, 1, 0).reshape(1, S, D)
```

```python
import math
from contextlib import ExitStack

import numpy as np
import concourse.bass as bass
from concourse import mybir

P = 128
F32 = mybir.dt.float32
F32R = mybir.dt.float32r
ALU = mybir.AluOpType
ACT = mybir.ActivationFunctionType
AX = mybir.AxisListType

D, S, L = 1024, 512, 2
KD = D // P
TB = S // P
DFF = 2816
FT = DFF // P
EPS = 1e-6
LN_EPS = 1e-5
NEG = -1e30

UNIT = 8 * P
SLOTS = 4
AHEAD = 3
FFN_UNITS = 2 * FT + KD * 3

HD, G, SB_H = 64, 2, 4
STRIDE, NC = 16, 32
IDX_D = 32
GATE = 2 * HD
SMALL = GATE + 24 + 8
QS = HD ** -0.5

NG, NH2, CW = 3, 8, 31
CU = S + CW - 1
BW = 640
B2_WIDTHS = dict(b_value=KD, b_gate=KD, b_dw=KD, w_dw=KD * CW, g_ln=KD, b_ln=KD, b_conv_out=KD, g_post_mix=KD, g_post_ffn=KD)
B2 = {n: (sum(list(B2_WIDTHS.values())[:i]), w) for i, (n, w) in enumerate(B2_WIDTHS.items())}
B2_COLS = sum(B2_WIDTHS.values())
SBUF_END = 229344


class Place:

    def __init__(self, nc, start):
        self.nc, self.at, self.most = nc, start, start

    def tensor(self, name, cols, dtype=F32):
        t = self.nc.alloc_sbuf_tensor_at(name, [P, cols], dtype, offset=self.at)
        self.at += -(-cols * 4 // 32) * 32
        assert self.at <= 229368, (name, self.at)
        return t


def program(nc, A, out, layers=L, dumps=()):
    n_units = A["units"].shape[0]

    fixed = Place(nc, 16512)
    x = fixed.tensor("x", KD * S)
    h_hi_at = fixed.at
    h_hi = fixed.tensor("h_hi", KD * S, F32R)
    h_lo = fixed.tensor("h_lo", KD * S, F32R)
    raw = [fixed.tensor(f"unit_raw{s}", UNIT) for s in range(SLOTS)]
    w_hi = [fixed.tensor(f"unit_hi{s}", UNIT, F32R) for s in range(SLOTS)]
    w_lo = [fixed.tensor(f"unit_lo{s}", UNIT, F32R) for s in range(SLOTS)]
    cst = fixed.tensor("constants", A["constants"].shape[1])
    gains = fixed.tensor("gains", A["gains"].shape[1])
    tiny = fixed.tensor("norm_small", 8)
    eps_col = fixed.tensor("eps_col", 2)
    val = [fixed.tensor(f"val{i}", S) for i in range(2)]
    sq = [fixed.tensor(f"sq{i}", S) for i in range(2)]
    ssq = fixed.tensor("ssq", S)
    diag = val[0]
    ident, ones = cst[:, 0:P], cst[:, P:2 * P]
    inv_d_sq = cst[:, 2 * P:3 * P]
    inv_d = inv_d_sq[:, 0:1]
    arena = fixed.at
    ffn = Place(nc, arena)
    act_hi = ffn.tensor("act_hi", FT * S, F32R)
    act_lo = ffn.tensor("act_lo", FT * S, F32R)
    silu = [ffn.tensor(f"silu{i}", S) for i in range(2)]
    rs_ffn = ffn.tensor("rstd_full_ffn", S)
    mix = Place(nc, arena)
    o_t = mix.tensor("o_t", KD * S)
    rs_full = mix.tensor("rstd_full", S)
    part3 = Place(nc, mix.at)
    o_hi = part3.tensor("o_hi", KD * S, F32R)
    o_lo = part3.tensor("o_lo", KD * S, F32R)
    m_hi = part3.tensor("m_hi", KD * S, F32R)
    m_lo = part3.tensor("m_lo", KD * S, F32R)
    mc = mix.tensor("mixer_constants", A["mixer_constants"].shape[1])
    heads_t = mix.tensor("heads_t", 12 * S)
    v_nat = mix.tensor("v_nat", TB * 512)
    small = mix.tensor("small", TB * SMALL)
    sb_t = mix.tensor("sb_t", 4 * S)
    kc_t = mix.tensor("kc_t", NC)
    vc_blk = mix.tensor("vc_blk", G * 256)
    part1 = Place(nc, mix.at)
    gn = part1.tensor("mixer_gains", A["mixer_gains"].shape[2])
    xc_hi = [part1.tensor(f"xc_hi{i}", S + STRIDE, F32R) for i in range(4)]
    xc_lo = [part1.tensor(f"xc_lo{i}", S + STRIDE, F32R) for i in range(4)]
    zn = [part1.tensor(f"zn{i}", 512) for i in range(TB)]
    zsq = val[0]
    kcn, hss, hstd, hrs = ssq[:, 0:P], ssq[:, P:P + 32], ssq[:, P + 32:P + 64], ssq[:, P + 64:P + 72]
    rot = [part1.tensor(f"rot{i}", P) for i in range(2)]
    hid = [part1.tensor(f"hid{i}", NC if i < 2 else P) for i in range(4)]
    part2 = Place(nc, mix.at)
    sb_z = part2.tensor("sb_z", 1280)
    sb_a = part2.tensor("sb_a", 1280)
    relu, neg_s = val, sq
    index_s, picked, mask_k = ssq, val[0], val[1]
    prob = [part2.tensor(f"prob{i}", 4 * S) for i in range(2)]
    prob_t = [part2.tensor(f"prob_t{i}", S) for i in range(2)]
    cmp_s, cmp_t = (part2.tensor(n, 256) for n in ("cmp_s", "cmp_t"))
    cmp_p = cmp_s
    cmp_m = part2.tensor("cmp_m", 16)
    top8 = part2.tensor("top8", 8)
    neg_m = part2.tensor("neg_m", 80)
    den = part2.tensor("den", 80)
    coef = part2.tensor("coef", 80)
    zsq2 = relu
    sig = [part3.tensor(f"sig{i}", S) for i in range(3)]
    part = [silu_tile for silu_tile in (part3.tensor(f"part{i}", S) for i in range(3))]
    norm_heads = (8, 8, 2)

    def w2(kv):
        return gn[:, 1280 + kv * HD:1280 + (kv + 1) * HD]

    def pe_t(q):
        return gn[:, 1408 + q * STRIDE:1408 + (q + 1) * STRIDE]

    def const(n, cols=[0]):
        cols[0] += n
        return mc[:, cols[0] - n:cols[0]]

    tri, mask_c, mask_strict, mask_cmp = const(P), const(S), const(P), const(TB * NC)
    cos16, sin16, cos8, sin8 = const(TB * 16), const(TB * 16), const(TB * 8), const(TB * 8)
    cos_c, sin_c = const(16), const(16)

    def rstd_col(b):
        return tiny[:, 4 + b:5 + b]

    one_col = ones[:, 0:1]
    y = nc.alloc_sbuf_tensor_at("y", [P, KD * S], F32, offset=h_hi_at)
    b2 = nc.alloc_sbuf_tensor_at("block2_columns", [P, B2_COLS], F32, offset=SBUF_END - B2_COLS * 4)
    start = Place(nc, arena)
    tab_rep = start.tensor("bias_table", NG * NH2 * P)
    one_hot = start.tensor("bias_one_hot", NG * BW)
    bias_row = [start.tensor(f"bias_row{i}", BW) for i in range(2)]
    blk = Place(nc, arena)
    u_conv = blk.tensor("u_conv", KD * CU)
    merge = Place(nc, blk.at)
    m_lo2 = merge.tensor("m_lo2", KD * S, F32R)
    ya = nc.alloc_sbuf_tensor_at("ya", [P, KD * S], F32, offset=merge.at)
    m_hi2 = merge.tensor("m_hi2", KD * S, F32R)
    c_hi_at = merge.at
    c_hi = merge.tensor("c_hi", KD * S, F32R)
    c_lo = merge.tensor("c_lo", KD * S, F32R)
    o_lo2 = nc.alloc_sbuf_tensor_at("o_lo2", [P, 4 * S], F32R, offset=merge.at)
    sig2 = [merge.tensor(f"sig2_{i}", S) for i in range(2)]
    part2_ = [merge.tensor(f"part2_{i}", S) for i in range(2)]
    o2 = blk.tensor("o2", TB * NH2 * HD)
    split_o = Place(nc, blk.at)
    o_hi2 = split_o.tensor("o_hi2", 4 * S, F32R)
    v2 = blk.tensor("v2", TB * NG * 512)
    qk = [blk.tensor(f"qk{i}", 6 * S) for i in range(2)]
    neg_s2, prob2, prob_t2 = (blk.tensor(n, 1280) for n in ("neg_s2", "prob2", "prob_t2"))
    bias_t = [blk.tensor(f"bias_t{i}", 1280) for i in range(2)]
    neg_m3 = blk.tensor("neg_m3", 8)
    neg_m2, den2, rden2 = (blk.tensor(n, 32) for n in ("neg_m2", "den2", "rden2"))
    o_bank_cols = slice(256, 256 + HD)
    y_mix = nc.alloc_sbuf_tensor_at("y_mix", [P, KD * S], F32, offset=c_hi_at)
    bias_dram = nc.dram_tensor("bias_rows", (NG * NH2, P * BW), F32, kind="Internal").ap()

    def bc(name, i):
        return b2[:, B2[name][0] + i:B2[name][0] + i + 1]

    def tile(t, k, n=S):
        return t[:, k * n:(k + 1) * n]

    bank = [nc.alloc_psum_tensor(f"bank{i}", [P, S], F32) for i in range(8)]

    o_bank = bank[5][:, 256:256 + HD]

    sem = nc.alloc_semaphore
    loaded, gains_loaded, consts_loaded = sem("x_loaded"), sem("gains_loaded"), sem("constants_loaded")
    raw_full = [sem(f"raw_full{s}") for s in range(SLOTS)]
    unit_hi, unit_lo, unit_used = sem("unit_hi_done"), sem("unit_lo_done"), sem("unit_used")
    arrived, released = sem("arrived"), sem("released")
    passed = sem("passed")
    stored, x_final = sem("stored"), sem("x_final")
    bias_stored = [sem(f"bias_stored{i}") for i in range(2)]
    bias_in = [sem(f"bias_in{i}") for i in range(2)]
    s = {}
    for n in ("gains_in bias_tab_in bias_mm bias_out_a bias_out_v glu qk_out o_out conv job_parts mean centred c_norm c_val c_hi c_lo ya_out x_post y_norm "
              "stat_sum stat_std stat_rs stat_diag rstd h_f32 h_hi h_lo "
              "dve_step x_val x_hi x_lo pad sb_out v_out t_out turned roped small_out hid cmp_mm cmp_turned mixer_in zn head_sum head_std gates vcb_zero "
              "job_red job_sc job_exp job_tr job_pv pt_out gate up gate_free rs_out hid_n hid_tr coef scaled_a scaled_p cmp_scaled sb_z sb_sp sb_c sb_w sb_o sb_d sb_zm sb_abs sb_e sb_ln idx_mm idx_relu idx_acc "
              "cmp_sc cmp_exp cmp_tr cmp_pt cmp_o cmp_sub merged_o o_hi o_lo o_tr sig branches part_sum m_val m_hi m_lo "
              "silu prod act_hi act_lo x_new sq zeroed ssq_add").split():
        s[n] = sem(n)
    nums = [v.num for v in s.values()]
    assert nums == list(range(nums[0], nums[0] + len(nums)))
    phase_sems = range(nums[0], nums[-1] + 1)

    def fence(e, f):
        e.drain().then_inc(arrived, 1)
        if e is nc.gpsimd:
            e.wait_ge(arrived, 4 * f + 4)
            e.sem_inc(passed, 1)
            e.sem_clear(phase_sems)
            e.drain().then_inc(released, 1)
        e.wait_ge(released, f + 1)
        e.sem_inc(passed, 1)

    def split_hi(act, r, u):
        act.wait_ge(raw_full[u % SLOTS], 16 * (r + u // SLOTS + 1))
        if not isinstance(r, int) or r * SLOTS + u >= SLOTS:
            act.wait_ge(unit_used, SLOTS * r + u - (SLOTS - 1) + 1)
        nc.scalar.activation(w_hi[u % SLOTS][:], raw[u % SLOTS][:], ACT.Copy).then_inc(unit_hi, 1)

    def split_lo(dve, r, u):
        dve.wait_ge(unit_hi, SLOTS * r + u + 1)
        nc.vector.tensor_tensor(w_lo[u % SLOTS][:], raw[u % SLOTS][:], w_hi[u % SLOTS][:].bitcast(F32),
                                ALU.subtract).then_inc(unit_lo, 1)

    def three(out_ap, w_h, w_l, r_h, r_l, first, last):
        nc.tensor.matmul(out_ap, w_h, r_h, start=first, stop=False)
        nc.tensor.matmul(out_ap, w_h, r_l, start=False, stop=False)
        return nc.tensor.matmul(out_ap, w_l, r_h, start=False, stop=last)

    def unit_product(pe, r, u, dst, hi, lo, k0=0, n=8, first=True, last=True):
        pe.wait_ge(unit_lo, SLOTS * r + u + 1)
        for k in range(n):
            w = slice(k * P, (k + 1) * P)
            mm = three(dst, w_hi[u % SLOTS][:, w], w_lo[u % SLOTS][:, w], tile(hi, k0 + k), tile(lo, k0 + k),
                       first and k == 0, last and k == n - 1)
        mm.then_inc(unit_used, 1)

    def both(e, body, last):
        if last:
            body(0)
            body(1, final=True)
        else:
            with e.Fori(0, 2) as i:
                body(i)

    def sum_pe(pe):
        for b in range(TB):
            mm = nc.tensor.matmul(bank[7][:, b:b + 1], ssq[:, b * P:(b + 1) * P], inv_d, start=True, stop=True)
        mm.then_inc(s["stat_sum"], 1)

    def spread_pe(pe, use):
        pe.wait_ge(s["stat_diag"], TB * (use + 1))
        nc.tensor.matmul(bank[6][:], ones, diag[:], start=True, stop=True).then_inc(s["rstd"], 1)

    def stats_pe(pe, use):
        sum_pe(pe)
        spread_pe(pe, use)

    def stats_act(act, use, eps):
        act.wait_ge(s["stat_sum"], use + 1)
        nc.scalar.activation(tiny[:, 0:TB], bank[7][:, 0:TB], ACT.Sqrt, bias=eps).then_inc(s["stat_std"], 1)

    def stats_dve(dve, use):
        dve.wait_ge(s["stat_std"], use + 1)
        nc.vector.reciprocal(tiny[:, 4:4 + TB], tiny[:, 0:TB]).then_inc(s["stat_rs"], 1)
        dve.wait_ge(s["stat_rs"], use + 1)
        for b in range(TB):
            nc.vector.tensor_scalar(diag[:, b * P:(b + 1) * P], ident, tiny[:, 4 + b:5 + b], None,
                                    ALU.mult).then_inc(s["stat_diag"], 1)
        dve.wait_ge(s["rstd"], use + 1)

    def norm_pe(pe):
        stats_pe(pe, 0)

    def norm_act(act):
        stats_act(act, 0, eps_col[:, 0:1])
        for k in range(KD):
            act.wait_ge(s["h_f32"], k + 1)
            nc.scalar.activation(tile(h_hi, k), val[k % 2][:], ACT.Copy).then_inc(s["h_hi"], 1)

    def norm_dve(dve, g):
        stats_dve(dve, 0)
        for k in range(KD + 1):
            if k < KD:
                if k >= 2:
                    dve.wait_ge(s["h_lo"], k - 1)
                nc.vector.scalar_tensor_tensor(out=val[k % 2][:], in0=tile(x, k), scalar=gains[:, g + k:g + k + 1],
                                               in1=bank[6][:], op0=ALU.mult, op1=ALU.mult).then_inc(s["h_f32"], 1)
            if k >= 1:
                dve.wait_ge(s["h_hi"], k)
                nc.vector.tensor_tensor(tile(h_lo, k - 1), val[(k - 1) % 2][:], tile(h_hi, k - 1).bitcast(F32),
                                        ALU.subtract).then_inc(s["h_lo"], 1)

    def scaled_hi(act, xk, hk, gain):
        nc.scalar.activation(hk, xk, ACT.Copy, scale=gain).then_inc(s["h_hi"], 1)

    def scaled_lo(dve, xk, hk, lk, gain, no):
        dve.wait_ge(s["h_hi"], no)
        nc.vector.scalar_tensor_tensor(out=lk, in0=xk, scalar=gain, in1=hk.bitcast(F32), op0=ALU.mult,
                                       op1=ALU.subtract).then_inc(s["h_lo"], 1)

    def ffn_pe(pe, f, r, post=False):
        fence(pe, f)
        sum_pe(pe)

        def gate_up(i, t):
            for gu in range(2):
                unit_product(pe, r + i, 2 * t + gu, bank[t + 2 * gu][:], h_hi, h_lo)

        gate_up(0, 0)
        spread_pe(pe, 0)
        gate_up(0, 1)
        with pe.Fori(1, FT // 2) as i:
            for t in range(2):
                pe.wait_ge(s["prod"], 2 * i + t - 1)
                gate_up(i, t)
        rd = r + FT // 2
        pe.wait_ge(s["act_lo"], FT + 2)
        with pe.Fori(0, 2) as i:
            for t in range(4):
                pe.wait_ge(s["x_new"], 4 * i + t + 1)
                for j, n in enumerate((8, 8, 6)):
                    unit_product(pe, rd + 3 * i, 3 * t + j, bank[4 + t % 2][:], act_hi, act_lo, 8 * j, n, j == 0, j == 2)
        if post:
            pe.wait_ge(s["ssq_add"], 2 + KD)
            stats_pe(pe, 1)

    def ffn_act(act, f, r, g=None, last=False):
        fence(act, f)
        stats_act(act, 0, eps_col[:, 0:1])
        with act.Fori(0, FT // 2) as i:
            for t in range(2):
                split_hi(act, r + i, 2 * t + AHEAD)
                act.wait_ge(s["gate"], 2 * i + t + 1)
                nc.scalar.activation(silu[t][:], silu[t][:], ACT.Silu).then_inc(s["silu"], 1)
                split_hi(act, r + i, 2 * t + 1 + AHEAD)
                act.wait_ge(s["prod"], 2 * i + t + 3)
                nc.scalar.activation(act_hi[:, bass.ds(2 * i * S + t * S, S)], val[t][:], ACT.Copy).then_inc(s["act_hi"], 1)
        rd = r + FT // 2
        res = y if last else x

        def down(i, final=False):
            for t in range(4):
                for j in range(3):
                    if not final or 3 * t + j + AHEAD < 12:
                        split_hi(act, rd + 3 * i, 3 * t + j + AHEAD)
                act.wait_ge(s["x_new"], 4 * i + t + 3)
                act.wait_ge(s["ssq_add"], 4 * i + t + 1)
                a = bass.ds(4 * i * S + t * S, S)
                nc.scalar.activation(sq[t % 2][:], res[:, a], ACT.Square).then_inc(s["sq"], 1)
                if not last:
                    scaled_hi(act, x[:, a], h_hi[:, a], gains[:, bass.ds(g + 4 * i + t, 1)])

        both(act, down, last)
        if last:
            stats_act(act, 1, eps_col[:, 0:1])

    def ffn_dve(dve, f, r, g=None, last=False):
        fence(dve, f)
        dve.sem_inc(s["prod"], 2)
        stats_dve(dve, 0)
        nc.vector.tensor_copy(rs_ffn[:], bank[6][:]).then_inc(s["rs_out"], 1)
        dve.wait_ge(s["rs_out"], 1)
        dve.sem_inc(s["x_new"], 2)
        dve.sem_inc(s["act_lo"], 2)
        with dve.Fori(0, FT // 2) as i:
            for t in range(2):
                for gu in range(2):
                    split_lo(dve, r + i, 2 * t + gu + AHEAD)
                    if gu == 0:
                        dve.wait_ge(unit_used, SLOTS * (r + i) + 2 * t + 1 + 1)
                        dve.wait_ge(s["prod"], 2 * i + t + 1)
                        nc.vector.tensor_tensor(silu[t][:], bank[t][:], rs_ffn[:], ALU.mult).then_inc(s["gate"], 1)
                dve.wait_ge(unit_used, SLOTS * (r + i) + 2 * t + 2 + 1)
                dve.wait_ge(s["silu"], 2 * i + t + 1)
                dve.wait_ge(s["act_lo"], 2 * i + t + 1)
                nc.vector.tensor_tensor(val[t][:], silu[t][:], bank[2 + t][:], ALU.mult).then_inc(s["up"], 1)
                dve.wait_ge(s["up"], 2 * i + t + 1)
                nc.vector.tensor_tensor(val[t][:], val[t][:], rs_ffn[:], ALU.mult).then_inc(s["prod"], 1)
                dve.wait_ge(s["act_hi"], 2 * i + t + 1)
                a = bass.ds(2 * i * S + t * S, S)
                nc.vector.tensor_tensor(act_lo[:, a], val[t][:], act_hi[:, a].bitcast(F32),
                                        ALU.subtract).then_inc(s["act_lo"], 1)
        rd = r + FT // 2

        def down(i, final=False):
            for t in range(4):
                for j in range(3):
                    if not final or 3 * t + j + AHEAD < 12:
                        split_lo(dve, rd + 3 * i, 3 * t + j + AHEAD)
                dve.wait_ge(unit_used, SLOTS * (rd + 3 * i) + 3 * t + 3 + 1)
                a = bass.ds(4 * i * S + t * S, S)
                if last:
                    ins = nc.vector.tensor_copy(y[:, a], bank[4 + t % 2][:])
                else:
                    ins = nc.vector.scalar_tensor_tensor(out=x[:, a], in0=bank[4 + t % 2][:], scalar=0.5, in1=x[:, a],
                                                         op0=ALU.mult, op1=ALU.add)
                ins.then_inc(s["x_new"], 1)
                if not last:
                    scaled_lo(dve, x[:, a], h_hi[:, a], h_lo[:, a], gains[:, bass.ds(g + 4 * i + t, 1)], 4 * i + t + 1)

        both(dve, down, last)
        if last:
            stats_dve(dve, 1)
            post_dve(dve, y, "g_post_ffn", x_final)

    def ffn_pool(pool, f):
        fence(pool, f)
        pool.wait_ge(s["stat_sum"], 1)
        nc.gpsimd.memset(ssq[:], 0.0).then_inc(s["ssq_add"], 2)
        sum_squares(pool)

    def sum_squares(pool, use=0):
        for m in range(KD):
            pool.wait_ge(s["sq"], KD * use + m + 1)
            pool.wait_ge(s["ssq_add"], (KD + 2) * use + m + 2)
            nc.gpsimd.tensor_tensor(ssq[:], ssq[:], sq[m % 2][:], ALU.add).then_inc(s["ssq_add"], 1)
    NAT_BANKS = ([6, 7, 0, 1], [2, 3, 4, 5])

    def chunk_banks(c):
        return NAT_BANKS[(c + 1) % 2]

    def natural_unit(pe, r, u, banks, k0, nk, cols, first, last):
        pe.wait_ge(unit_lo, SLOTS * r + u + 1)
        for k in range(nk):
            w = slice(k * cols, (k + 1) * cols)
            for b in range(TB):
                t = slice((k0 + k) * S + b * P, (k0 + k) * S + (b + 1) * P)
                mm = three(bank[banks[b]][:, 0:cols], h_hi[:, t], h_lo[:, t], w_hi[u % SLOTS][:, w],
                           w_lo[u % SLOTS][:, w], first and k == 0, last and k == nk - 1)
        mm.then_inc(unit_used, 1)

    def transposes(pe, c, b):
        pe.wait_ge(s["roped"], 4 * c + b + 1)
        for j in range(4):
            mm = nc.tensor.transpose(bank[chunk_banks(c)[b]][:, j * P:(j + 1) * P], zn[b][:, j * P:(j + 1) * P], ident)
        mm.then_inc(s["turned"], 1)

    TURN_AFTER = {15: [(0, 0), (0, 1)], 16: [(0, 2)], 17: [(0, 3)], 19: [(1, 0), (1, 1)], 20: [(1, 2)], 21: [(1, 3)],
                  23: [(2, 0), (2, 1)], 24: [(2, 2)], 25: [(2, 3)]}

    def mix1_pe(pe, f, r):
        fence(pe, f)
        sum_pe(pe)
        for u in range(6):
            unit_product(pe, r, u, bank[u][:], h_hi, h_lo)
            if u == 1:
                spread_pe(pe, 0)
        for u in range(6, 24):
            c = (u - 10) // 4 if u < 22 else 3
            j = (u - 10) % 4 if u < 22 else u - 22
            if j == 0:
                if c == -1:
                    pe.wait_ge(s["x_val"], 4)
                elif c == 0:
                    pe.wait_ge(s["sb_out"], 4)
                elif c == 1:
                    pe.wait_ge(s["v_out"], TB)
                elif c == 2:
                    pe.wait_ge(s["t_out"], TB)
                else:
                    pe.wait_ge(s["t_out"], 2 * TB)
            if c < 3:
                natural_unit(pe, r, u, chunk_banks(c), 2 * j, 2, 512, j == 0, j == 3)
            else:
                natural_unit(pe, r, u, chunk_banks(c), 4 * j, 4, SMALL, j == 0, j == 1)
            for cb in TURN_AFTER.get(u, ()):
                transposes(pe, *cb)
        pe.wait_ge(s["x_lo"], 4)
        pe.wait_ge(s["small_out"], TB)
        for u in range(24, 32):
            kv, part = (u - 24) // 4, (u - 24) % 4
            pe.wait_ge(unit_lo, SLOTS * r + u + 1)
            pe.sem_inc(passed, 1)
            for i in range(8):
                pos, q = 8 * (part % 2) + i, 2 * kv + part // 2
                w = slice(i * P, (i + 1) * P)
                for xs, ws in ((xc_hi, w_hi), (xc_lo, w_hi), (xc_hi, w_lo)):
                    for g in range(G):
                        half = slice(64 * g, 64 * g + 64)
                        blocks = xs[q][half, :].rearrange("p (c l) -> p c l", l=STRIDE)[:, part // 2:part // 2 + NC, pos]
                        mm = nc.tensor.matmul(bank[[6, 7, 0, 1][2 * kv + g]][0:NC, 0:P], blocks, ws[u % SLOTS][half, w],
                                              start=(part == 0 and i == 0 and xs is xc_hi and ws is w_hi),
                                              stop=(part == 3 and i == 7 and ws is w_lo))
            mm.then_inc(unit_used, 1)
            for cb in TURN_AFTER.get(u, ()):
                transposes(pe, *cb)
            if u in (28, 31):
                kv = 0 if u == 28 else 1
                pe.wait_ge(s["hid_n"], 2 * kv + 2)
                if kv == 0:
                    pe.wait_ge(s["t_out"], 3 * TB)
                for g in range(G):
                    mm = nc.tensor.transpose(bank[5 - kv][:, g * NC:(g + 1) * NC], zn[2 * kv + g][0:NC, 0:P], ident[0:NC, 0:NC])
                mm.then_inc(s["hid_tr"], 1)
        pe.wait_ge(s["t_out"], 3 * TB)
        pe.wait_ge(s["hid"], 4)
        for g in range(G):
            mm = nc.tensor.matmul(bank[2][0:NC, g * HD:(g + 1) * HD], hid[2 * 0 + g][:, 0:NC], w2(0), start=True, stop=True)
        for g in range(G):
            mm = nc.tensor.matmul(bank[3][:, g * HD:(g + 1) * HD], hid[2 + g][:, 0:P], w2(1), start=True, stop=True)
        mm.then_inc(s["cmp_mm"], 1)
        pe.wait_ge(s["roped"], 13)
        nc.tensor.transpose(bank[5][:, 0:NC], kcn[0:NC, 0:P], ident[0:NC, 0:NC]).then_inc(s["cmp_turned"], 1)

    def mix1_act(act, f, r, l):
        fence(act, f)
        act.dma_start(mc[:], A["mixer_constants"]).then_inc(s["mixer_in"], 16)
        act.dma_start(gn[:], A["mixer_gains"][l]).then_inc(s["mixer_in"], 16)
        stats_act(act, 0, eps_col[:, 0:1])
        ends = {13: 0, 17: 1, 21: 2}
        act.wait_ge(s["mixer_in"], 32)
        for u in range(32):
            def out_t(c, b):
                act.wait_ge(s["turned"], 4 * c + b + 1)
                src = bank[chunk_banks(c)[b]][:, 0:512].rearrange("p (j t) -> p j t", j=4)
                dst = heads_t[:, 4 * c * S:4 * (c + 1) * S].rearrange("p (j t) -> p j t", j=4)[:, :, b * P:(b + 1) * P]
                for lo, hi, scale in {0: ((0, 4, QS),), 1: ((0, 2, 1.0), (2, 4, QS)), 2: ((0, 4, 1.0),)}[c]:
                    a = nc.scalar.activation(dst[:, lo:hi, :], src[:, lo:hi, :], ACT.Copy, scale=scale)
                a.then_inc(s["t_out"], 1)

            for c in range(3):
                for b, at in enumerate((16, 16, 17, 18)):
                    if u == at + 4 * c:
                        out_t(c, b)
            split_hi(act, r, u + AHEAD)
            if u in (1, 2, 3, 4):
                q = u - 1
                act.wait_ge(s["x_val"], q + 1)
                act.wait_ge(s["pad"], 1)
                nc.scalar.activation(xc_hi[q][:, 0:S], val[q % 2][:], ACT.Copy).then_inc(s["x_hi"], 1)
            if u == 9:
                act.wait_ge(s["stat_rs"], 1)
                act.wait_ge(unit_used, SLOTS * r + u + 1 + 1)
                for b in range(TB):
                    nc.scalar.activation(v_nat[:, b * 512:(b + 1) * 512], bank[chunk_banks(-1)[b]][:], ACT.Copy, scale=rstd_col(b)).then_inc(s["v_out"], 1)
            if u in ends:
                act.wait_ge(unit_used, SLOTS * r + u + 1 + 1)
                for b in range(TB):
                    if ends[u] >= 1:
                        act.wait_ge(s["turned"], 4 * (ends[u] - 1) + b + 1)
                    nc.scalar.activation(zn[b][:], bank[chunk_banks(ends[u])[b]][:], ACT.Copy, scale=rstd_col(b)).then_inc(s["zn"], 1)
            for c in range(3):
                for b, at in enumerate((14, 14, 15, 15)):
                    if u == at + 4 * c:
                        n = norm_heads[c]
                        act.wait_ge(s["head_sum"], 4 * c + b + 1)
                        nc.scalar.activation(hstd[:, b * 8:b * 8 + n], hss[:, b * 8:b * 8 + n], ACT.Sqrt,
                                             bias=eps_col[:, 0:1], scale=1.0 / HD).then_inc(s["head_std"], 1)
            if u == 23:
                act.wait_ge(unit_used, SLOTS * r + u + 1 + 1)
                for b in range(TB):
                    nc.scalar.activation(small[:, b * SMALL:(b + 1) * SMALL], bank[chunk_banks(3)[b]][:, 0:SMALL], ACT.Copy, scale=rstd_col(b)).then_inc(s["small_out"], 1)
            if u in (28, 31):
                kv = 0 if u == 28 else 1
                act.wait_ge(unit_used, SLOTS * r + (28 if kv == 0 else 32) + 1)
                act.wait_ge(s["turned"], 3 * TB)
                for g in range(G):
                    nc.scalar.activation(zn[2 * kv + g][0:NC, 0:P], bank[[6, 7, 0, 1][2 * kv + g]][0:NC, 0:P], ACT.Silu).then_inc(s["hid_n"], 1)
            if u in (30, 31):
                kv = u - 30
                act.wait_ge(s["hid_tr"], kv + 1)
                for g in range(G):
                    n = 1 if kv == 0 else 4
                    nc.scalar.activation(hid[2 * kv + g][:, 0:n * NC].rearrange("p (n c) -> p n c", n=n),
                                         bank[5 - kv][:, g * NC:(g + 1) * NC].unsqueeze(1).to_broadcast([P, n, NC]), ACT.Copy).then_inc(s["hid"], 1)
        act.wait_ge(s["small_out"], TB)
        sm = small[:].rearrange("p (b c) -> p b c", b=TB)
        nc.scalar.activation(sm[:, :, GATE:GATE + 24], sm[:, :, GATE:GATE + 24], ACT.Sigmoid).then_inc(s["gates"], 1)
        act.wait_ge(s["cmp_mm"], 1)
        nc.scalar.activation(kcn[0:NC, 0:P], bank[2][0:NC, 0:P], ACT.Copy).then_inc(s["zn"], 1)
        act.wait_ge(s["vcb_zero"], 1)
        for h in range(4):
            rows = slice(32 * h, 32 * h + 32)
            nc.scalar.activation(vc_blk[rows, h * P:(h + 1) * P], bank[3][rows, 0:P], ACT.Copy)
        act.wait_ge(s["head_sum"], 13)
        nc.scalar.activation(hstd[0:NC, 0:2], hss[0:NC, 0:2], ACT.Sqrt, bias=eps_col[0:NC, 0:1],
                             scale=1.0 / HD).then_inc(s["head_std"], 1)
        act.wait_ge(s["cmp_turned"], 1)
        nc.scalar.activation(kc_t[:], bank[5][:, 0:NC], ACT.Copy)

    def mix1_dve(dve, f, r):
        fence(dve, f)
        steps = [0]

        def link(ins):
            steps[0] += 1
            ins.then_inc(s["dve_step"], 1)
            dve.wait_ge(s["dve_step"], steps[0])

        stats_dve(dve, 0)
        nc.vector.tensor_copy(rs_full[:], bank[6][:]).then_inc(s["rs_out"], 1)
        dve.wait_ge(s["rs_out"], 1)

        def squares(q, z, rows, n):
            dve.wait_ge(s["zn"], q + 1)
            if q > 0:
                dve.wait_ge(s["head_sum"], q)
                dve.wait_ge(s["roped"], q // 4 * 4)
            link(nc.vector.tensor_tensor(zsq[rows, 0:n * HD], z[rows, 0:n * HD], z[rows, 0:n * HD], ALU.mult))
            b = q % 4 if q < 12 else 0
            nc.vector.tensor_reduce(hss[rows, b * 8:b * 8 + n], zsq[rows, 0:n * HD].rearrange("p (h d) -> p h d", d=HD),
                                    AX.X, ALU.add).then_inc(s["head_sum"], 1)

        def rope(z, rows, n, hd, half, cos, sin):
            zv = z.rearrange("p (h d) -> p h d", d=hd)
            m = n * 2 * half
            pa = rot[0][rows, 0:m].rearrange("p (h d) -> p h d", h=n)
            pb = rot[1][rows, 0:m].rearrange("p (h d) -> p h d", h=n)
            nc.vector.tensor_tensor(pa, zv[:, :, 0:2 * half], cos.unsqueeze(1).to_broadcast([cos.shape[0], n, 2 * half]), ALU.mult)
            nc.vector.tensor_tensor(pb[:, :, 0:half], zv[:, :, half:2 * half],
                                    sin[:, 0:half].unsqueeze(1).to_broadcast([cos.shape[0], n, half]), ALU.mult)
            link(nc.vector.tensor_tensor(pb[:, :, half:2 * half], zv[:, :, 0:half],
                                         sin[:, half:2 * half].unsqueeze(1).to_broadcast([cos.shape[0], n, half]), ALU.mult))
            return nc.vector.tensor_tensor(zv[:, :, 0:2 * half], pa, pb, ALU.add)

        def normalise(q, z, rows, n, gain, cos, sin):
            b = q % 4 if q < 12 else 0
            p = rows.stop
            dve.wait_ge(s["head_std"], q + 1)
            link(nc.vector.reciprocal(hrs[rows, 0:n], hstd[rows, b * 8:b * 8 + n]))
            zv = z[rows, 0:n * HD].rearrange("p (h d) -> p h d", d=HD)
            link(nc.vector.tensor_tensor(zv, zv, hrs[rows, 0:n].unsqueeze(2).to_broadcast([p, n, HD]), ALU.mult))
            link(nc.vector.tensor_tensor(z[rows, 0:n * HD], z[rows, 0:n * HD], gain, ALU.mult))
            return rope(z[rows, 0:n * HD], rows, n, HD, 8, cos, sin)

        every = slice(0, P)
        for u in range(32):
            split_lo(dve, r, u + AHEAD)
            if u in (1, 2, 3, 4):
                q = u - 1
                if q == 0:
                    dve.wait_ge(s["mixer_in"], 32)
                    for t in xc_hi + xc_lo:
                        z = nc.vector.memset(t[:, S:S + STRIDE].bitcast(F32), 0.0)
                    z.then_inc(s["pad"], 1)
                if q >= 2:
                    dve.wait_ge(s["x_lo"], q - 1)
                dve.wait_ge(unit_used, SLOTS * r + 2 + 1)
                link(nc.vector.tensor_tensor(val[q % 2][:], bank[q // 2][:], rs_full[:], ALU.mult))
                nc.vector.tensor_tensor(val[q % 2][:].rearrange("p (c l) -> p c l", l=STRIDE),
                                        val[q % 2][:].rearrange("p (c l) -> p c l", l=STRIDE),
                                        pe_t(q).unsqueeze(1).to_broadcast([P, S // STRIDE, STRIDE]), ALU.add).then_inc(s["x_val"], 1)
                dve.wait_ge(s["x_hi"], q + 1)
                nc.vector.tensor_tensor(xc_lo[q][:, 0:S], val[q % 2][:], xc_hi[q][:, 0:S].bitcast(F32),
                                        ALU.subtract).then_inc(s["x_lo"], 1)
            if 2 <= u < 6:
                dve.wait_ge(unit_used, SLOTS * r + u + 1 + 1)
                nc.vector.scalar_tensor_tensor(out=sb_t[:, (u - 2) * S:(u - 1) * S], in0=bank[u][:], scalar=QS if u < 4 else 1.0,
                                               in1=rs_full[:], op0=ALU.mult, op1=ALU.mult).then_inc(s["sb_out"], 1)
            for c in range(3):
                for pair, at in enumerate((14, 15)):
                    if u != at + 4 * c:
                        continue
                    n = norm_heads[c]
                    blocks = (2 * pair, 2 * pair + 1)
                    for b in blocks:
                        squares(4 * c + b, zn[b], every, n)
                    for b in blocks:
                        last = normalise(4 * c + b, zn[b], every, n, gn[:, c * 512:c * 512 + n * HD],
                                         cos16[:, b * 16:(b + 1) * 16], sin16[:, b * 16:(b + 1) * 16])
                        if c == 2:
                            link(last)
                            last = rope(zn[b][:, 128:512], every, 12, IDX_D, 4, cos8[:, b * 8:(b + 1) * 8], sin8[:, b * 8:(b + 1) * 8])
                        last.then_inc(s["roped"], 1)
        nc.vector.memset(vc_blk[:], 0.0).then_inc(s["vcb_zero"], 1)
        dve.wait_ge(s["gates"], 1)
        sm = small[:].rearrange("p (b c) -> p b c", b=TB)
        nc.vector.tensor_scalar(sm[:, :, GATE + 24:GATE + 32], sm[:, :, GATE + 24:GATE + 32], float(np.float32(8 ** -0.5)), float(np.float32(32 ** -0.5)), ALU.mult, ALU.mult)
        rows = slice(0, NC)
        squares(12, kcn, rows, 2)
        normalise(12, kcn, rows, 2, gn[0:NC, 1152:1280], cos_c[0:NC, :], sin_c[0:NC, :]).then_inc(s["roped"], 1)

    def scores_q(tile_i, half, b):
        return heads_t[half, tile_i * S + b * P:tile_i * S + (b + 1) * P]

    JOBS, BATCHES = 20, 5
    ORDER = (0, 2, 1, 3)
    O_BANK = (4, 5, 4, 5, 7)

    def job(b, j):
        n, bt = (b + 1) * P, j // 4
        if bt < 4:
            c = ORDER[j % 4]
            half, t = slice(64 * (c // 2), 64 * (c // 2) + 64), 2 * (bt % 2) + c % 2
            key = (4 + bt // 2) * S
        else:
            c = j % 4
            half, t = slice(64 * (c % 2), 64 * (c % 2) + 64), 6 + c // 2
            key = 8 * S
        return bt, c, scores_q(t, half, b), heads_t[half, key:key + n]

    def batch_values(bt, kb):
        if bt < 4:
            v0 = kb * 512 + SB_H * HD + (bt // 2) * P
            return v_nat[:, v0:v0 + P]
        return small[:, kb * SMALL:kb * SMALL + P]

    def place(b, bt, c=0):
        return JOBS * b + 4 * bt + c

    def score_bank(n):
        return bank[(0, 1, 6)[n % 3]]

    def steps_of(b):
        def half(bt, first):
            seq, lead = [], 2
            for kb in range(b + 1 + lead):
                if kb <= b:
                    seq.append(("turn", bt, kb))
                if kb >= lead:
                    seq.append(("values", bt, kb - lead))
            if bt < 2:
                seq.append(("cmp", bt, 0))
            cut = (len(seq) + 1) // 2
            return seq[:cut] if first else seq[cut:]
        out = []
        for bt in range(BATCHES + 1):
            if bt < BATCHES:
                out.append(("scores", bt, 0))
            if bt >= 2:
                out += half(bt - 2, False)
            if bt < BATCHES:
                out.append(("scores", bt, 2))
            if bt >= 1:
                out += half(bt - 1, True)
        return out + half(BATCHES - 1, False)

    IDX_BANK = (2, 4, 5, 7)
    SB_OFF = {0: 0, 1: 512, 3: 896, 2: 1024}

    def sb_bank(j):
        return {0: bank[0][:, 0:512], 1: bank[1][:, 0:384], 3: bank[1][:, 384:512], 2: bank[6][:, 0:256]}[j]

    def mix2_pe(pe, f):
        fence(pe, f)
        def stick_logits(h):
            half = slice(64 * (h % 2), 64 * (h % 2) + 64)
            if h > 0:
                pe.wait_ge(s["job_red"], JOBS * h)
            for j in (0, 1, 3, 2):
                mm = nc.tensor.matmul(sb_bank(j), sb_t[half, (2 + h // 2) * S + j * P:(2 + h // 2) * S + (j + 1) * P],
                                      sb_t[half, (h // 2) * S + j * P:(h // 2) * S + S], start=True, stop=True)
            mm.then_inc(s["sb_z"], 1)

        def stick_sums(h):
            pe.wait_ge(s["sb_sp"], h + 1)
            for j in (0, 1, 3, 2):
                n = S - j * P
                nc.tensor.matmul(sb_bank(j), tri, sb_a[:, SB_OFF[j]:SB_OFF[j] + n], start=True, stop=(j == 3))
                for jj in range(j + 1, 4):
                    mm = nc.tensor.matmul(sb_bank(j)[:, (jj - j) * P:n], ones, sb_a[:, SB_OFF[jj]:SB_OFF[jj] + S - jj * P],
                                          start=False, stop=(jj == 3))
            mm.then_inc(s["sb_c"], 1)

        def stick_out(h):
            pe.wait_ge(s["sb_w"], h + 1)
            for j in range(TB):
                n = S - j * P
                mm = nc.tensor.matmul(bank[3][:, j * P:S], v_nat[:, j * 512 + (h // 2) * P:j * 512 + (h // 2 + 1) * P],
                                      sb_z[:, SB_OFF[j]:SB_OFF[j] + n], start=(j == 0), stop=(j == 3))
            mm.then_inc(s["sb_o"], 1)

        def index(b, heads):
            n = (b + 1) * P
            if 0 in heads:
                pe.wait_ge(s["o_out"], 3 * b)
                pe.wait_ge(s["pt_out"], turns_before(b, 0))
            for h in heads:
                if h >= 4:
                    pe.wait_ge(s["idx_relu"], 8 * (b - 1) + h - 3)
                rows = slice(32 * (h % 4), 32 * (h % 4) + 32)
                nc.tensor.matmul(bank[IDX_BANK[h % 4]][:, 0:n], heads_t[rows, (9 + h // 4) * S + b * P:(9 + h // 4) * S + (b + 1) * P],
                                 heads_t[rows, 11 * S:11 * S + n], start=True, stop=True).then_inc(s["idx_mm"], 1)

        def compressed(b):
            if b > 0:
                pe.wait_ge(s["idx_relu"], 8 * b)
            for h in range(8):
                half = slice(64 * (h // 4), 64 * (h // 4) + 64)
                mm = nc.tensor.matmul(bank[(2, 7)[h // 4]][:, h % 4 * NC:(h % 4 + 1) * NC], scores_q(h % 4, half, b), kc_t[half, :], start=True, stop=True)
            mm.then_inc(s["cmp_sc"], 1)

        def compressed_turn(b):
            pe.wait_ge(s["cmp_scaled"], b + 1)
            for g in range(G):
                mm = nc.tensor.transpose(bank[7][:, g * P:(g + 1) * P], cmp_p[:, g * P:(g + 1) * P], ident)
            mm.then_inc(s["cmp_tr"], 1)

        def compressed_values(b, bt):
            pe.wait_ge(s["cmp_pt"], b + 1)
            probs = cmp_t[:].rearrange("p (g q) -> p g q", g=G)
            for i in range(2):
                h = 2 * bt + i
                dst = bank[O_BANK[bt]][:].rearrange("p (g i q) -> p g i q", g=G, i=2)[:, :, i, :]
                mm = nc.tensor.matmul(dst, vc_blk[:, h * P:(h + 1) * P], probs, start=False, stop=False)
            mm.then_inc(s["cmp_o"], 1)

        def scores(b, bt, first):
            n = JOBS * b + 4 * bt + first
            if bt == 0 and first == 0:
                pe.wait_ge(s["sb_out"], b + 1)
                pe.wait_ge(s["sb_d"], b + 1)
            if n >= 2:
                pe.wait_ge(s["job_red"], n - 1)
            for i in range(2):
                _, _, q, k = job(b, 4 * bt + first + i)
                nc.tensor.matmul(score_bank(n + i)[:, 0:(b + 1) * P], q, k, start=True, stop=True).then_inc(s["job_sc"], 1)

        turns = [0]

        def turn(b, bt, kb):
            pe.wait_ge(s["scaled_a"], BATCHES * b + bt + 1)
            pe.wait_ge(s["scaled_p"], BATCHES * b + bt + 1)
            if turns[0] >= 2:
                pe.wait_ge(s["pt_out"], turns[0] - 1)
            for c in range(4):
                mm = nc.tensor.transpose(bank[2 + turns[0] % 2][:, c * P:(c + 1) * P], prob[bt % 2][:, c * S + kb * P:c * S + (kb + 1) * P], ident)
            mm.then_inc(s["job_tr"], 1)
            turns[0] += 1

        products = [0]

        def values(b, bt, kb):
            pe.wait_ge(s["pt_out"], products[0] + 1)
            if kb == 0 and b > 0 and bt in (0, 1, 4):
                pe.wait_ge(s["o_out"], 3 * b)
            nc.tensor.matmul(bank[O_BANK[bt]][:], batch_values(bt, kb), prob_t[products[0] % 2][:],
                             start=(kb == 0 and bt in (0, 1, 4)), stop=(kb == b and bt >= 2)).then_inc(s["job_pv"], 1)
            products[0] += 1

        stick_logits(0)
        for b in range(TB):
            if b > 0:
                index(b, range(4))
            stick_sums(b)
            if b > 0:
                index(b, range(4, 8))
            stick_out(b)
            compressed(b)
            turned = False
            for kind, bt, at in steps_of(b):
                if kind == "scores":
                    scores(b, bt, at)
                    if (bt, at) == (BATCHES - 1, 2) and b + 1 < TB:
                        stick_logits(b + 1)
                elif kind == "turn":
                    if not turned:
                        compressed_turn(b)
                        turned = True
                    turn(b, bt, at)
                elif kind == "values":
                    values(b, bt, at)
                else:
                    compressed_values(b, bt)

    def mix2_act(act, f):
        fence(act, f)
        turns = [0]

        def stick_softplus(h):
            act.wait_ge(s["sb_zm"], h + 1)
            nc.scalar.activation(sb_a[:], sb_z[:], ACT.Abs).then_inc(s["sb_abs"], 1)
            act.wait_ge(s["sb_abs"], h + 1)
            nc.scalar.activation(sb_a[:], sb_a[:], ACT.Exp, scale=-1.0).then_inc(s["sb_e"], 1)
            act.wait_ge(s["sb_e"], h + 1)
            nc.scalar.activation(sb_a[:], sb_a[:], ACT.Ln, bias=one_col).then_inc(s["sb_ln"], 1)

        def index_relu(b, heads):
            for h in heads:
                q = 8 * (b - 1) + h
                act.wait_ge(s["idx_mm"], q + 1)
                if q >= 2:
                    act.wait_ge(s["idx_acc"], q - 1)
                nc.scalar.activation(relu[q % 2][:, 0:(b + 1) * P], bank[IDX_BANK[h % 4]][:, 0:(b + 1) * P], ACT.Relu).then_inc(s["idx_relu"], 1)

        def scale_probs(b, bt):
            act.wait_ge(s["coef"], BATCHES * b + bt + 1)
            for c in range(3):
                head = prob[bt % 2][:, c * S:c * S + (b + 1) * P]
                a = nc.scalar.activation(head, head, ACT.Copy, scale=coef[:, place(b, bt, c):place(b, bt, c) + 1])
            a.then_inc(s["scaled_a"], 1)

        stick_softplus(0)
        for b in range(TB):
            if b > 0:
                index_relu(b, range(4))
            act.wait_ge(s["sb_d"], b + 1)
            nc.scalar.activation(sb_z[:], sb_z[:], ACT.Exp).then_inc(s["sb_w"], 1)
            if b > 0:
                index_relu(b, range(4, 8))
            act.wait_ge(s["sb_o"], b + 1)
            rows = slice(64 * (b % 2), 64 * (b % 2) + 64)
            nc.scalar.activation(o_t[rows, (b // 2) * S:(b // 2 + 1) * S], bank[3][rows, :], ACT.Copy).then_inc(s["sb_out"], 1)
            act.wait_ge(s["cmp_sub"], b + 1)
            nc.scalar.activation(cmp_p[:], cmp_s[:], ACT.Exp).then_inc(s["cmp_exp"], 1)
            first = True
            w = (b + 1) * P
            for kind, bt, at in steps_of(b):
                if kind == "scores":
                    if at == 2 and bt > 0:
                        scale_probs(b, bt - 1)
                    for i in range(2):
                        j = 4 * bt + at + i
                        n = JOBS * b + j
                        _, c, _, _ = job(b, j)
                        m = place(b, bt, c)
                        act.wait_ge(s["job_red"], n + 1)
                        if bt >= 2 and at == 0 and i == 0:
                            act.wait_ge(s["job_tr"], turns_before(b, bt - 1))
                        elif b > 0 and bt < 2 and at == 0 and i == 0:
                            act.wait_ge(s["job_tr"], turns_before(b, 0))
                        nc.scalar.activation(prob[bt % 2][:, c * S:c * S + w], neg_s[n % 2][:, 0:w], ACT.Exp, scale=-1.0,
                                             bias=neg_m[:, m:m + 1], accum_out=den[:, m:m + 1]).then_inc(s["job_exp"], 1)
                elif kind == "turn":
                    if bt == BATCHES - 1 and at == 0:
                        scale_probs(b, bt)
                    if first:
                        first = False
                        act.wait_ge(s["cmp_tr"], b + 1)
                        if b > 0:
                            act.wait_ge(s["cmp_o"], 2 * b)
                        nc.scalar.activation(cmp_t[:], bank[7][:, 0:256], ACT.Copy).then_inc(s["cmp_pt"], 1)
                    t = turns[0]
                    act.wait_ge(s["job_tr"], t + 1)
                    if t >= 2:
                        act.wait_ge(s["job_pv"], t - 1)
                    nc.scalar.activation(prob_t[t % 2][:], bank[2 + t % 2][:], ACT.Copy).then_inc(s["pt_out"], 1)
                    turns[0] += 1
            if b + 1 < TB:
                stick_softplus(b + 1)
            act.wait_ge(s["job_pv"], turns[0])
            for i, (bk, tile0) in enumerate(((4, 2), (5, 4), (7, 6))):
                for g in range(2):
                    rows = slice(64 * g, 64 * g + 64)
                    dst = o_t[rows, tile0 * S:(tile0 + 2) * S].rearrange("p (i t) -> p i t", i=2)[:, :, b * P:(b + 1) * P]
                    src = bank[bk][rows, 2 * g * P:2 * (g + 1) * P].rearrange("p (i t) -> p i t", i=2)
                    a = nc.scalar.activation(dst, src, ACT.Copy)
                a.then_inc(s["o_out"], 1)

    def turns_before(b, bt):
        return BATCHES * b * (b + 1) // 2 + bt * (b + 1)

    def mix2_pool(pool, f):
        fence(pool, f)
        for b in range(TB):
            for bt in range(BATCHES):
                pool.wait_ge(s["coef"], BATCHES * b + bt + 1)
                tile3 = prob[bt % 2][:, 3 * S:3 * S + (b + 1) * P]
                nc.gpsimd.tensor_scalar(tile3, tile3, coef[:, place(b, bt, 3):place(b, bt, 4)], None, ALU.mult).then_inc(s["scaled_p"], 1)

    def mix2_dve(dve, f):
        fence(dve, f)
        steps = [0]

        def link(ins):
            steps[0] += 1
            ins.then_inc(s["dve_step"], 1)
            dve.wait_ge(s["dve_step"], steps[0])

        sm = small[:].rearrange("p (b c) -> p b c", b=TB)
        def stick_masked(h):
            dve.wait_ge(s["sb_z"], h + 1)
            nc.vector.tensor_copy(sb_z[:, 0:512], bank[0][:])
            nc.vector.tensor_copy(sb_z[:, 512:1024], bank[1][:])
            link(nc.vector.tensor_copy(sb_z[:, 1024:1280], bank[6][:, 0:256]))
            for j in range(4):
                d = sb_z[:, SB_OFF[j]:SB_OFF[j] + P]
                last = nc.vector.tensor_tensor(d, d, mask_strict, ALU.add)
            last.then_inc(s["sb_zm"], 1)

        def index_sum(b, heads):
            for h in heads:
                q, n = 8 * (b - 1) + h, (b + 1) * P
                dve.wait_ge(s["idx_relu"], q + 1)
                if h > 0:
                    dve.wait_ge(s["idx_acc"], q)
                prev = index_s[:, 0:n] if h else mask_c[:, 512 - n:512]
                nc.vector.scalar_tensor_tensor(out=index_s[:, 0:n], in0=relu[q % 2][:, 0:n], scalar=sm[:, b, GATE + 24 + h:GATE + 25 + h],
                                               in1=prev, op0=ALU.mult, op1=ALU.add).then_inc(s["idx_acc"], 1)

        stick_masked(0)
        for b in range(TB):
            n = (b + 1) * P
            dve.wait_ge(s["sb_ln"], b + 1)
            nc.vector.scalar_tensor_tensor(out=sb_a[:], in0=sb_z[:], scalar=0.0, in1=sb_a[:], op0=ALU.max,
                                           op1=ALU.add).then_inc(s["sb_sp"], 1)
            if b > 0:
                index_sum(b, range(4))
            dve.wait_ge(s["sb_c"], b + 1)
            nc.vector.tensor_tensor(sb_z[:, 0:512], sb_z[:, 0:512], bank[0][:], ALU.subtract)
            nc.vector.tensor_tensor(sb_z[:, 512:1024], sb_z[:, 512:1024], bank[1][:], ALU.subtract)
            nc.vector.tensor_tensor(sb_z[:, 1024:1280], sb_z[:, 1024:1280], bank[6][:, 0:256], ALU.subtract).then_inc(s["sb_d"], 1)
            if b > 0:
                index_sum(b, range(4, 8))
                dve.wait_ge(s["idx_acc"], 8 * b)
            dve.wait_ge(s["cmp_sc"], b + 1)
            cs = cmp_s[:].rearrange("p (h c) -> p h c", h=8)
            for g in range(G):
                last = nc.vector.tensor_tensor(cs[:, 4 * g:4 * g + 4, :], bank[(2, 7)[g]][:, 0:P].rearrange("p (h c) -> p h c", h=4),
                                               mask_cmp[:, b * NC:(b + 1) * NC].unsqueeze(1).to_broadcast([P, 4, NC]), ALU.add)
            link(last)
            link(nc.vector.tensor_reduce(cmp_m[:, 0:8], cs, AX.X, ALU.max))
            link(nc.vector.tensor_scalar(cmp_m[:, 0:8], cmp_m[:, 0:8], -1e20, None, ALU.max))
            nc.vector.tensor_tensor(cs, cs, cmp_m[:, 0:8].unsqueeze(2).to_broadcast([P, 8, NC]), ALU.subtract).then_inc(s["cmp_sub"], 1)
            dve.wait_ge(s["cmp_exp"], b + 1)
            link(nc.vector.tensor_reduce(cmp_m[:, 8:16], cmp_p[:].rearrange("p (h c) -> p h c", h=8), AX.X, ALU.add))
            link(nc.vector.tensor_scalar(cmp_m[:, 8:16], cmp_m[:, 8:16], 0.5, None, ALU.max))
            link(nc.vector.reciprocal(cmp_m[:, 8:16], cmp_m[:, 8:16]))
            gate = sm[:, b, GATE:GATE + 24].rearrange("p (h k) -> p k h", k=3)
            link(nc.vector.tensor_tensor(cmp_m[:, 8:16], cmp_m[:, 8:16], gate[:, 0, :], ALU.mult))
            cp = cmp_p[:].rearrange("p (h c) -> p h c", h=8)
            nc.vector.tensor_tensor(cp, cp, cmp_m[:, 8:16].unsqueeze(2).to_broadcast([P, 8, NC]), ALU.mult).then_inc(s["cmp_scaled"], 1)

            def weights(bt):
                m = place(b, bt)
                dve.wait_ge(s["job_exp"], m + 4)
                ins = nc.vector.reciprocal(coef[:, m:m + 4], den[:, m:m + 4])
                if bt < 4:
                    link(ins)
                    gates = gate[:, 1 + bt // 2, :].rearrange("p (g h) -> p g h", g=G)[:, :, 2 * (bt % 2):2 * (bt % 2) + 2]
                    both4 = coef[:, m:m + 4].rearrange("p (g h) -> p g h", g=G)
                    ins = nc.vector.tensor_tensor(both4, both4, gates, ALU.mult)
                ins.then_inc(s["coef"], 1)

            for j in range(JOBS):
                q = JOBS * b + j
                bt, c, _, _ = job(b, j)
                m = place(b, bt, c)
                mask = mask_c[:, 512 - n:512] if j < 16 or b == 0 else mask_k[:, 0:n]
                dve.wait_ge(s["job_sc"], q + 1)
                if q >= 2:
                    dve.wait_ge(s["job_exp"], q - 1)
                nc.vector.tensor_tensor_reduce(out=neg_s[q % 2][:, 0:n], in0=score_bank(q)[:, 0:n], in1=mask, scale=-1.0,
                                               scalar=3e38, op0=ALU.add, op1=ALU.min,
                                               accum_out=neg_m[:, m:m + 1]).then_inc(s["job_red"], 1)
                if bt > 0 and j % 4 == 0:
                    weights(bt - 1)
                if b > 0 and j < 16:
                    src = index_s if j == 0 else picked
                    link(nc.vector.max(top8[:, 0:8], src[:, 0:n]))
                    link(nc.vector.match_replace(picked[:, 0:n], top8[:, 0:8], src[:, 0:n], -3e38))
                    if j == 15:
                        link(nc.vector.tensor_scalar(mask_k[:, 0:n], picked[:, 0:n], -2e38, NEG, ALU.is_gt, ALU.mult))
            weights(BATCHES - 1)
            if b + 1 < TB:
                stick_masked(b + 1)

    def mix3_pe(pe, f, r):
        fence(pe, f)
        pe.wait_ge(s["o_lo"], KD)
        with pe.Fori(0, KD) as m:
            for g in range(3):
                pe.wait_ge(s["gate_free"], 3 * m + g + 1)
                unit_product(pe, r + m, g, bank[g][:], h_hi, h_lo)
            pe.wait_ge(s["branches"], m + 1)
            pe.wait_ge(unit_lo, SLOTS * (r + m) + 3 + 1)
            for k in range(KD):
                br = 0 if k < 2 else 1 if k < 6 else 2
                w = slice(k * P, (k + 1) * P)
                mm = three(bank[3 + br][:], w_hi[3][:, w], w_lo[3][:, w], tile(o_hi, k), tile(o_lo, k), k in (0, 2, 6), k in (1, 5, 7))
            mm.then_inc(unit_used, 1)
        pe.wait_ge(s["m_lo"], KD)
        rd = r + KD
        with pe.Fori(0, 2) as i:
            for t in range(4):
                pe.wait_ge(s["x_new"], 4 * i + t + 1)
                unit_product(pe, rd + i, t, bank[6 + t % 2][:], m_hi, m_lo)

    def mix3_act(act, f, r, gn_col):
        fence(act, f)
        for t in range(KD):
            nc.scalar.activation(tile(o_hi, t), tile(o_t, t), ACT.Copy).then_inc(s["o_hi"], 1)
        with act.Fori(0, KD) as m:
            for g in range(3):
                split_hi(act, r + m, g + AHEAD)
                act.wait_ge(s["gate"], 3 * m + g + 1)
                nc.scalar.activation(sig[g][:], sig[g][:], ACT.Sigmoid).then_inc(s["sig"], 1)
            split_hi(act, r + m, 3 + AHEAD)
            act.wait_ge(s["m_val"], m + 1)
            nc.scalar.activation(m_hi[:, bass.ds(m * S, S)], val[0][:], ACT.Copy).then_inc(s["m_hi"], 1)
        rd = r + KD
        with act.Fori(0, 2) as i:
            for t in range(4):
                split_hi(act, rd + i, t + AHEAD)
                act.wait_ge(s["x_new"], 4 * i + t + 3)
                act.wait_ge(s["ssq_add"], 4 * i + t + 1)
                a = bass.ds(4 * i * S + t * S, S)
                nc.scalar.activation(sq[t % 2][:], x[:, a], ACT.Square).then_inc(s["sq"], 1)
                scaled_hi(act, x[:, a], h_hi[:, a], gains[:, bass.ds(gn_col + 4 * i + t, 1)])

    def mix3_dve(dve, f, r, gn_col):
        fence(dve, f)
        dve.sem_inc(s["x_new"], 2)
        dve.sem_inc(s["gate_free"], 3)
        dve.sem_inc(s["branches"], 1)
        for t in range(KD):
            dve.wait_ge(s["o_hi"], t + 1)
            nc.vector.tensor_tensor(tile(o_lo, t), tile(o_t, t), tile(o_hi, t).bitcast(F32), ALU.subtract).then_inc(s["o_lo"], 1)
        with dve.Fori(0, KD) as m:
            for g in range(4):
                split_lo(dve, r + m, g + AHEAD)
                if g < 3:
                    dve.wait_ge(unit_used, SLOTS * (r + m) + g + 1 + 1)
                    dve.wait_ge(s["branches"], m + 1)
                    ins = nc.vector.tensor_tensor(sig[g][:], bank[g][:], rs_full[:], ALU.mult)
                    ins.then_inc(s["gate"], 1)
                    dve.wait_ge(s["gate"], 3 * m + g + 1)
                    dve.sem_inc(s["gate_free"], 1)
            dve.wait_ge(unit_used, SLOTS * (r + m) + 4 + 1)
            dve.wait_ge(s["sig"], 3 * m + 3)
            nc.vector.tensor_tensor(part[0][:], sig[0][:], bank[3][:], ALU.mult)
            nc.vector.tensor_tensor(part[1][:], sig[1][:], bank[4][:], ALU.mult)
            nc.vector.tensor_tensor(part[2][:], sig[2][:], bank[5][:], ALU.mult).then_inc(s["branches"], 1)
            dve.wait_ge(s["branches"], m + 2)
            nc.vector.tensor_tensor(part[0][:], part[0][:], part[1][:], ALU.add).then_inc(s["part_sum"], 1)
            dve.wait_ge(s["part_sum"], m + 1)
            nc.vector.tensor_tensor(val[0][:], part[0][:], part[2][:], ALU.add).then_inc(s["m_val"], 1)
            dve.wait_ge(s["m_hi"], m + 1)
            a = bass.ds(m * S, S)
            nc.vector.tensor_tensor(m_lo[:, a], val[0][:], m_hi[:, a].bitcast(F32), ALU.subtract).then_inc(s["m_lo"], 1)
        rd = r + KD
        with dve.Fori(0, 2) as i:
            for t in range(4):
                split_lo(dve, rd + i, t + AHEAD)
                dve.wait_ge(unit_used, SLOTS * (rd + i) + t + 1 + 1)
                a = bass.ds(4 * i * S + t * S, S)
                nc.vector.tensor_tensor(x[:, a], x[:, a], bank[6 + t % 2][:], ALU.add).then_inc(s["x_new"], 1)
                scaled_lo(dve, x[:, a], h_hi[:, a], h_lo[:, a], gains[:, bass.ds(gn_col + 4 * i + t, 1)], 4 * i + t + 1)

    def mix3_pool(pool, f):
        fence(pool, f)
        nc.gpsimd.memset(ssq[:], 0.0).then_inc(s["ssq_add"], 2)
        sum_squares(pool)

    def bias_rows_pe(pe):
        pe.wait_ge(s["bias_tab_in"], 32)
        for i in range(NG * NH2):
            if i >= 2:
                pe.wait_ge(s["bias_out_a"], i - 1)
                pe.wait_ge(s["bias_out_v"], i - 1)
            lhs = tab_rep[0:33, i * P:(i + 1) * P]
            hot = one_hot[0:33, (i // NH2) * BW:(i // NH2 + 1) * BW]
            nc.tensor.matmul(bank[2 * (i % 2)][:], lhs, hot[:, 0:512], start=True, stop=True)
            nc.tensor.matmul(bank[2 * (i % 2) + 1][:, 0:P], lhs, hot[:, 512:BW], start=True, stop=True).then_inc(s["bias_mm"], 1)

    def bias_loads_act(act):
        act.dma_start(tab_rep[0:33, :], A["bias_table"]).then_inc(s["bias_tab_in"], 16)
        act.dma_start(one_hot[0:33, :], A["bias_one_hot"]).then_inc(s["bias_tab_in"], 16)

    def bias_rows_act(act, first, end):
        for i in range(first, end):
            act.wait_ge(s["bias_mm"], i + 1)
            if i >= 2:
                act.wait_ge(bias_stored[i % 2], 16 * (i // 2))
            nc.scalar.activation(bias_row[i % 2][:, 0:512], bank[2 * (i % 2)][:], ACT.Copy).then_inc(s["bias_out_a"], 1)

    def bias_rows_dve(dve):
        for i in range(NG * NH2):
            dve.wait_ge(s["bias_mm"], i + 1)
            if i >= 2:
                dve.wait_ge(bias_stored[i % 2], 16 * (i // 2))
            nc.vector.tensor_copy(bias_row[i % 2][:, 512:BW], bank[2 * (i % 2) + 1][:, 0:P]).then_inc(s["bias_out_v"], 1)

    def bias_rows_pool(pool, first, end):
        for i in range(first, end):
            pool.wait_ge(s["bias_out_a"], i + 1)
            pool.wait_ge(s["bias_out_v"], i + 1)
            pool.dma_start(bias_dram[i].rearrange("(a w) -> a w", w=BW), bias_row[i % 2][:]).then_inc(bias_stored[i % 2], 16)

    PAIRS = NH2 // 2
    VB = ([0, 1, 2, 3], [4, 5, 6, 7], [0, 1, 2, 3])

    def spans(b):
        n0, n = min(b + 1, 2) * P, (b + 1) * P
        return ((0, n0), (n0, n), (n0 + n, n)), n0 + 2 * n

    def job2(n):
        return n // 8, n // 4, n % 4

    def qk_tile(p, h, i):
        return slice(64 * (h % 2), 64 * (h % 2) + 64), qk[p % 2], i * S

    def blk1_pe(pe, f, r):
        fence(pe, f)
        norm_pe(pe)
        pe.wait_ge(s["h_lo"], KD)
        for u in range(12):
            g, j = divmod(u, 4)
            if u == 8:
                pe.wait_ge(s["v_out"], TB)
            natural_unit(pe, r, u, VB[g], 2 * j, 2, 512, j == 0, j == 3)
        for u in range(12, 28):
            c, j = divmod(u - 12, 2)
            if j == 0:
                if c < 2:
                    pe.wait_ge(s["v_out"], 2 * TB)
                else:
                    pe.wait_ge(s["glu"], c - 1)
            unit_product(pe, r, u, bank[4 + 2 * (c % 2) + j][:], h_hi, h_lo)

        def sc(n):
            p, h, b = job2(n)
            if n == 0:
                pe.wait_ge(s["v_out"], 3 * TB)
                pe.wait_ge(s["glu"], KD)
            else:
                pe.wait_ge(s["job_red"], n)
            pe.wait_ge(s["qk_out"], 6 * (p + 1))
            for g, (_, w) in enumerate(spans(b)[0]):
                half, t, q0 = qk_tile(p, h, 2 * g)
                _, _, k0 = qk_tile(p, h, 2 * g + 1)
                first_key = (b + 1) * P - w
                mm = nc.tensor.matmul(bank[2 + g][:, 0:w], t[half, q0 + b * P:q0 + (b + 1) * P],
                                      t[half, k0 + first_key:k0 + first_key + w], start=True, stop=True)
            mm.then_inc(s["job_sc"], 1)

        def tr(n):
            b = n % 4
            pe.wait_ge(s["job_exp"], n + 1)
            if n >= 1:
                pe.wait_ge(s["pt_out"], n)
            else:
                pe.wait_ge(s["glu"], KD)
            for g in (1, 2, 0):
                at, w = spans(b)[0][g]
                if g == 0 and n >= 1:
                    pe.wait_ge(s["o_out"], n)
                for kb in range(w // P):
                    mm = nc.tensor.transpose(bank[5 + g][:, kb * P:(kb + 1) * P], prob2[:, at + kb * P:at + (kb + 1) * P], ident)
            mm.then_inc(s["job_tr"], 1)

        def pv(n):
            p, h, b = job2(n)
            pe.wait_ge(s["pt_out"], n + 1)
            if n >= 1:
                pe.wait_ge(s["o_out"], n)
            parts = [(at + kb * P, g, b + 1 - w // P + kb) for g, (at, w) in enumerate(spans(b)[0]) for kb in range(w // P)]
            for i, (col, g, kb) in enumerate(parts):
                v0 = kb * 3 * 512 + g * 512 + h * HD
                mm = nc.tensor.matmul(o_bank, prob_t2[:, col:col + P], v2[:, v0:v0 + HD],
                                      start=(i == 0), stop=(i == len(parts) - 1))
            mm.then_inc(s["job_pv"], 1)

        def slot(p, t):
            if 0 <= t - 2 < 8:
                pv(8 * p + t - 2)
            if t < 8:
                sc(8 * p + t)
            if 0 <= t - 1 < 8:
                tr(8 * p + t - 1)

        for p in range(PAIRS):
            for i in range(6):
                u = 28 + 6 * p + i
                pe.wait_ge(s["v_out"], 3 * TB)
                if 6 * p + i >= 2:
                    pe.wait_ge(s["qk_out"], 6 * p + i - 1)
                pe.wait_ge(unit_lo, SLOTS * r + u + 1)
                for k in range(KD):
                    w = slice(k * P, (k + 1) * P)
                    mm = three(bank[i % 2][:], w_hi[u % SLOTS][:, w], w_lo[u % SLOTS][:, w], tile(h_hi, k), tile(h_lo, k),
                               k == 0, k == KD - 1)
                    if k == 3 and p > 0:
                        slot(p - 1, 2 * i)
                mm.then_inc(unit_used, 1)
                if p > 0:
                    slot(p - 1, 2 * i + 1)
        for t in range(10):
            slot(PAIRS - 1, t)

    def blk1_act(act, f, r):
        fence(act, f)
        act.dma_start(b2[:], A["block2_columns"]).then_inc(s["mixer_in"], 16)
        norm_act(act)
        for u in range(12):
            split_hi(act, r, u + AHEAD)
            if u % 4 == 3:
                g = u // 4
                act.wait_ge(unit_used, SLOTS * r + u + 1 + 1)
                for b in range(TB):
                    nc.scalar.activation(v2[:, b * 1536 + g * 512:b * 1536 + (g + 1) * 512], bank[VB[g][b]][:], ACT.Copy).then_inc(s["v_out"], 1)
        act.wait_ge(s["mixer_in"], 16)
        for u in range(12, 28):
            c, j = divmod(u - 12, 2)
            split_hi(act, r, u + AHEAD)
            if j == 1:
                act.wait_ge(unit_used, SLOTS * r + u + 1 + 1)
                if c >= 2:
                    act.wait_ge(s["glu"], c - 1)
                nc.scalar.activation(sq[c % 2][:], bank[5 + 2 * (c % 2)][:], ACT.Sigmoid, bias=bc("b_gate", c)).then_inc(s["sig"], 1)

        def slot(p, t):
            if not 1 <= t <= 8:
                return
            n = 8 * p + t - 1
            b = n % 4
            (c0, c1, c2), width = spans(b)
            act.wait_ge(s["job_red"], n + 1)
            if n >= 1:
                act.wait_ge(s["job_tr"], n)
            nc.scalar.activation(prob2[:, 0:width], neg_s2[:, 0:width], ACT.Exp, scale=-1.0, bias=neg_m2[:, n:n + 1],
                                 accum_out=den2[:, n:n + 1]).then_inc(s["job_exp"], 1)
            act.wait_ge(s["job_tr"], n + 1)
            if n >= 1:
                act.wait_ge(s["job_pv"], n)
            for g, (at, w) in enumerate((c0, c1, c2)):
                a = nc.scalar.activation(prob_t2[:, at:at + w], bank[5 + g][:, 0:w], ACT.Copy)
            a.then_inc(s["pt_out"], 1)

        for p in range(PAIRS):
            for i in range(6):
                u = 28 + 6 * p + i
                split_hi(act, r, u + AHEAD)
                if p > 0:
                    slot(p - 1, 2 * i)
                act.wait_ge(unit_used, SLOTS * r + u + 1 + 1)
                if p >= 2 and i == 0:
                    act.wait_ge(s["job_pv"], 8 * (p - 1))
                nc.scalar.activation(qk[p % 2][:, i * S:(i + 1) * S], bank[i % 2][:], ACT.Copy,
                                     scale=QS if i % 2 == 0 else 1.0).then_inc(s["qk_out"], 1)
                if p > 0:
                    slot(p - 1, 2 * i + 1)
        for t in range(10):
            slot(PAIRS - 1, t)

    def blk1_dve(dve, f, r):
        fence(dve, f)
        norm_dve(dve, 3 * L * KD)
        taps = [(c, k) for c in range(KD) for k in range(CW)]
        at = [0]

        def convolve(count, tiles):
            while count > 0 and at[0] < len(taps) and taps[at[0]][0] < tiles:
                c, k = taps[at[0]]
                u0 = c * CU
                w = bc("w_dw", c * CW + k)
                if at[0] > 0:
                    dve.wait_ge(s["conv"], at[0])
                if k == 0:
                    dve.wait_ge(s["glu"], c + 1)
                    ins = nc.vector.tensor_scalar(val[0][:], u_conv[:, u0:u0 + S], w, bc("b_dw", c), ALU.mult, ALU.add)
                else:
                    dst = val[0][:] if k < CW - 1 else u_conv[:, u0 + CW - 1:u0 + CU]
                    ins = nc.vector.scalar_tensor_tensor(out=dst, in0=u_conv[:, u0 + k:u0 + k + S], scalar=w, in1=val[0][:],
                                                         op0=ALU.mult, op1=ALU.add)
                ins.then_inc(s["conv"], 1)
                at[0] += 1
                count -= 1

        for u in range(12):
            split_lo(dve, r, u + AHEAD)
        dve.wait_ge(s["mixer_in"], 16)
        nc.vector.memset(u_conv[:], 0.0).then_inc(s["pad"], 1)
        dve.wait_ge(s["pad"], 1)
        for u in range(12, 28):
            c, j = divmod(u - 12, 2)
            split_lo(dve, r, u + AHEAD)
            if j == 1:
                dve.wait_ge(unit_used, SLOTS * r + u + 1 + 1)
                dve.wait_ge(s["sig"], c + 1)
                nc.vector.scalar_tensor_tensor(out=u_conv[:, c * CU + CW - 1:(c + 1) * CU], in0=bank[4 + 2 * (c % 2)][:],
                                               scalar=bc("b_value", c), in1=sq[c % 2][:], op0=ALU.add, op1=ALU.mult).then_inc(s["glu"], 1)
            convolve(5, (u - 11) // 2)

        def slot(p, t):
            if 0 <= t - 2 < 8:
                n = 8 * p + t - 2
                _, h, b = job2(n)
                dve.wait_ge(s["job_pv"], n + 1)
                nc.vector.reciprocal(rden2[:, n:n + 1], den2[:, n:n + 1]).then_inc(s["dve_step"], 1)
                dve.wait_ge(s["dve_step"], n + 1)
                nc.vector.tensor_scalar(o2[:, b * 512 + h * HD:b * 512 + (h + 1) * HD], o_bank, rden2[:, n:n + 1], None,
                                        ALU.mult).then_inc(s["o_out"], 1)
            if t < 8:
                n = 8 * p + t
                _, h, b = job2(n)
                dve.wait_ge(s["job_sc"], n + 1)
                dve.wait_ge(bias_in[h % 2], 16 * 3 * (h // 2 + 1))
                if n >= 1:
                    dve.wait_ge(s["job_exp"], n)
                for g, (c0, w) in enumerate(spans(b)[0]):
                    off = (256, 768, 1280)[g]
                    ins = nc.vector.tensor_tensor_reduce(out=neg_s2[:, c0:c0 + w], in0=bank[2 + g][:, 0:w],
                                                         in1=bias_t[h % 2][:, off - w:off], scale=-1.0, scalar=3e38,
                                                         op0=ALU.add, op1=ALU.min, accum_out=neg_m3[:, g:g + 1])
                ins.then_inc(s["job_parts"], 1)
                dve.wait_ge(s["job_parts"], n + 1)
                nc.vector.tensor_reduce(neg_m2[:, n:n + 1], neg_m3[:, 0:3], AX.X, ALU.min).then_inc(s["job_red"], 1)
                dve.wait_ge(s["job_red"], n + 1)

        for p in range(PAIRS):
            for i in range(6):
                u = 28 + 6 * p + i
                split_lo(dve, r, u + AHEAD)
                for half in range(2):
                    if p > 0:
                        slot(p - 1, 2 * i + half)
                    convolve(3, KD)
        for t in range(10):
            slot(PAIRS - 1, t)
            convolve(3, KD)
        convolve(1000, KD)

    def blk1_pool(pool, f):
        fence(pool, f)
        for h in range(NH2):
            if h >= 2:
                pool.wait_ge(s["job_red"], 4 * (h - 1))
            for g in range(NG):
                src = bias_dram[g * NH2 + h][P - 1:P - 1 + P * (BW - 1)].rearrange("(a w) -> a w", w=BW - 1)
                lo = 256 if g == 0 else 0
                off = (0, 256, 768)[g]
                pool.dma_start(bias_t[h % 2][:, off:off + 512 - lo], src[:, lo:512]).then_inc(bias_in[h % 2], 16)

    def blk2_pe(pe, f, r):
        fence(pe, f)
        for k in range(KD):
            mm = nc.tensor.matmul(bank[5][:], inv_d_sq, u_conv[:, k * CU + CW - 1:(k + 1) * CU], start=(k == 0), stop=(k == KD - 1))
        mm.then_inc(s["mean"], 1)
        for t in range(4):
            if t >= 2:
                pe.wait_ge(s["o_lo"], t - 1)
            for b in range(TB):
                mm = nc.tensor.transpose(bank[t % 2][:, b * P:(b + 1) * P], o2[:, b * 512 + t * P:b * 512 + (t + 1) * P], ident)
            mm.then_inc(s["o_tr"], 1)
        pe.wait_ge(s["o_lo"], 4)
        for u in range(4):
            pe.wait_ge(unit_lo, SLOTS * r + u + 1)
            for i in range(2):
                if 2 * u + i >= 2:
                    pe.wait_ge(s["ya_out"], 2 * u + i - 1)
                for k in range(4):
                    w = slice((4 * i + k) * P, (4 * i + k + 1) * P)
                    mm = three(bank[i][:], w_hi[u][:, w], w_lo[u][:, w], tile(o_hi2, k), tile(o_lo2, k), k == 0, k == 3)
            mm.then_inc(unit_used, 1)
            if u == 2:
                pe.wait_ge(s["ssq_add"], 2 + KD)
                sum_pe(pe)
        spread_pe(pe, 0)
        pe.wait_ge(s["ya_out"], KD)
        with pe.Fori(0, 2) as i:
            for t in range(4):
                pe.wait_ge(s["m_val"], 4 * i + t + 1)
                for j in range(3):
                    hi, lo = (c_hi, c_lo) if j == 2 else (h_hi, h_lo)
                    if j == 2:
                        pe.wait_ge(s["c_lo"], KD)
                    unit_product(pe, r + 1 + 3 * i, 3 * t + j, bank[3 * (t % 2) + j][:], hi, lo)
        pe.wait_ge(s["m_lo"], KD)
        with pe.Fori(0, 2) as i:
            for t in range(4):
                pe.wait_ge(s["x_new"], 4 * i + t + 1)
                unit_product(pe, r + 7 + i, t, bank[6 + t % 2][:], m_hi2, m_lo2)
        pe.wait_ge(s["ssq_add"], 4 + 2 * KD)
        stats_pe(pe, 1)

    def blk2_act(act, f, r):
        fence(act, f)
        for t in range(4):
            act.wait_ge(s["o_tr"], t + 1)
            nc.scalar.activation(tile(o_hi2, t), bank[t % 2][:], ACT.Copy).then_inc(s["o_hi"], 1)

        def square(k):
            act.wait_ge(s["centred"], k + 1)
            act.wait_ge(s["ssq_add"], k + 1)
            nc.scalar.activation(sq[k % 2][:], u_conv[:, k * CU + CW - 1:(k + 1) * CU], ACT.Square).then_inc(s["sq"], 1)

        def attention_out(u):
            act.wait_ge(unit_used, SLOTS * r + u + 1 + 1)
            for i in range(2):
                nc.scalar.activation(tile(ya, 2 * u + i), bank[i][:], ACT.Copy).then_inc(s["ya_out"], 1)

        split_hi(act, r, AHEAD)
        for u, tiles in enumerate(((0, 1, 2), (3, 4, 5), (6, 7))):
            for k in tiles:
                square(k)
            attention_out(u)
            split_hi(act, r, u + 1 + AHEAD)
        stats_act(act, 0, eps_col[:, 1:2])
        for k in range(KD):
            act.wait_ge(s["c_norm"], k + 1)
            nc.scalar.activation(val[k % 2][:], val[k % 2][:], ACT.Silu, bias=bc("b_ln", k)).then_inc(s["c_val"], 1)
            act.wait_ge(s["c_val"], k + 1)
            nc.scalar.activation(tile(c_hi, k), val[k % 2][:], ACT.Copy).then_inc(s["c_hi"], 1)
            if k == 0:
                attention_out(3)
        with act.Fori(0, 2) as i:
            for t in range(4):
                for j in range(3):
                    split_hi(act, r + 1 + 3 * i, 3 * t + j + AHEAD)
                    if j < 2:
                        act.wait_ge(unit_used, SLOTS * (r + 1 + 3 * i) + 3 * t + j + 1 + 1)
                        act.wait_ge(s["branches"], 4 * i + t + 1)
                        nc.scalar.activation(sig2[j][:], bank[3 * (t % 2) + j][:], ACT.Sigmoid).then_inc(s["sig"], 1)
                act.wait_ge(s["m_val"], 4 * i + t + 3)
                nc.scalar.activation(m_hi2[:, bass.ds(4 * i * S + t * S, S)], val[t % 2][:], ACT.Copy).then_inc(s["m_hi"], 1)
        with act.Fori(0, 2) as i:
            for t in range(4):
                split_hi(act, r + 7 + i, t + AHEAD)
                act.wait_ge(s["x_new"], 4 * i + t + 3)
                act.wait_ge(s["ssq_add"], KD + 2 + 4 * i + t + 1)
                nc.scalar.activation(sq[t % 2][:], y_mix[:, bass.ds(4 * i * S + t * S, S)], ACT.Square).then_inc(s["sq"], 1)
        stats_act(act, 1, eps_col[:, 0:1])
        for k in range(KD):
            act.wait_ge(s["x_post"], k + 1)
            act.wait_ge(s["ssq_add"], 2 * KD + 4 + k + 1)
            nc.scalar.activation(sq[k % 2][:], tile(x, k), ACT.Square).then_inc(s["sq"], 1)
            g = (3 * L + 1) * KD + k
            scaled_hi(act, tile(x, k), tile(h_hi, k), gains[:, g:g + 1])

    def blk2_dve(dve, f, r):
        fence(dve, f)
        dve.sem_inc(s["m_val"], 2)
        dve.sem_inc(s["branches"], 1)
        dve.sem_inc(s["x_new"], 2)
        for t in range(4):
            dve.wait_ge(s["o_hi"], t + 1)
            nc.vector.tensor_tensor(tile(o_lo2, t), bank[t % 2][:], tile(o_hi2, t).bitcast(F32), ALU.subtract).then_inc(s["o_lo"], 1)
        dve.wait_ge(s["mean"], 1)
        for k in range(KD):
            uk = u_conv[:, k * CU + CW - 1:(k + 1) * CU]
            nc.vector.tensor_tensor(uk, uk, bank[5][:], ALU.subtract).then_inc(s["centred"], 1)
        for u in range(AHEAD):
            split_lo(dve, r, u + AHEAD)
        stats_dve(dve, 0)
        for k in range(KD + 1):
            if k < KD:
                if k >= 2:
                    dve.wait_ge(s["c_lo"], k - 1)
                nc.vector.scalar_tensor_tensor(out=val[k % 2][:], in0=u_conv[:, k * CU + CW - 1:(k + 1) * CU],
                                               scalar=bc("g_ln", k), in1=bank[6][:], op0=ALU.mult, op1=ALU.mult).then_inc(s["c_norm"], 1)
            if k >= 1:
                dve.wait_ge(s["c_hi"], k)
                nc.vector.tensor_tensor(tile(c_lo, k - 1), val[(k - 1) % 2][:], tile(c_hi, k - 1).bitcast(F32),
                                        ALU.subtract).then_inc(s["c_lo"], 1)
            if k == 0:
                split_lo(dve, r, 2 * AHEAD)
        with dve.Fori(0, 2) as i:
            for t in range(4):
                for j in range(3):
                    split_lo(dve, r + 1 + 3 * i, 3 * t + j + AHEAD)
                dve.wait_ge(unit_used, SLOTS * (r + 1 + 3 * i) + 3 * t + 3 + 1)
                dve.wait_ge(s["sig"], 8 * i + 2 * t + 2)
                a = bass.ds(4 * i * S + t * S, S)
                nc.vector.tensor_tensor(part2_[0][:], sig2[0][:], ya[:, a], ALU.mult)
                nc.vector.scalar_tensor_tensor(out=part2_[1][:], in0=bank[3 * (t % 2) + 2][:], scalar=b2[:, bass.ds(B2["b_conv_out"][0] + 4 * i + t, 1)],
                                               in1=sig2[1][:], op0=ALU.add, op1=ALU.mult).then_inc(s["branches"], 1)
                dve.wait_ge(s["branches"], 4 * i + t + 2)
                nc.vector.tensor_tensor(val[t % 2][:], part2_[0][:], part2_[1][:], ALU.add).then_inc(s["m_val"], 1)
                dve.wait_ge(s["m_hi"], 4 * i + t + 1)
                nc.vector.tensor_tensor(m_lo2[:, a], val[t % 2][:], m_hi2[:, a].bitcast(F32), ALU.subtract).then_inc(s["m_lo"], 1)
        with dve.Fori(0, 2) as i:
            for t in range(4):
                split_lo(dve, r + 7 + i, t + AHEAD)
                dve.wait_ge(unit_used, SLOTS * (r + 7 + i) + t + 1 + 1)
                nc.vector.tensor_copy(y_mix[:, bass.ds(4 * i * S + t * S, S)], bank[6 + t % 2][:]).then_inc(s["x_new"], 1)
        stats_dve(dve, 1)
        post_dve(dve, y_mix, "g_post_mix", s["x_post"], split=True)

    def blk2_pool(pool, f):
        fence(pool, f)
        nc.gpsimd.memset(ssq[:], 0.0).then_inc(s["ssq_add"], 2)
        sum_squares(pool)
        pool.wait_ge(s["stat_sum"], 1)
        nc.gpsimd.memset(ssq[:], 0.0).then_inc(s["ssq_add"], 2)
        sum_squares(pool, 1)
        pool.wait_ge(s["stat_sum"], 2)
        nc.gpsimd.memset(ssq[:], 0.0).then_inc(s["ssq_add"], 2)
        sum_squares(pool, 2)

    def post_dve(dve, y, gain, done, split=False):
        for k in range(KD):
            if k >= 2:
                dve.wait_ge(done, k - 1)
            nc.vector.scalar_tensor_tensor(out=val[k % 2][:], in0=tile(y, k), scalar=bc(gain, k), in1=bank[6][:],
                                           op0=ALU.mult, op1=ALU.mult).then_inc(s["y_norm"], 1)
            dve.wait_ge(s["y_norm"], k + 1)
            nc.vector.tensor_tensor(tile(x, k), tile(x, k), val[k % 2][:], ALU.add).then_inc(done, 1)
            if split:
                g = (3 * L + 1) * KD + k
                scaled_lo(dve, tile(x, k), tile(h_hi, k), tile(h_lo, k), gains[:, g:g + 1], k + 1)

    BIAS_FIRST = 10
    PER_LAYER, PHASES = 52, 5
    R2, F2 = L * PER_LAYER, L * PHASES

    with nc.Block() as block:
        @block.sync
        def _(sp):
            sp.dma_start(cst[:], A["constants"]).then_inc(consts_loaded, 16)
            sp.dma_start(gains[:], A["gains"]).then_inc(gains_loaded, 16)
            sp.dma_start(x[:], A["x"]).then_inc(loaded, 16)
            for q in range(SLOTS):
                sp.dma_start(raw[q][:], A["units"][q]).then_inc(raw_full[q], 16)
            with sp.Fori(1, n_units // SLOTS) as r:
                for q in range(SLOTS):
                    sp.wait_ge(unit_lo, SLOTS * r + q - (SLOTS - 1))
                    sp.dma_start(raw[q][:], A["units"][SLOTS * r + q]).then_inc(raw_full[q], 16)
            for k in range(KD):
                sp.wait_ge(x_final, k + 1)
                sp.dma_start(out[:, k * S:(k + 1) * S], tile(x, k)).then_inc(stored, 16)
            sp.wait_ge(stored, 16 * KD)

        @block.tensor
        def _(pe):
            pe.sem_inc(unit_used, 1)
            bias_rows_pe(pe)
            pe.wait_ge(consts_loaded, 16)
            with pe.Fori(0, L) as l:
                r, f = l * PER_LAYER, l * PHASES
                ffn_pe(pe, f, r)
                mix1_pe(pe, f + 1, r + 17)
                mix2_pe(pe, f + 2)
                mix3_pe(pe, f + 3, r + 25)
                ffn_pe(pe, f + 4, r + 35)
            blk1_pe(pe, F2, R2)
            blk2_pe(pe, F2 + 1, R2 + 13)
            ffn_pe(pe, F2 + 2, R2 + 22, post=True)

        @block.scalar
        def _(act):
            bias_loads_act(act)
            bias_rows_act(act, 0, BIAS_FIRST)
            act.wait_ge(loaded, 16)
            act.wait_ge(gains_loaded, 16)
            for m in range(KD):
                act.wait_ge(s["ssq_add"], m + 1)
                nc.scalar.activation(sq[m % 2][:], tile(x, m), ACT.Square).then_inc(s["sq"], 1)
                scaled_hi(act, tile(x, m), tile(h_hi, m), gains[:, m:m + 1])
            bias_rows_act(act, BIAS_FIRST, NG * NH2)
            for u in range(AHEAD):
                split_hi(act, 0, u)
            with act.Fori(0, L) as l:
                r, f = l * PER_LAYER, l * PHASES
                ffn_act(act, f, r, 3 * KD * l + KD)
                mix1_act(act, f + 1, r + 17, l)
                mix2_act(act, f + 2)
                mix3_act(act, f + 3, r + 25, 3 * KD * l + 2 * KD)
                ffn_act(act, f + 4, r + 35, 3 * KD * l + 3 * KD)
            blk1_act(act, F2, R2)
            blk2_act(act, F2 + 1, R2 + 13)
            ffn_act(act, F2 + 2, R2 + 22, last=True)

        @block.vector
        def _(dve):
            nc.vector.memset(eps_col[:, 0:1], EPS)
            nc.vector.memset(eps_col[:, 1:2], LN_EPS)
            bias_rows_dve(dve)
            dve.wait_ge(consts_loaded, 16)
            dve.wait_ge(loaded, 16)
            dve.wait_ge(gains_loaded, 16)
            for m in range(KD):
                scaled_lo(dve, tile(x, m), tile(h_hi, m), tile(h_lo, m), gains[:, m:m + 1], m + 1)
            for u in range(AHEAD):
                split_lo(dve, 0, u)
            with dve.Fori(0, L) as l:
                r, f = l * PER_LAYER, l * PHASES
                ffn_dve(dve, f, r, 3 * KD * l + KD)
                mix1_dve(dve, f + 1, r + 17)
                mix2_dve(dve, f + 2)
                mix3_dve(dve, f + 3, r + 25, 3 * KD * l + 2 * KD)
                ffn_dve(dve, f + 4, r + 35, 3 * KD * l + 3 * KD)
            blk1_dve(dve, F2, R2)
            blk2_dve(dve, F2 + 1, R2 + 13)
            ffn_dve(dve, F2 + 2, R2 + 22, last=True)

        @block.gpsimd
        def _(pool):
            bias_rows_pool(pool, 0, BIAS_FIRST)
            nc.gpsimd.memset(ssq[:], 0.0).then_inc(s["ssq_add"], 2)
            sum_squares(pool)
            bias_rows_pool(pool, BIAS_FIRST, NG * NH2)
            for q in range(2):
                pool.wait_ge(bias_stored[q], 16 * NG * NH2 // 2)
            with pool.Fori(0, L) as l:
                f = l * PHASES
                ffn_pool(pool, f)
                fence(pool, f + 1)
                mix2_pool(pool, f + 2)
                mix3_pool(pool, f + 3)
                ffn_pool(pool, f + 4)
            blk1_pool(pool, F2)
            blk2_pool(pool, F2 + 1)
            ffn_pool(pool, F2 + 2)


def column_tiles(w):
    k, c = w.shape
    return w.reshape(k // P, P, c // P, P).transpose(2, 1, 0, 3)


def whole_units(w):
    return column_tiles(w).reshape(-1, P, UNIT)


def gate_up_units(w):
    return w.reshape(KD, P, 2, FT, P).transpose(3, 2, 1, 0, 4).reshape(2 * FT, P, UNIT)


def down_units(w):
    tiles = column_tiles(w)
    units = np.zeros((KD, 3, P, 8, P), np.float32)
    for j, n in enumerate((8, 8, 6)):
        units[:, j, :, :n] = tiles[:, :, 8 * j:8 * j + n]
    return units.reshape(3 * KD, P, UNIT)


def natural_units(w):
    q = w.shape[1] // 512
    return w.reshape(4, 2, P, q, 512).transpose(3, 0, 2, 1, 4).reshape(4 * q, P, UNIT)


def small_units(w):
    units = np.zeros((2, P, UNIT), np.float32)
    units[:, :, :4 * SMALL] = w.reshape(2, 4, P, SMALL).transpose(0, 2, 1, 3).reshape(2, P, 4 * SMALL)
    return units


def columns(v):
    return v.reshape(-1, P).T


def mixer_units(a, l):
    w, parts, at = a["w_in"][l], {}, 0
    for name, width in (("sb_q", 256), ("sb_k", 256), ("sb_v", 256), ("nq", 512), ("nkc", 128), ("nvc", 128),
                        ("nks", 128), ("nvs", 128), ("nkw", 128), ("nvw", 128), ("gate", 24), ("dq", 256),
                        ("dk", HD), ("dv", HD), ("iq", 256), ("ik", IDX_D), ("iw", 8)):
        parts[name] = w[:, at:at + width]
        at += width
    nq = parts["nq"].reshape(D, G, 4, HD).transpose(0, 2, 1, 3).reshape(D, 512)
    turned = np.concatenate([parts[n] for n in ("nkc", "nvc", "sb_q", "sb_k")], 1)
    values = np.concatenate([parts[n] for n in ("sb_v", "nvs", "nvw")], 1)
    heads = np.concatenate([nq] + [parts[n] for n in ("nks", "nkw", "dq", "dk", "dk", "iq", "ik", "ik", "ik", "ik")], 1)
    small = np.concatenate([parts[n] for n in ("dv", "dv", "gate", "iw")], 1)
    w1 = a["nsa_cmp_w1"][l].reshape(2, 4, 8, HD, P).transpose(0, 1, 3, 2, 4).reshape(8, HD, UNIT)
    gates = whole_units(a["w_gate"][l]).reshape(3, KD, P, UNIT)
    heads_b = a["w_br_b"][l].reshape(2, 4, HD, D).transpose(1, 0, 2, 3).reshape(512, D)
    heads_c = a["w_br_c"][l].reshape(2, 2, HD, D).transpose(1, 0, 2, 3).reshape(256, D)
    branches = whole_units(np.concatenate([a["w_br_a"][l], heads_b, heads_c], 0))[None]
    return [whole_units(turned), natural_units(values), natural_units(heads), small_units(small),
            np.concatenate([w1, w1], 1), np.concatenate([gates, branches]).transpose(1, 0, 2, 3).reshape(4 * KD, P, UNIT),
            whole_units(a["w_out"][l])]


def block2_units(a):
    w = a["w_in_2"][0]
    aw = NG * NH2 * HD
    q, k, v = w[:, :aw], w[:, aw:2 * aw], w[:, 2 * aw:3 * aw]
    glu, ga, gc = w[:, 3 * aw:3 * aw + 2 * D], w[:, 3 * aw + 2 * D:3 * aw + 3 * D], w[:, 3 * aw + 3 * D:]
    glu = whole_units(glu).reshape(2, KD, P, UNIT).transpose(1, 0, 2, 3).reshape(2 * KD, P, UNIT)
    qk = np.stack([whole_units(q).reshape(NG, NH2 // 2, P, UNIT), whole_units(k).reshape(NG, NH2 // 2, P, UNIT)], 1)
    qk = qk.transpose(2, 0, 1, 3, 4).reshape(-1, P, UNIT)
    ao = column_tiles(a["w_attn_out_2"][0]).reshape(4, 2, P, 4, P).transpose(0, 2, 1, 3, 4).reshape(4, P, UNIT)
    merge = np.stack([whole_units(ga), whole_units(gc), whole_units(a["w_conv_out_2"][0])], 1).reshape(-1, P, UNIT)
    return [natural_units(v), glu, qk, ao, merge, whole_units(a["w_mix_out_2"][0])]


def mixer_gains(a, l):
    q, k, dq, dk = a["nsa_q_norm"][l], a["nsa_k_norm"][l], a["dsa_q_norm"][l], a["dsa_k_norm"][l]
    row = np.concatenate([q] * 8 + [k[1]] * 2 + [k[2]] * 2 + [dq] * 4 + [dk] * 2 + [k[0]] * 2)
    w2 = a["nsa_cmp_w2"][l].transpose(1, 0, 2).reshape(P, 2 * HD)
    pos = a["nsa_cmp_pe"][l].reshape(2, 2, STRIDE, HD).transpose(3, 0, 1, 2).reshape(HD, 4 * STRIDE)
    return np.concatenate([np.broadcast_to(row, (P, len(row))), w2, np.concatenate([pos, pos])], 1)


def rope_table(pos, rot):
    inv = (np.float32(500000.0) ** (-np.arange(0, rot, 2, dtype=np.float32) / np.float32(rot))).astype(np.float32)
    angle = pos.astype(np.float32)[:, None] * inv[None, :]
    c, sn = np.cos(angle), np.sin(angle)
    return np.concatenate([c, c], 1), np.concatenate([-sn, sn], 1)


def by_block(t):
    return t.reshape(TB, P, -1).transpose(1, 0, 2).reshape(P, -1)


def mixer_constants():
    i, t = np.arange(P), np.arange(S)
    later = i[:, None] >= i[None, :]
    causal = np.where(i[:, None] + S - P - t[None, :] >= 0, 0.0, NEG)
    strict = np.where(i[:, None] < i[None, :], 0.0, NEG)
    compressed = np.where(STRIDE * np.arange(NC)[None, :] + 2 * STRIDE - 1 <= t[:, None], 0.0, NEG)
    tables = [by_block(x) for x in (*rope_table(t, 16), *rope_table(t, 8))]
    return np.concatenate([later, causal, strict, by_block(compressed), *tables, *rope_table(STRIDE * i + 2 * STRIDE - 1, 16)],
                          1).astype(np.float32)


def bias_one_hot():
    dist = S - 1 - np.arange(BW)
    d = np.maximum(dist, 0)
    far = 16 + (np.log(np.maximum(d, 1).astype(np.float32) / np.float32(16)) / np.float32(math.log(2048 / 16)) * np.float32(16)).astype(np.int32)
    bucket = np.where(d < 16, d, np.minimum(far, 31))
    out = np.zeros((33, NG, BW), np.float32)
    for g, step in enumerate((1, 4, 16)):
        valid = (dist >= 0) & (dist % step == 0) & (dist <= 128 * step)
        out[bucket[valid], g, np.arange(BW)[valid]] = 1.0
        out[32, g, ~valid] = NEG
    return out.reshape(33, NG * BW)


def layout(a):
    units = []
    for l in range(L):
        units += [gate_up_units(a["ffn1_w_gu"][l]), down_units(a["ffn1_w_down"][l]), *mixer_units(a, l),
                  gate_up_units(a["ffn2_w_gu"][l]), down_units(a["ffn2_w_down"][l])]
    units += [*block2_units(a), gate_up_units(a["w_ffn_in_2"][0]), down_units(a["w_ffn_out_2"][0])]
    gains = [columns(a[n][l]) for l in range(L) for n in ("ffn1_norm", "mix_norm", "ffn2_norm")]
    gains += [columns(a[n][0]) for n in ("g_pre_mix_2", "g_pre_ffn_2")]
    b_glu = a["b_glu_2"][0]
    block2 = [columns(b_glu[:D]), columns(b_glu[D:]), columns(a["b_dw_2"][0]),
              a["w_dw_2"][0].reshape(CW, KD, P).transpose(2, 1, 0).reshape(P, KD * CW)]
    block2 += [columns(a[n][0]) for n in ("g_conv_ln_2", "b_conv_ln_2", "b_conv_out_2", "g_post_mix_2", "g_post_ffn_2")]
    table = np.ones((33, NG * NH2, P), np.float32)
    table[:32] = a["rel_bias_table_2"][:, :, None]
    return dict(
        x=a["x"][0].reshape(S, KD, P).transpose(2, 1, 0).reshape(P, KD * S),
        units=np.concatenate(units),
        constants=np.concatenate([np.eye(P), np.ones((P, P)), np.full((P, P), 1.0 / D)], 1).astype(np.float32),
        gains=np.concatenate(gains, 1),
        mixer_constants=mixer_constants(),
        mixer_gains=np.stack([mixer_gains(a, l) for l in range(L)]),
        block2_columns=np.concatenate(block2, 1),
        bias_table=table.reshape(33, NG * NH2 * P),
        bias_one_hot=bias_one_hot(),
    )


def kernel(**inputs):
    import concourse.bacc as bacc
    from concourse.bass_utils import run_bass_kernel_spmd

    nc = bacc.Bacc("TRN2", target_bir_lowering=False, num_devices=1)
    arrays = {n: np.ascontiguousarray(v) for n, v in layout({n: np.asarray(v) for n, v in inputs.items()}).items()}
    aps = {n: nc.dram_tensor(f"in_{n}", v.shape, F32, kind="ExternalInput").ap() for n, v in arrays.items()}
    out = nc.dram_tensor("out_x", (P, KD * S), F32, kind="ExternalOutput").ap()
    program(nc, aps, out)
    got = run_bass_kernel_spmd(nc, [{f"in_{n}": v for n, v in arrays.items()}], core_ids=[0]).results[0]["out_x"]
    return got.reshape(P, KD, S).transpose(2, 1, 0).reshape(1, S, D)
```
